# Optimizing a Trainium2 kernel written in Bass

```python
import jax, jax.numpy as jnp
from jax import lax
import numpy as np

D_MODEL = 1024
BATCH = 1
SEQ = 256
DEPTH = 4

N_MIXERS = 3
PLE_DIM = 256
D_FF = 2816
EPS = 1e-6
HG_HEADS = 8
HG_DK = D_MODEL // HG_HEADS
HG_DV = D_MODEL // HG_HEADS
HG_CHUNK = 64
ML_HEADS = 4
ML_DQK = D_MODEL // 2 // ML_HEADS
ML_DV = D_MODEL // ML_HEADS
ML_CHUNK = 64
ML_GATE_CAP = 15.0
SW_HEADS = 16
SW_KV_HEADS = 4
SW_GROUP = SW_HEADS // SW_KV_HEADS
SW_HD = 64
WINDOW = 128
SW_BLOCK = 128
N_A = (DEPTH + 2) // 3
N_B = (DEPTH + 1) // 3
N_C = DEPTH // 3


def rmsnorm(x, gain):
    xf = x.astype(jnp.float32)
    y = xf * lax.rsqrt(jnp.mean(xf * xf, axis=-1, keepdims=True) + EPS)
    return (y * gain.astype(jnp.float32)).astype(x.dtype)

def swiglu(x, w_gu, w_down):
    g, u = jnp.split(x @ w_gu, 2, axis=-1)
    return (jax.nn.silu(g) * u) @ w_down

def to_chunks(t, L):
    B, T, H, d = t.shape
    return t.reshape(B, T // L, L, H, d).transpose(1, 0, 3, 2, 4)

def from_chunks(t):
    N, B, H, L, d = t.shape
    return t.transpose(1, 0, 3, 2, 4).reshape(B, N * L, H, d)

def gate_chunks(t, L):
    B, T, H = t.shape
    return t.reshape(B, T // L, L, H).transpose(1, 0, 3, 2)

def alibi_slopes(n_heads):
    return jnp.asarray([2.0 ** (-8.0 * (h + 1) / n_heads) for h in range(n_heads)], jnp.float32)

def hgrn2_mixer(x, lb, w_in, g_norm, w_out):
    B, T, _ = x.shape
    q, f, i, og = jnp.split(x @ w_in, 4, axis=-1)
    q = jax.nn.silu(q).astype(jnp.float32)
    f = f.astype(jnp.float32)
    lb = lb.astype(jnp.float32)
    log_f = jnp.logaddexp(jnp.log(lb), jnp.log1p(-lb) + jax.nn.log_sigmoid(f))
    k = (1.0 - lb) * jax.nn.sigmoid(-f)
    L = HG_CHUNK
    qc = to_chunks(q.reshape(B, T, HG_HEADS, HG_DK), L)
    kc = to_chunks(k.reshape(B, T, HG_HEADS, HG_DK), L)
    gc = to_chunks(log_f.reshape(B, T, HG_HEADS, HG_DK), L)
    vc = to_chunks(i.astype(jnp.float32).reshape(B, T, HG_HEADS, HG_DV), L)
    causal = jnp.tril(jnp.ones((L, L), bool))

    def step(S, inp):
        q_, k_, v_, g_ = inp
        b = jnp.cumsum(g_, axis=2)
        o_inter = jnp.einsum('bhtk,bhkv->bhtv', q_ * jnp.exp(b), S)
        diff = b[:, :, :, None, :] - b[:, :, None, :, :]
        decay = jnp.exp(jnp.where(causal[:, :, None], diff, -jnp.inf))
        A = jnp.einsum('bhtk,bhsk,bhtsk->bhts', q_, k_, decay)
        o_intra = jnp.einsum('bhts,bhsv->bhtv', A, v_)
        b_last = b[:, :, -1:, :]
        S_new = jnp.exp(b_last[:, :, 0, :])[..., None] * S + jnp.einsum(
            'bhsk,bhsv->bhkv', k_ * jnp.exp(b_last - b), v_)
        return S_new, o_inter + o_intra

    S0 = jnp.zeros((B, HG_HEADS, HG_DK, HG_DV), jnp.float32)
    _, o = lax.scan(step, S0, (qc, kc, vc, gc))
    o = rmsnorm(from_chunks(o), g_norm)
    o = o.reshape(B, T, D_MODEL).astype(x.dtype) * jax.nn.silu(og)
    return o @ w_out

def mlstm_mixer(x, w_qkvo, w_if, b_if, norm_g, w_out):
    B, T, _ = x.shape
    dqk_all = ML_HEADS * ML_DQK
    q, k, v, og = jnp.split(x @ w_qkvo, [dqk_all, 2 * dqk_all, 2 * dqk_all + D_MODEL], axis=-1)
    gates = (x @ w_if).astype(jnp.float32) + b_if.astype(jnp.float32)
    gates = ML_GATE_CAP * jnp.tanh(gates / ML_GATE_CAP)
    ig, fg = jnp.split(gates, 2, axis=-1)
    lf = jax.nn.log_sigmoid(fg)
    L = ML_CHUNK
    qc = to_chunks(q.astype(jnp.float32).reshape(B, T, ML_HEADS, ML_DQK), L)
    kc = to_chunks(k.astype(jnp.float32).reshape(B, T, ML_HEADS, ML_DQK), L) * (ML_DQK ** -0.5)
    vc = to_chunks(v.astype(jnp.float32).reshape(B, T, ML_HEADS, ML_DV), L)
    ic = gate_chunks(ig, L)
    fc = gate_chunks(lf, L)
    causal = jnp.tril(jnp.ones((L, L), bool))

    def step(carry, inp):
        C, n, m = carry
        q_, k_, v_, i_, f_ = inp
        b = jnp.cumsum(f_, axis=-1)
        log_intra = jnp.where(causal, b[..., :, None] - b[..., None, :] + i_[..., None, :], -jnp.inf)
        log_inter = b + m[..., None]
        m_t = jnp.maximum(jnp.max(log_intra, axis=-1), log_inter)
        w_intra = jnp.exp(log_intra - m_t[..., None])
        w_inter = jnp.exp(log_inter - m_t)
        scores = jnp.einsum('bhtk,bhsk->bhts', q_, k_) * w_intra
        num = w_inter[..., None] * jnp.einsum('bhtk,bhkv->bhtv', q_, C) + jnp.einsum('bhts,bhsv->bhtv', scores, v_)
        den = w_inter * jnp.einsum('bhtk,bhk->bht', q_, n) + jnp.sum(scores, axis=-1)
        h = num / jnp.maximum(jnp.abs(den), jnp.exp(-m_t))[..., None]
        b_L = b[..., -1]
        log_state = b_L + m
        log_src = b_L[..., None] - b + i_
        m_new = jnp.maximum(log_state, jnp.max(log_src, axis=-1))
        w_src = jnp.exp(log_src - m_new[..., None])
        decay = jnp.exp(log_state - m_new)
        C_new = decay[..., None, None] * C + jnp.einsum('bhsk,bhsv->bhkv', k_ * w_src[..., None], v_)
        n_new = decay[..., None] * n + jnp.einsum('bhs,bhsk->bhk', w_src, k_)
        return (C_new, n_new, m_new), h

    carry0 = (jnp.zeros((B, ML_HEADS, ML_DQK, ML_DV), jnp.float32),
              jnp.zeros((B, ML_HEADS, ML_DQK), jnp.float32),
              jnp.zeros((B, ML_HEADS), jnp.float32))
    _, h = lax.scan(step, carry0, (qc, kc, vc, ic, fc))
    h = rmsnorm(from_chunks(h), norm_g.reshape(ML_HEADS, ML_DV))
    h = h.reshape(B, T, D_MODEL).astype(x.dtype) * jax.nn.sigmoid(og)
    return h @ w_out

def swa_mixer(x, w_qkv, q_gain, k_gain, sinks, w_o):
    B, T, _ = x.shape
    nq = SW_HEADS * SW_HD
    nk = SW_KV_HEADS * SW_HD
    q, k, v = jnp.split(x @ w_qkv, [nq, nq + nk], axis=-1)
    q = rmsnorm(q.reshape(B, T, SW_HEADS, SW_HD), q_gain)
    k = rmsnorm(k.reshape(B, T, SW_KV_HEADS, SW_HD), k_gain)
    v = v.reshape(B, T, SW_KV_HEADS, SW_HD)
    nb = T // SW_BLOCK
    qb = q.reshape(B, nb, SW_BLOCK, SW_KV_HEADS, SW_GROUP, SW_HD)

    def band(t):
        tb = t.reshape(B, nb, SW_BLOCK, SW_KV_HEADS, SW_HD)
        prev = jnp.pad(tb, ((0, 0), (1, 0), (0, 0), (0, 0), (0, 0)))[:, :-1]
        return jnp.concatenate([prev, tb], axis=2)

    kk, vv = band(k), band(v)
    s = jnp.einsum('bnqkgd,bnskd->bnkgqs', qb, kk).astype(jnp.float32) * (SW_HD ** -0.5)
    qpos = jnp.arange(SW_BLOCK)
    kpos = jnp.arange(2 * SW_BLOCK) - SW_BLOCK
    dist = (qpos[:, None] - kpos[None, :]).astype(jnp.float32)
    blk_start = jnp.arange(nb) * SW_BLOCK
    valid = (dist >= 0) & (dist < WINDOW) & ((blk_start[:, None, None] + kpos[None, None, :]) >= 0)
    slopes = alibi_slopes(SW_HEADS).reshape(SW_KV_HEADS, SW_GROUP)
    s = s - slopes[:, :, None, None] * dist
    s = jnp.where(valid[None, :, None, None], s, -jnp.inf)
    sink = jnp.broadcast_to(sinks.astype(jnp.float32).reshape(SW_KV_HEADS, SW_GROUP)[:, :, None, None],
                            s.shape[:-1] + (1,))
    probs = jax.nn.softmax(jnp.concatenate([s, sink], axis=-1), axis=-1)[..., :-1]
    o = jnp.einsum('bnkgqs,bnskd->bnqkgd', probs.astype(vv.dtype), vv).reshape(B, T, nq)
    return o @ w_o

def first_inputs(seed: int = 0) -> dict:
    key = jax.random.key(seed)
    ks = jax.random.split(key, 24)
    f32 = jnp.float32

    def nrm(k, shape, fan_in):
        return jax.random.normal(k, shape, f32) * (fan_in ** -0.5)

    D = D_MODEL
    b_if = jnp.concatenate([
        0.1 * jax.random.normal(ks[11], (N_B, ML_HEADS), f32),
        jnp.linspace(3.0, 6.0, ML_HEADS, dtype=f32)[None, :] + 0.1 * jax.random.normal(ks[12], (N_B, ML_HEADS), f32),
    ], axis=-1)
    return {
        "x": jax.random.normal(ks[0], (BATCH, SEQ, D), f32),
        "p": jax.random.normal(ks[1], (DEPTH, BATCH, SEQ, PLE_DIM), f32),
        "norm_gains": 1.0 + 0.02 * jax.random.normal(ks[2], (DEPTH, 4, D), f32),
        "w_ffn_gu": nrm(ks[3], (DEPTH, 2, D, 2 * D_FF), D),
        "w_ffn_down": nrm(ks[4], (DEPTH, 2, D_FF, D), D_FF),
        "w_ple_gate": nrm(ks[5], (DEPTH, D, D), D),
        "w_ple_proj": nrm(ks[6], (DEPTH, PLE_DIM, D), PLE_DIM),
        "hg_lower_bounds": 0.5 * jax.random.normal(ks[7], (DEPTH, D), f32),
        "hg_w_in": nrm(ks[8], (N_A, D, 4 * D), D),
        "hg_g_norm": 1.0 + 0.02 * jax.random.normal(ks[9], (N_A, HG_DV), f32),
        "hg_w_out": nrm(ks[10], (N_A, D, D), D),
        "ml_w_qkvo": nrm(ks[13], (N_B, D, 2 * ML_HEADS * ML_DQK + 2 * D), D),
        "ml_w_if": nrm(ks[14], (N_B, D, 2 * ML_HEADS), D),
        "ml_b_if": b_if,
        "ml_norm": 1.0 + 0.02 * jax.random.normal(ks[15], (N_B, D), f32),
        "ml_w_out": nrm(ks[16], (N_B, D, D), D),
        "sw_w_qkv": nrm(ks[17], (N_C, D, (SW_HEADS + 2 * SW_KV_HEADS) * SW_HD), D),
        "sw_q_norm": 1.0 + 0.02 * jax.random.normal(ks[18], (N_C, SW_HD), f32),
        "sw_k_norm": 1.0 + 0.02 * jax.random.normal(ks[19], (N_C, SW_HD), f32),
        "sw_sinks": 0.5 * jax.random.normal(ks[20], (N_C, SW_HEADS), f32),
        "sw_w_o": nrm(ks[21], (N_C, SW_HEADS * SW_HD, D), SW_HEADS * SW_HD),
    }

def first_block(x, p, norm_gains, w_ffn_gu, w_ffn_down, w_ple_gate, w_ple_proj,
              hg_lower_bounds, hg_w_in, hg_g_norm, hg_w_out,
              ml_w_qkvo, ml_w_if, ml_b_if, ml_norm, ml_w_out,
              sw_w_qkv, sw_q_norm, sw_k_norm, sw_sinks, sw_w_o):
    lbs = jnp.cumsum(jax.nn.softmax(hg_lower_bounds.astype(jnp.float32), axis=0), axis=0)
    lbs = lbs - lbs[0:1]
    for layer in range(DEPTH):
        g = norm_gains[layer]
        h = x + 0.5 * swiglu(rmsnorm(x, g[0]), w_ffn_gu[layer, 0], w_ffn_down[layer, 0])
        xn = rmsnorm(h, g[1])
        kind = layer % N_MIXERS
        j = layer // N_MIXERS
        if kind == 0:
            mix = hgrn2_mixer(xn, lbs[layer], hg_w_in[j], hg_g_norm[j], hg_w_out[j])
        elif kind == 1:
            mix = mlstm_mixer(xn, ml_w_qkvo[j], ml_w_if[j], ml_b_if[j], ml_norm[j], ml_w_out[j])
        else:
            mix = swa_mixer(xn, sw_w_qkv[j], sw_q_norm[j], sw_k_norm[j], sw_sinks[j], sw_w_o[j])
        h = h + mix
        h = h + 0.5 * swiglu(rmsnorm(h, g[2]), w_ffn_gu[layer, 1], w_ffn_down[layer, 1])
        gate = jax.nn.sigmoid(rmsnorm(h, g[3]) @ w_ple_gate[layer])
        x = h + gate * (p[layer] @ w_ple_proj[layer])
    return x


DEPTH_2 = 1

HEAD_DIM = 64
BRANCH_WIDTH = D_MODEL // 2
A_GROUPS = ((128, 1), (512, 4), (2048, 16))
A_HEADS = BRANCH_WIDTH // HEAD_DIM
B_HEADS = BRANCH_WIDTH // HEAD_DIM
B_KV_HEADS = B_HEADS // 4
M_HEADS = 4
M_HEAD_DIM = BRANCH_WIDTH // M_HEADS
N_MEM = 256
GRID_W = 64
ROPE_THETA = 10000.0
Q_BLOCK = 128
NORM_EPS = 1e-6
NEG_INF = -1e30
N_BRANCHES = 3

A_QKV = 3 * len(A_GROUPS) * A_HEADS * HEAD_DIM
B_Q = B_HEADS * HEAD_DIM
B_KV = B_KV_HEADS * HEAD_DIM
M_Q = M_HEADS * M_HEAD_DIM
SPLIT_SIZES = (A_QKV, B_Q, B_KV, B_KV, M_Q, BRANCH_WIDTH, BRANCH_WIDTH, BRANCH_WIDTH, N_BRANCHES * D_MODEL)
IN_WIDTH = A_QKV + B_Q + 2 * B_KV + M_Q + 3 * BRANCH_WIDTH + N_BRANCHES * D_MODEL


def rms_norm(x, g):
    xf = x.astype(jnp.float32)
    y = xf * lax.rsqrt(jnp.mean(xf * xf, axis=-1, keepdims=True) + NORM_EPS)
    return (y * g.astype(jnp.float32)).astype(x.dtype)

def rope(x, pos):
    dr = x.shape[-1]
    half = dr // 2
    inv = jnp.power(ROPE_THETA, -jnp.arange(half, dtype=jnp.float32) * 2.0 / dr)
    ang = pos.astype(jnp.float32)[:, None] * inv[None, :]
    cos = jnp.cos(ang)[:, None, :]
    sin = jnp.sin(ang)[:, None, :]
    xf = x.astype(jnp.float32)
    x1, x2 = xf[..., :half], xf[..., half:]
    return jnp.concatenate([x1 * cos - x2 * sin, x1 * sin + x2 * cos], axis=-1).astype(x.dtype)

def axial_rope(x, row_pos, col_pos):
    half = x.shape[-1] // 2
    return jnp.concatenate([rope(x[..., :half], row_pos), rope(x[..., half:], col_pos)], axis=-1)

def dilated_window_attention(q, k, v, window, dilation):
    b, s, h, dh = q.shape
    half = window // (2 * dilation)
    blk = half
    L = s // dilation
    nb = -(-L // blk)
    lp = nb * blk
    z = b * dilation

    def regroup(t):
        return t.reshape(b, L, dilation, h, dh).transpose(0, 2, 1, 3, 4).reshape(z, L, h, dh)

    qg, kg, vg = regroup(q), regroup(k), regroup(v)
    qb = jnp.pad(qg, ((0, 0), (0, lp - L), (0, 0), (0, 0))).reshape(z, nb, blk, h, dh)

    def band(t):
        tp = jnp.pad(t, ((0, 0), (blk, lp - L + blk), (0, 0), (0, 0))).reshape(z, nb + 2, blk, h, dh)
        return jnp.concatenate([tp[:, :-2], tp[:, 1:-1], tp[:, 2:]], axis=2)

    kw, vw = band(kg), band(vg)
    qpos = jnp.arange(nb)[:, None] * blk + jnp.arange(blk)[None, :]
    kpos = (jnp.arange(nb)[:, None] - 1) * blk + jnp.arange(3 * blk)[None, :]
    valid = ((jnp.abs(qpos[:, :, None] - kpos[:, None, :]) <= half)
             & (kpos[:, None, :] >= 0) & (kpos[:, None, :] < L))
    sc = jnp.einsum('znqhd,znkhd->znhqk', qb, kw).astype(jnp.float32) * (dh ** -0.5)
    sc = jnp.where(valid[None, :, None], sc, NEG_INF)
    m = jnp.max(sc, axis=-1, keepdims=True)
    p = jnp.exp(sc - m)
    l = jnp.sum(p, axis=-1, keepdims=True)
    o = jnp.einsum('znhqk,znkhd->znqhd', (p / l).astype(v.dtype), vw)
    lse = (m + jnp.log(l))[..., 0]
    o = o.reshape(b, dilation, lp, h, dh)[:, :, :L].transpose(0, 2, 1, 3, 4).reshape(b, s, h, dh)
    lse = lse.transpose(0, 1, 3, 2).reshape(b, dilation, lp, h)[:, :, :L]
    lse = lse.transpose(0, 2, 1, 3).reshape(b, s, h)
    return o, lse

def second_inputs(seed: int = 0) -> dict:
    key = jax.random.key(seed)
    ks = jax.random.split(key, 16)
    nrm = jax.random.normal
    f32 = jnp.float32
    return {
        'x': nrm(ks[0], (BATCH, SEQ, D_MODEL), f32),
        'mem': nrm(ks[1], (BATCH, N_MEM, D_MODEL), f32),
        'g_pre': 1.0 + 0.05 * nrm(ks[2], (DEPTH_2, D_MODEL), f32),
        'w_in': nrm(ks[3], (DEPTH_2, D_MODEL, IN_WIDTH), f32) * D_MODEL ** -0.5,
        'b_merge': 0.1 * nrm(ks[4], (DEPTH_2, N_BRANCHES * D_MODEL), f32),
        'q_norm': 1.0 + 0.05 * nrm(ks[5], (DEPTH_2, HEAD_DIM), f32),
        'k_norm': 1.0 + 0.05 * nrm(ks[6], (DEPTH_2, HEAD_DIM), f32),
        'g_mem': 1.0 + 0.05 * nrm(ks[7], (DEPTH_2, D_MODEL), f32),
        'w_mem_kv': nrm(ks[8], (DEPTH_2, D_MODEL, 2 * M_Q), f32) * D_MODEL ** -0.5,
        'w_br_a': nrm(ks[9], (DEPTH_2, BRANCH_WIDTH, D_MODEL), f32) * BRANCH_WIDTH ** -0.5,
        'w_br_b': nrm(ks[10], (DEPTH_2, BRANCH_WIDTH, D_MODEL), f32) * BRANCH_WIDTH ** -0.5,
        'w_br_m': nrm(ks[11], (DEPTH_2, BRANCH_WIDTH, D_MODEL), f32) * BRANCH_WIDTH ** -0.5,
        'w_out': nrm(ks[12], (DEPTH_2, D_MODEL, D_MODEL), f32) * D_MODEL ** -0.5,
        'g_post': 1.0 + 0.05 * nrm(ks[13], (DEPTH_2, D_MODEL), f32),
    }

def second_block(x, mem, g_pre, w_in, b_merge, q_norm, k_norm, g_mem, w_mem_kv, w_br_a, w_br_b, w_br_m, w_out, g_post):
    b, s, d = x.shape
    dt = x.dtype
    pos = jnp.arange(s, dtype=jnp.float32)
    rows = s // GRID_W
    row_pos = jnp.repeat(jnp.arange(rows, dtype=jnp.float32), GRID_W)
    col_pos = (jnp.arange(s) % GRID_W).astype(jnp.float32)
    split_at = np.cumsum(SPLIT_SIZES)[:-1].tolist()
    n_groups = len(A_GROUPS)
    kv_rep = B_HEADS // B_KV_HEADS
    n_q_blocks = s // Q_BLOCK

    for layer in range(DEPTH_2):
        h = rms_norm(x, g_pre[layer])
        a_qkv, bq, bk, bv, mq, ga, gb, gm, mg = jnp.split(h @ w_in[layer], split_at, axis=-1)

        a_qkv = a_qkv.reshape(b, s, 3, n_groups * A_HEADS, HEAD_DIM)
        aq = rope(a_qkv[:, :, 0], pos)
        ak = rope(a_qkv[:, :, 1], pos)
        av = a_qkv[:, :, 2]
        outs, lses = [], []
        for gi, (window, dil) in enumerate(A_GROUPS):
            hs = slice(gi * A_HEADS, (gi + 1) * A_HEADS)
            o_g, lse_g = dilated_window_attention(aq[:, :, hs], ak[:, :, hs], av[:, :, hs], window, dil)
            outs.append(o_g)
            lses.append(lse_g)
        wts = jax.nn.softmax(jnp.stack(lses, axis=0), axis=0).astype(dt)
        oa = jnp.einsum('gbsh,gbshd->bshd', wts, jnp.stack(outs, axis=0)).reshape(b, s, BRANCH_WIDTH)

        qb_ = axial_rope(rms_norm(bq.reshape(b, s, B_HEADS, HEAD_DIM), q_norm[layer]), row_pos, col_pos)
        kb_ = axial_rope(rms_norm(bk.reshape(b, s, B_KV_HEADS, HEAD_DIM), k_norm[layer]), row_pos, col_pos)
        vb_ = bv.reshape(b, s, B_KV_HEADS, HEAD_DIM)
        q_blocks = qb_.reshape(b, n_q_blocks, Q_BLOCK, B_KV_HEADS, kv_rep, HEAD_DIM).transpose(1, 0, 2, 3, 4, 5)

        def attend(qc, kb_=kb_, vb_=vb_):
            sc = jnp.einsum('bqkgd,bskd->bkgqs', qc, kb_).astype(jnp.float32) * (HEAD_DIM ** -0.5)
            p = jax.nn.softmax(sc, axis=-1).astype(vb_.dtype)
            return jnp.einsum('bkgqs,bskd->bqkgd', p, vb_)

        ob = lax.map(attend, q_blocks).transpose(1, 0, 2, 3, 4, 5).reshape(b, s, B_Q)

        kvm = rms_norm(mem, g_mem[layer]) @ w_mem_kv[layer]
        n_mem = mem.shape[1]
        km = kvm[..., :M_Q].reshape(b, n_mem, M_HEADS, M_HEAD_DIM)
        vm = kvm[..., M_Q:].reshape(b, n_mem, M_HEADS, M_HEAD_DIM)
        sm = jnp.einsum('bshd,bnhd->bhsn', mq.reshape(b, s, M_HEADS, M_HEAD_DIM), km).astype(jnp.float32)
        pm = jax.nn.softmax(sm * (M_HEAD_DIM ** -0.5), axis=-1).astype(dt)
        om = jnp.einsum('bhsn,bnhd->bshd', pm, vm).reshape(b, s, M_Q)

        ya = (oa * jax.nn.silu(ga)) @ w_br_a[layer]
        yb = (ob * jax.nn.silu(gb)) @ w_br_b[layer]
        ym = (om * jax.nn.silu(gm)) @ w_br_m[layer]
        gates = jax.nn.sigmoid((mg + b_merge[layer]).astype(jnp.float32)).astype(dt).reshape(b, s, N_BRANCHES, d)
        merged = gates[:, :, 0] * ya + gates[:, :, 1] * yb + gates[:, :, 2] * ym
        out = merged @ w_out[layer]
        x = x + rms_norm(out, g_post[layer])
    return x


def setup_inputs(seed=0):
    out = dict(first_inputs(seed))
    for name, value in second_inputs(seed + 1).items():
        if name != "x":
            out[name + "_2"] = value
    return out


def reference(
    x, p, norm_gains, w_ffn_gu, w_ffn_down, w_ple_gate, w_ple_proj, hg_lower_bounds, hg_w_in,
    hg_g_norm, hg_w_out, ml_w_qkvo, ml_w_if, ml_b_if, ml_norm, ml_w_out, sw_w_qkv, sw_q_norm,
    sw_k_norm, sw_sinks, sw_w_o, mem_2, g_pre_2, w_in_2, b_merge_2, q_norm_2, k_norm_2, g_mem_2,
    w_mem_kv_2, w_br_a_2, w_br_b_2, w_br_m_2, w_out_2, g_post_2,
):
    x = first_block(
        x, p, norm_gains, w_ffn_gu, w_ffn_down, w_ple_gate, w_ple_proj, hg_lower_bounds,
        hg_w_in, hg_g_norm, hg_w_out, ml_w_qkvo, ml_w_if, ml_b_if, ml_norm, ml_w_out, sw_w_qkv,
        sw_q_norm, sw_k_norm, sw_sinks, sw_w_o,
    )
    return second_block(
        x, mem_2, g_pre_2, w_in_2, b_merge_2, q_norm_2, k_norm_2, g_mem_2, w_mem_kv_2, w_br_a_2,
        w_br_b_2, w_br_m_2, w_out_2, g_post_2,
    )


_drawn_inputs = setup_inputs


def setup_inputs(seed=0):
    import zlib

    import numpy as np

    out = dict(_drawn_inputs(seed))
    spreads = {}
    factors = {'hg_g_norm': 3.362,
     'ml_norm': 6.156,
     'sw_q_norm': 8.0,
     'sw_k_norm': 8.0,
     'sw_sinks': 117.573,
     'b_merge_2': 3.172,
     'q_norm_2': 3.883,
     'k_norm_2': 14.668,
     'g_mem_2': 9.524,
     'w_br_a_2': 3.67,
     'g_post_2': 5.481}
    for name, (base, spread) in spreads.items():
        noise = np.random.default_rng([zlib.crc32(name.encode()), seed]).standard_normal(out[name].shape)
        drawn = base * np.exp(spread * noise) if base else spread * noise
        out[name] = __import__('jax').numpy.asarray(drawn.astype(out[name].dtype))
    for name, factor in factors.items():
        out[name] = (out[name] * factor).astype(out[name].dtype)
    return out
```

```python
from contextlib import ExitStack

import numpy as np

import concourse.bass as bass
from concourse import mybir

F32 = mybir.dt.float32
F32R = mybir.dt.float32r
U8 = mybir.dt.uint8
ALU = mybir.AluOpType
ACT = mybir.ActivationFunctionType
AX_X = mybir.AxisListType.X

P = 128
T = 256
TB = T // P
D_MODEL = 1024
KC = D_MODEL // P
D_FF = 2816
HCH = D_FF // P
STEPS = HCH // 2
DEPTH = 4
EPS = 1e-6
PLE_DIM = 256
HG_HEADS = 8
ML_HEADS = 4
ML_DQK = 128
ML_DV = 256
GATE_CAP = 15.0
SW_HEADS = 16
SW_KV = 4
HD = 64
A_HEADS = 8
A_GROUPS = 3
B_HEADS = 8
M_HEADS = 4

UNIT = 2048
RAW = 6
SPLIT = 3
BANKS = 4

KINDS = {
    "ffn": dict(units=HCH + STEPS, banks=HCH, norms=1, resid=KC, hidden=HCH, acc=3),
    "ple": dict(units=5, banks=4, norms=1, resid=KC, ple=1),
    "hg": dict(units=20, banks=20, norms=1, resid=KC, hg=1),
    "ml": dict(units=16, banks=16, norms=1, resid=KC, ml=1),
    "sw": dict(units=11, banks=11, norms=1, resid=KC, sw=1),
    "second": dict(units=56, banks=50, norms=1, resid=KC, second=1),
}
PHASES = [(k, l) for l in range(DEPTH) for k in ("ffn", ("hg", "ml", "sw")[l % 3], "ffn", "ple")]
PHASES.append(("second", 0))


def starts(phases):
    done, out = {}, []
    for kind, _ in phases:
        out.append(dict(done))
        for what, n in KINDS[kind].items():
            done[what] = done.get(what, 0) + n
    out.append(done)
    return out


def columns_unit(w, cols):
    return w[:, cols].reshape(KC, P, 256).transpose(1, 0, 2).reshape(P, UNIT)


def rows_unit(w, r0):
    return w[r0:r0 + 256].reshape(2, P, D_MODEL).transpose(1, 0, 2).reshape(P, UNIT)


def span(a, n=256):
    return np.arange(a, a + n)


def weight_units(inputs, phases):
    a = {k: np.asarray(v) for k, v in inputs.items()}
    ffn = 0
    for kind, layer in phases:
        if kind == "ffn":
            gu, down = a["w_ffn_gu"][layer, ffn % 2], a["w_ffn_down"][layer, ffn % 2]
            ffn += 1

            def up(j):
                return columns_unit(gu, np.concatenate([span(P * j, P), span(D_FF + P * j, P)]))
            yield up(0)
            yield up(1)
            for s in range(1, STEPS):
                yield up(2 * s)
                yield up(2 * s + 1)
                yield rows_unit(down, 256 * (s - 1))
            yield rows_unit(down, 256 * (STEPS - 1))
        elif kind == "ple":
            yield rows_unit(a["w_ple_proj"][layer], 0)
            for u in range(4):
                yield columns_unit(a["w_ple_gate"][layer], span(256 * u))
        elif kind == "hg":
            w = a["hg_w_in"][layer // 3]
            for part in (1, 0, 2, 3):
                for u in range(4):
                    yield columns_unit(w, span(part * D_MODEL + 256 * u))
            for u in range(4):
                yield columns_unit(a["hg_w_out"][layer // 3], span(256 * u))
        elif kind == "ml":
            for u in range(12):
                yield columns_unit(a["ml_w_qkvo"][0], span(256 * u))
            for u in range(4):
                yield columns_unit(a["ml_w_out"][0], span(256 * u))
        elif kind == "sw":
            w = a["sw_w_qkv"][0]
            for u in range(4):
                yield columns_unit(w, span(256 * u))
            for u in range(2):
                k0 = SW_HEADS * HD + 2 * u * HD
                yield columns_unit(w, np.concatenate([span(k0, HD), span(k0, HD), span(k0 + HD, HD), span(k0 + HD, HD)]))
            yield columns_unit(w, span((SW_HEADS + SW_KV) * HD))
            for u in range(4):
                yield columns_unit(a["sw_w_o"][0], span(256 * u))
        else:
            yield from second_units(a)


def second_units(a):
    w = a["w_in_2"][0]
    mkv = a["w_mem_kv_2"][0]
    gh = A_GROUPS * A_HEADS * HD
    b0 = 3 * gh
    bk = b0 + B_HEADS * HD
    bv = bk + 2 * HD
    mq = bv + 2 * HD
    ga = mq + 512
    mg = ga + 3 * 512
    for u in range(4):
        yield columns_unit(mkv, span(256 * u))
    for u in range(2):
        yield columns_unit(w, span(mq + 256 * u))
    for u in range(2):
        yield columns_unit(w, span(b0 + 256 * u))
    yield columns_unit(w, np.concatenate([span(bk, HD), span(bk, HD), span(bk + HD, HD), span(bk + HD, HD)]))
    yield columns_unit(w, np.concatenate([span(bv, P), span(bv, P)]))
    for half in range(2):
        for part in range(3):
            for g in range(A_GROUPS):
                yield columns_unit(w, span(part * gh + g * 512 + 256 * half))
    for u in range(6):
        yield columns_unit(w, span(ga + 256 * u))
    for br, name in enumerate(("w_br_a_2", "w_br_b_2", "w_br_m_2")):
        for u in range(2):
            yield rows_unit(a[name][0], 256 * u)
        for u in range(4):
            yield columns_unit(w, span(mg + br * D_MODEL + 256 * u))
    for u in range(4):
        yield columns_unit(a["w_out_2"][0], span(256 * u))


S_GAIN = 0
S_GPRE = S_GAIN + DEPTH * 4 * KC
S_GMEM = S_GPRE + KC
S_GPOST = S_GMEM + KC
S_LB = S_GPOST + KC
S_HGN = S_LB + DEPTH * KC
S_MLN = S_HGN + 2
S_BIF = S_MLN + KC
S_WIF = S_BIF + 2
S_SWN = S_WIF + KC * 8
S_SINK = S_SWN + 2
S_BN = S_SINK + SW_HEADS
S_BM = S_BN + 2
SMALLS = S_BM + 3 * KC


def small_parameters(inputs):
    a = {k: np.asarray(v) for k, v in inputs.items()}
    s = np.zeros((P, SMALLS), np.float32)

    def put(at, v):
        v = np.asarray(v).reshape(-1, P)
        s[:, at:at + v.shape[0]] = v.T
    put(S_GAIN, a["norm_gains"])
    put(S_GPRE, a["g_pre_2"])
    put(S_GMEM, a["g_mem_2"])
    put(S_GPOST, a["g_post_2"])
    put(S_LB, a["hg_lower_bounds"])
    put(S_HGN, a["hg_g_norm"])
    put(S_MLN, a["ml_norm"])
    s[0:4, S_BIF] = a["ml_b_if"][0, 0:4]
    s[0:4, S_BIF + 1] = a["ml_b_if"][0, 4:8]
    s[:, S_WIF:S_WIF + KC * 8] = a["ml_w_if"][0].reshape(KC, P, 8).transpose(1, 0, 2).reshape(P, KC * 8)
    for i, name in enumerate(("sw_q_norm", "sw_k_norm")):
        s[:, S_SWN + i] = np.tile(a[name][0], 2)
    s[:, S_SINK:S_SINK + SW_HEADS] = a["sw_sinks"][0][None, :]
    for i, name in enumerate(("q_norm_2", "k_norm_2")):
        s[:, S_BN + i] = np.tile(a[name][0], 2)
    put(S_BM, a["b_merge_2"])
    return s


LEVELS = (64, 32, 16, 8, 4, 2, 1)
NEG = -1e30


def constants():
    p = np.arange(P)
    ident = np.eye(P, dtype=np.float32)
    ones = np.ones((P, P), np.float32)
    halves = (p[:, None] // HD == p[None, :] // HD).astype(np.float32)
    causal = (p[:, None] <= p[None, :]).astype(np.float32)
    rot = np.zeros((P, P), np.float32)
    rot32 = np.zeros((P, P), np.float32)
    for m in range(P):
        for r, w in ((rot, HD), (rot32, HD // 2)):
            lo = m % w < w // 2
            r[m + w // 2 if lo else m - w // 2, m] = -1.0 if lo else 1.0
    selector = np.zeros((P, ML_HEADS, P), np.float32)
    for h in range(ML_HEADS):
        selector[h, h] = 1.0
    common = np.concatenate([ident, ones, halves, causal, rot, rot32, selector.reshape(P, -1)], axis=1)

    level = np.zeros((P, len(LEVELS), P), np.float32)
    for i, m in enumerate(LEVELS):
        s, t = p[:, None], p[None, :]
        level[:, i] = (s // (2 * m) == t // (2 * m)) & (s % (2 * m) < m) & (t % (2 * m) >= m)

    q, k = p[:, None], np.arange(2 * P)[None, :]
    dist = (q + P - k).astype(np.float32)
    window = np.where((dist >= 0) & (dist < 128), 0.0, NEG).astype(np.float32)
    swa = np.where(window < 0, NEG, -dist).astype(np.float32)

    pos = np.arange(T)
    d = p % HD
    inv = np.power(10000.0, -np.arange(HD // 2) * 2.0 / HD)
    ang = (pos[None, :] * inv[d % (HD // 2)][:, None])
    inv2 = np.power(10000.0, -np.arange(HD // 4) * 2.0 / (HD // 2))
    place = np.where((d < HD // 2)[:, None], (pos // 64)[None, :], (pos % 64)[None, :])
    ang2 = place * inv2[d % (HD // 4)][:, None]
    ropes = np.concatenate([np.cos(ang), np.sin(ang), np.cos(ang2), np.sin(ang2)], axis=1).astype(np.float32)
    tq = (np.arange(TB)[:, None, None, None] * P + p[None, :, None, None])
    tk = np.arange(T)[None, None, None, :]
    diff = np.abs(tq - tk)[:, :, 0, :]
    groups = np.stack([diff <= 64, diff % 4 == 0, diff % 16 == 0], axis=2)
    groups = np.where(groups, 0.0, NEG).astype(np.float32).transpose(1, 0, 2, 3).reshape(P, -1)
    return {
        "c_common": common,
        "c_levels": level.reshape(P, -1),
        "c_swa": swa,
        "c_second": np.concatenate([ropes, groups], axis=1),
    }


def lay_out(inputs, phases):
    x, p, mem = (np.asarray(inputs[n]) for n in ("x", "p", "mem_2"))

    def feature_major(a):
        return np.ascontiguousarray(a.T.reshape(-1, P, T).transpose(1, 0, 2))
    n = sum(KINDS[k]["units"] for k, _ in phases)
    weights = np.empty((n, P, UNIT), np.float32)
    for i, u in enumerate(weight_units(inputs, phases)):
        weights[i] = u
    assert i == n - 1
    out = {
        "x_t": feature_major(x[0]),
        "p_t": np.stack([feature_major(p[l, 0]) for l in range(DEPTH)]),
        "mem_t": feature_major(mem[0]),
        "weights": weights,
        "smalls": small_parameters(inputs),
    }
    out.update(constants())
    return out


def build(nc, phases, x_t, p_t, mem_t, weights, smalls_d, c_common, c_levels, c_swa, c_second, out):
    begin = starts(phases)
    NU = begin[-1]["units"]
    with ExitStack() as ctx:
        def sb(name, shape, dt=F32):
            return ctx.enter_context(nc.sbuf_tensor(name, shape, dt))

        def sem(name):
            return ctx.enter_context(nc.semaphore(name))

        raw = sb("raw", [P, RAW, UNIT])
        w_hi = sb("w_hi", [P, SPLIT, UNIT], F32R)
        w_lo = sb("w_lo", [P, SPLIT, UNIT], F32R)
        x = sb("x", [P, KC, T])
        xg_hi = sb("xg_hi", [P, KC, T], F32R)
        xg_lo = sb("xg_lo", [P, KC, T], F32R)
        mo_hi = sb("mo_hi", [P, KC, T], F32R)
        mo_lo = sb("mo_lo", [P, KC, T], F32R)
        common = sb("common", [P, 1280])
        smalls = sb("smalls", [P, SMALLS])
        levels = sb("levels", [P, len(LEVELS) * P], U8)
        rstd = sb("rstd", [P, T])
        rcol = sb("rcol", [P, 4])
        tiny = sb("tiny", [P, 96])
        S = sb("scratch", [P, 7 * UNIT + UNIT // 2])
        ps = ctx.enter_context(nc.psum_tensor("ps", [P, 8, 512], F32))

        eps = sb("eps", [P, 1])
        EPSB = eps[:, 0:1]

        ident, ones, halves, causal, rot, rot32 = (common[:, i * P:(i + 1) * P] for i in range(6))

        def selector(h):
            return common[0:ML_HEADS, (6 + h) * P:(7 + h) * P]

        def gain(at, c):
            return smalls[:, at + c:at + c + 1]

        def chunks(at, n, t=T):
            return S[:, at:at + n * t].rearrange("p (c t) -> p c t", t=t)

        raw_full = [sem(f"raw_full{i}") for i in range(RAW)]
        weights_hi = sem("weights_hi")
        weights_split = sem("weights_split")
        weights_used = sem("weights_used")
        bank_read = sem("bank_read")
        acc_ready = sem("acc_ready")
        consts_loaded = sem("consts_loaded")
        x_loaded = sem("x_loaded")
        x_updated = sem("x_updated")
        xg_ready = sem("xg_ready")
        squares_ready = sem("squares_ready")
        square_sum = sem("square_sum")
        sums_ready = sem("sums_ready")
        rstd_ready = sem("rstd_ready")
        up_scaled = sem("up_scaled")
        silu_ready = sem("silu_ready")
        mo_high = sem("mo_high")
        hidden_value = sem("hidden_value")
        hidden_hi = sem("hidden_hi")
        hidden_ready = sem("hidden_ready")
        p_loaded = sem("p_loaded")
        p_hi_ready = sem("p_hi_ready")
        p_ready = sem("p_ready")
        ple_gate = sem("ple_gate")
        eps_ready = sem("eps_ready")
        rcol_sums = sem("rcol_sums")
        rcol_ready = sem("rcol_ready")
        mo_ready = sem("mo_ready")
        dve_chain = sem("dve_chain")
        act_chain = sem("act_chain")
        phase_consts = sem("phase_consts")
        out_ready = sem("out_ready")
        out_stored = sem("out_stored")

        nphase = len(phases)

        def at(i, what):
            return begin[i].get(what, 0)

        def rcols(i):
            return sum(k not in ("ffn", "ple") for k, _ in phases[:i])

        def bank(e):
            return ps[:, e % BANKS, :]

        def next_gain(i):
            kind, layer = phases[i]
            if kind == "second":
                return S_GPRE
            place = {"hg": 1, "ml": 1, "sw": 1, "ple": 3}.get(kind)
            if place is None:
                place = 2 if i > 0 and phases[i - 1][0] in ("hg", "ml", "sw") else 0
            return S_GAIN + (4 * layer + place) * KC

        SQ = chunks(0, KC)
        SQ_SUM = S[:, UNIT:UNIT + T]
        FFN_T = chunks(UNIT + T, 6)
        FFN_H = chunks(UNIT + 7 * T, 2)
        PLE_P = chunks(6 * UNIT, 2)
        PLE_T = chunks(2 * UNIT, KC)
        HG_B, HG_Q, HG_K = (chunks(i * UNIT, KC) for i in range(3))
        HG_V = S[:, 3 * UNIT:4 * UNIT].rearrange("p (b f) -> p b f", b=TB)
        HG_D = [S[:, (4 + i) * UNIT:(5 + i) * UNIT] for i in range(2)]
        HG_AT = S[:, 6 * UNIT:7 * UNIT].rearrange("p (g t) -> p g t", t=P)
        HG_OFF = S[:, 7 * UNIT:7 * UNIT + 1024].rearrange("p (h t) -> p h t", t=P)
        HG_SQ = HG_D[0].rearrange("p (c t) -> p c t", t=T)
        HG_RS = HG_D[1].rearrange("p (c t) -> p c t", t=T)
        LEVELS_IN = S[:, 0:len(LEVELS) * P]
        HG_FLAT_B, HG_FLAT_Q, HG_FLAT_K = (S[:, i * UNIT:(i + 1) * UNIT] for i in range(3))
        OUT = chunks(UNIT, KC)
        ML_Q = chunks(UNIT, 4)
        ML_K = chunks(UNIT + 1024, 4)
        ML_V = S[:, 2 * UNIT:3 * UNIT].rearrange("p (b f) -> p b f", b=TB)
        ML_H = chunks(3 * UNIT, KC)
        ML_W = S[:, 4 * UNIT:4 * UNIT + ML_HEADS * 384].rearrange("p (h t) -> p h t", t=384)
        ML_GUARD = chunks(5 * UNIT, 4)
        ML_DEN = chunks(5 * UNIT + 1024, 4)
        ML_ROWS = chunks(6 * UNIT, 8)
        ML_T = chunks(0, KC)
        ATT_P = [S[:, 4 * UNIT + i * 1024:4 * UNIT + (i + 1) * 1024] for i in range(2)]
        ATT_PT = [S[:, 5 * UNIT + i * 1024:5 * UNIT + (i + 1) * 1024] for i in range(2)]
        SW_QK = chunks(UNIT, 12)
        SW_V = S[:, 5120:5632].rearrange("p (b f) -> p b f", b=TB)
        SW_SQ = chunks(3 * UNIT, 8)
        SW_O = chunks(6 * UNIT, 8)
        SW_BIAS = S[:, 7 * UNIT:7 * UNIT + 256]
        SE_QM, SE_KM = chunks(0, 4), chunks(1024, 4)
        SE_VM = S[:, 2048:3072].rearrange("p (b f) -> p b f", b=TB)
        SE_QB, SE_KB = chunks(3072, 4), chunks(4096, 2)
        SE_VB = S[:, 4608:4864].rearrange("p (b f) -> p b f", b=TB)
        SE_QA, SE_KA = chunks(0, 6), chunks(1536, 6)
        SE_VA = S[:, 3072:4608].rearrange("p (b f) -> p b f", b=TB)
        SE_O = chunks(4864, 12)
        SE_MSUM, SE_RMEM = S[:, 4864:5120], S[:, 5120:5376]
        SE_MEM, SE_MSQ = chunks(4 * UNIT, KC), chunks(5 * UNIT, KC)
        SE_SQ = chunks(4 * UNIT, 6)
        SE_X = [chunks(4 * UNIT + i * 512, 2) for i in range(2)]
        SE_COS = [chunks(5 * UNIT + i * 512, 2) for i in range(2)]
        SE_SIN = [chunks(5 * UNIT + 1024 + i * 512, 2) for i in range(2)]
        SE_GATE = [chunks(4 * UNIT + i * 512, 2) for i in range(2)]
        SE_MERGED, SE_Y, SE_YSQ = chunks(0, KC), chunks(2048, KC), chunks(5 * UNIT, KC)
        SE_YSUM, SE_YR = S[:, 4 * UNIT:4 * UNIT + T], S[:, 4 * UNIT + T:4 * UNIT + 2 * T]
        SE_CONST = S[:, 6 * UNIT:6 * UNIT + 2560]
        COS, SIN, COS2, SIN2 = (S[:, 6 * UNIT + i * T:6 * UNIT + (i + 1) * T] for i in range(4))
        SE_MASK = S[:, 6 * UNIT + 1024:6 * UNIT + 2560].rearrange("p (b k) -> p b k", b=TB)

        def head_half(h):
            return slice((h % 2) * HD, (h % 2 + 1) * HD)

        def quad_groups(Q, K, V, kvs, window):
            out = []
            for kv in range(kvs):
                for n in range(TB):
                    k0 = P if window and n == 0 else 0
                    g = dict(slots=4, width=256, k0=k0, scale=HD ** -0.5, scores=[], values=[], kv=kv, n=n)
                    for hh in range(4):
                        r, slot = head_half(hh), (hh % 2) * 2 + hh // 2
                        c = 2 * kv + hh // 2
                        keys = slice(0, T - k0)
                        g["scores"].append((slot * 256 + k0, T - k0, Q[r, c, n * P:(n + 1) * P], K[r, kv, keys]))
                        vs = [(V[:, (b * P - k0) // P, kv * HD:(kv + 1) * HD], 2 * slot + b) for b in range(k0 // P, 2)]
                        g["values"].append((r, (hh // 2) * P, vs))
                    out.append(g)
            return out

        def memory_groups():
            out = []
            for n in range(TB):
                g = dict(slots=4, width=256, k0=0, scale=P ** -0.5, scores=[], values=[], n=n)
                for h in range(M_HEADS):
                    g["scores"].append((h * 256, 256, SE_QM[:, h, n * P:(n + 1) * P], SE_KM[:, h, :]))
                    vs = [(SE_VM[:, b, h * P:(h + 1) * P], 2 * h + b) for b in range(2)]
                    g["values"].append((slice(0, P), h * P, vs))
                out.append(g)
            return out

        def dilated_groups():
            out = []
            for h in range(4):
                for n in range(TB):
                    r = head_half(h)
                    g = dict(slots=1, width=768, k0=0, scale=HD ** -0.5, scores=[], values=[], h=h, n=n)
                    for a in range(A_GROUPS):
                        c = 2 * a + h // 2
                        g["scores"].append((a * 256, 256, SE_QA[r, c, n * P:(n + 1) * P], SE_KA[r, c, :]))
                    vs = [(SE_VA[:, b, a * 256 + h * HD:a * 256 + (h + 1) * HD], 2 * a + b)
                          for a in range(A_GROUPS) for b in range(2)]
                    g["values"].append((r, 0, vs))
                    out.append(g)
            return out

        def new_sems(tag, names):
            return {n: sem(f"{tag}_{n}") for n in names.split()}

        ATT = "scores bias exp probs turned pt out taken"
        own = []
        for i, (kind, _) in enumerate(phases):
            names = {"hg": "lbdiff lbexp sig clamp qsilu logf scan diff exp qk level taken off o sq sums rs done gate prod",
                     "ml": "wif gates lin soft row cols ucol bcast arg exp scores w num den guard gexp nrm h sq sums rs done gate prod",
                     "sw": "sq sums rs qk",
                     "second": "memhi memready memsq memsum memsums memrs memcols sq sums rs x rot roped gate gated mhi mlo merge merged high low fsq fsum fin frs"
                     }.get(kind, "")
            own.append(new_sems(f"{kind}{i}", names) if names else {})
        att = new_sems("att", ATT)

        def att_before(i, stage=0):
            g = 2 * SW_KV * sum(k == "sw" for k, _ in phases[:i])
            return g + sum((2, 4, 8, 8)[:stage])


        block = ctx.enter_context(nc.Block())

        @block.sync
        def _(sp):
            sp.dma_start(x[:], x_t).then_inc(x_loaded, 16)
            sp.dma_start(smalls[:], smalls_d).then_inc(x_loaded, 16)
            for i in range(RAW):
                sp.dma_start(raw[:, i, :], weights[i]).then_inc(raw_full[i], 16)
            rounds = NU // RAW
            with sp.Fori(1, rounds) as it:
                for i in range(RAW):
                    sp.wait_ge(weights_split, RAW * it + (i + 1 - RAW))
                    sp.dma_start(raw[:, i, :], weights[RAW * it + i]).then_inc(raw_full[i], 16)
            for n in range(rounds * RAW, NU):
                sp.wait_ge(weights_split, n + 1 - RAW)
                sp.dma_start(raw[:, n % RAW, :], weights[n]).then_inc(raw_full[n % RAW], 16)
            sp.wait_ge(out_ready, 1)
            sp.dma_start(out, x[:]).then_inc(out_stored, 16)
            sp.wait_ge(out_stored, 16)

        @block.gpsimd
        def _(pool):
            pool.dma_start(common[:], c_common).then_inc(consts_loaded, 16)
            pool.dma_start(LEVELS_IN, c_levels).then_inc(consts_loaded, 16)
            seen = 0
            for i, (kind, layer) in enumerate(phases):
                if kind == "ple":
                    pool.wait_ge(x_updated, KC * i)
                    pool.dma_start(PLE_P, p_t[layer]).then_inc(p_loaded, 16)
                elif kind == "sw":
                    pool.wait_ge(x_updated, KC * (i + 1))
                    pool.dma_start(SW_BIAS, c_swa).then_inc(phase_consts, 16)
                elif kind == "second":
                    pool.wait_ge(x_updated, KC * (i + 1))
                    pool.dma_start(SE_MEM, mem_t).then_inc(p_loaded, 16)
                    pool.dma_start(SE_CONST, c_second).then_inc(phase_consts, 16)


        @block.tensor
        def _(pe):
            def passes(w, a, k, wc, ac, w_first):
                for wp, ap in ((w_hi, a[0]), (w_lo, a[0]), (w_hi, a[1])):
                    weight = wp[:, w, wc]
                    act = ap[:, k, ac]
                    yield (weight, act) if w_first else (act, weight)

            XG = (xg_hi, xg_lo)
            MO = (mo_hi, mo_lo)

            def project(n, e, a, operand_ready=None, dn=0, de=0):
                pe.wait_ge(weights_split, n + 1 + dn)
                pe.wait_ge(bank_read, e + 1 + de)
                for half in range(2):
                    for k in range(KC):
                        if operand_ready and half == 0:
                            pe.wait_ge(operand_ready[0], operand_ready[1] + k + 1)
                        wc = slice(k * 256 + half * P, k * 256 + (half + 1) * P)
                        for j, (l, r) in enumerate(passes(n % SPLIT, a, k, wc, slice(0, T), True)):
                            last = nc.tensor.matmul(bank(e)[:, half * T:(half + 1) * T], l, r,
                                                    start=(k == 0 and j == 0), stop=(k == KC - 1 and j == 2))
                last.then_inc(weights_used, 1)

            def project_tokens(n, e, a):
                pe.wait_ge(weights_split, n + 1)
                pe.wait_ge(bank_read, e + 1)
                for b in range(TB):
                    for k in range(KC):
                        wc = slice(k * 256, (k + 1) * 256)
                        for j, (l, r) in enumerate(passes(n % SPLIT, a, k, wc, slice(b * P, (b + 1) * P), False)):
                            last = nc.tensor.matmul(bank(e)[:, b * T:(b + 1) * T], l, r,
                                                    start=(k == 0 and j == 0), stop=(k == KC - 1 and j == 2))
                last.then_inc(weights_used, 1)

            def rows(n, a, slot, first, last_unit, dn=0, chunk_sem=None):
                pe.wait_ge(weights_split, n + 1 + dn)
                for c in range(KC):
                    for k in range(2):
                        wc = slice(k * D_MODEL + c * P, k * D_MODEL + (c + 1) * P)
                        for j, (l, r) in enumerate(passes(n % SPLIT, a, slot + k, wc, slice(0, T), True)):
                            last = nc.tensor.matmul(ps[:, 4 + c // 2, (c % 2) * T:(c % 2 + 1) * T], l, r,
                                                    start=(first and k == 0 and j == 0 and c % 2 == 0),
                                                    stop=(last_unit and k == 1 and j == 2), skip_group_check=True)
                    if chunk_sem is not None and c in (1, 3, 5):
                        last.then_inc(chunk_sem, 1)
                last.then_inc(weights_used, 1)

            def norm_sums(i, e, ready=square_sum, done=sums_ready):
                pe.wait_ge(bank_read, e + 1)
                pe.wait_ge(ready, i + 1)
                nc.tensor.matmul(bank(e)[:, 0:T], ones, SQ_SUM, start=True, stop=True).then_inc(done, 1)

            def token_columns(i, e):
                pe.wait_ge(rstd_ready, i + 1)
                for b in range(TB):
                    last = nc.tensor.matmul(bank(e)[:, 256 + b:257 + b], rstd[0:1, b * P:(b + 1) * P],
                                            ones[0:1, 0:1], start=True, stop=True)
                last.then_inc(rcol_sums, 1)

            def ffn(i):
                n0, e0, h0 = at(i, "units"), at(i, "banks"), at(i, "hidden")
                x0 = KC * i
                project(n0, e0, XG, (xg_ready, x0))
                norm_sums(i, e0 + 3)
                project(n0 + 1, e0 + 1, XG)
                project(n0 + 2, e0 + 2, XG)
                pe.wait_ge(rstd_ready, i + 1)
                project(n0 + 3, e0 + 3, XG)

                def down(s, n, dn=0, dh=0):
                    pe.wait_ge(hidden_ready, h0 + 2 * s + 2 + dh)
                    rows(n, MO, (2 * s) % 4, first=(s == 0), last_unit=(s == STEPS - 1), dn=dn,
                         chunk_sem=acc_ready if s == STEPS - 1 else None)
                down(0, n0 + 4)
                with pe.Fori(0, (STEPS - 3) // 2) as it:
                    for s in (2, 3):
                        project(n0 + 3 * s - 1, e0 + 2 * s, XG, dn=6 * it, de=4 * it)
                        project(n0 + 3 * s, e0 + 2 * s + 1, XG, dn=6 * it, de=4 * it)
                        down(s - 1, n0 + 3 * s + 1, dn=6 * it, dh=4 * it)
                s = STEPS - 1
                project(n0 + 3 * s - 1, e0 + 2 * s, XG)
                project(n0 + 3 * s, e0 + 2 * s + 1, XG)
                down(s - 1, n0 + 3 * s + 1)
                down(s, n0 + 3 * s + 2)

            def ple(i):
                n0, e0, x0 = at(i, "units"), at(i, "banks"), KC * i
                pe.wait_ge(p_ready, at(i, "ple") + 1)
                rows(n0, MO, 0, True, True)
                project(n0 + 1, e0, XG, (xg_ready, x0))
                norm_sums(i, e0 + 3)
                project(n0 + 2, e0 + 1, XG)
                project(n0 + 3, e0 + 2, XG)
                pe.wait_ge(rstd_ready, i + 1)
                project(n0 + 4, e0 + 3, XG)

            def mixer_head(i):
                n0, e0 = at(i, "units"), at(i, "banks")
                project(n0, e0, XG, (xg_ready, KC * i))
                norm_sums(i, e0 + 3)
                project(n0 + 1, e0 + 1, XG)
                token_columns(i, e0 + 3)
                project(n0 + 2, e0 + 2, XG)
                pe.wait_ge(rcol_ready, rcols(i) + 1)
                project(n0 + 3, e0 + 3, XG)

            def w_out(n, e):
                for u in range(4):
                    project(n + u, e + u, MO)

            def hg(i):
                m = own[i]
                n0, e0 = at(i, "units"), at(i, "banks")
                mixer_head(i)
                for u in range(4, 8):
                    project(n0 + u, e0 + u, XG)
                for u in range(8, 12):
                    project_tokens(n0 + u, e0 + u, XG)
                pe.wait_ge(bank_read, e0 + 12 + 4)
                pe.wait_ge(m["qsilu"], 4)
                pe.wait_ge(m["qk"], 1)
                for g in range(16):
                    h, b = g // 2, g % 2
                    last = nc.tensor.matmul(ps[:, g // 4, (g % 4) * P:(g % 4 + 1) * P],
                                            HG_K[:, h, b * P:(b + 1) * P], HG_Q[:, h, b * P:(b + 1) * P],
                                            start=True, stop=True)
                last.then_inc(m["level"], 1)
                for l in range(len(LEVELS)):
                    pe.wait_ge(m["qk"], l + 2)
                    if l >= 1:
                        pe.wait_ge(m["taken"], l)
                    D = HG_D[l % 2]
                    for g in range(16):
                        blk = D[:, g * P:(g + 1) * P]
                        last = nc.tensor.matmul(ps[:, 4 * ((l + 1) % 2) + g // 4, (g % 4) * P:(g % 4 + 1) * P],
                                                blk, blk, start=True, stop=True)
                    last.then_inc(m["level"], 1)
                l = len(LEVELS)
                pe.wait_ge(m["qk"], l + 2)
                pe.wait_ge(m["taken"], l)
                D = HG_D[l % 2]
                for h in range(HG_HEADS):
                    last = nc.tensor.matmul(ps[:, h // 4, (h % 4) * P:(h % 4 + 1) * P],
                                            D[:, h * T:h * T + P], D[:, h * T + P:(h + 1) * T],
                                            start=True, stop=True)
                last.then_inc(m["level"], 1)
                pe.wait_ge(m["taken"], len(LEVELS) + 1)
                pe.wait_ge(m["off"], 1)
                for h in range(HG_HEADS):
                    o = ps[:, h // 2, (h % 2) * T:(h % 2 + 1) * T]
                    v = HG_V[:, :, h * P:(h + 1) * P]
                    nc.tensor.matmul(o[:, 0:P], v[:, 0, :], HG_AT[:, 2 * h, :], start=True, stop=True)
                    nc.tensor.matmul(o[:, P:T], v[:, 0, :], HG_OFF[:, h, :], start=True, stop=False)
                    last = nc.tensor.matmul(o[:, P:T], v[:, 1, :], HG_AT[:, 2 * h + 1, :], start=False, stop=True)
                    if h % 2:
                        last.then_inc(m["o"], 1)
                for h in range(HG_HEADS):
                    if h % 2 == 0:
                        pe.wait_ge(m["sq"], h // 2 + 1)
                    last = nc.tensor.matmul(ps[:, 4 + h // 2, (h % 2) * T:(h % 2 + 1) * T], ones, HG_SQ[:, h, :],
                                            start=True, stop=True)
                    if h % 2:
                        last.then_inc(m["sums"], 1)
                pe.wait_ge(m["done"], 4)
                for u in range(12, 16):
                    project(n0 + u, e0 + u, XG)
                pe.wait_ge(mo_ready, 4 * rcols(i) + 4)
                w_out(n0 + 16, e0 + 16)

            def ml(i):
                m = own[i]
                n0, e0 = at(i, "units"), at(i, "banks")
                mixer_head(i)
                pe.wait_ge(m["wif"], 1)
                for g in range(2):
                    for k in range(KC):
                        last = nc.tensor.matmul(ps[0:4, 4, g * T:(g + 1) * T], tiny[:, k * 8 + 4 * g:k * 8 + 4 * g + 4],
                                                x[:, k, :], start=(k == 0), stop=(k == KC - 1))
                last.then_inc(m["gates"], 1)
                for u in range(4, 8):
                    project_tokens(n0 + u, e0 + u, XG)
                pe.wait_ge(m["row"], 1)
                for b in range(TB):
                    last = nc.tensor.matmul(ps[:, 4, 4 * b:4 * b + 4], ML_ROWS[0:4, 4, b * P:(b + 1) * P],
                                            ident[0:4, 0:4], start=True, stop=True)
                last.then_inc(m["cols"], 1)
                for h in range(ML_HEADS):
                    last = nc.tensor.matmul(ps[:, 6 + h // 2, (h % 2) * T:(h % 2 + 1) * T], selector(h),
                                            ML_ROWS[0:4, 6, :], start=True, stop=True)
                last.then_inc(m["bcast"], 1)
                pe.wait_ge(bank_read, e0 + 8 + 4)
                for h in range(ML_HEADS):
                    nc.tensor.matmul(ps[:, h, 0:T], ML_K[:, h, 0:P], ML_Q[:, h, :], start=True, stop=True)
                    nc.tensor.matmul(ps[:, h, T:T + P], ML_K[:, h, P:T], ML_Q[:, h, P:T],
                                     start=True, stop=True).then_inc(m["scores"], 1)
                pe.wait_ge(m["ucol"], 1)
                for h in range(ML_HEADS):
                    pe.wait_ge(m["w"], h + 1)
                    w0, w1 = ML_W[:, h, 0:T], ML_W[:, h, T:T + P]
                    for d in range(2):
                        v = ML_V[:, :, h * ML_DV + d * P:h * ML_DV + (d + 1) * P]
                        nc.tensor.matmul(ps[:, h, d * T:(d + 1) * T], v[:, 0], w0, start=True, stop=False,
                                         skip_group_check=True)
                        last = nc.tensor.matmul(ps[:, h, d * T + P:(d + 1) * T], v[:, 1], w1, start=False, stop=True,
                                                skip_group_check=True)
                    last.then_inc(m["num"], 1)
                    o = ps[:, 4 + h // 2, (h % 2) * T:(h % 2 + 1) * T]
                    nc.tensor.matmul(o, ones, w0, start=True, stop=False, skip_group_check=True)
                    nc.tensor.matmul(o[:, P:T], ones, w1, start=False, stop=True,
                                     skip_group_check=True).then_inc(m["den"], 1)
                pe.wait_ge(m["arg"], ML_HEADS)
                for h in range(ML_HEADS):
                    last = nc.tensor.matmul(ps[:, 6 + h // 2, (h % 2) * T:(h % 2 + 1) * T], selector(h),
                                            ML_ROWS[0:4, 7, :], start=True, stop=True)
                last.then_inc(m["guard"], 1)
                pe.wait_ge(m["nrm"], 1)
                for h in range(ML_HEADS):
                    pe.wait_ge(m["sq"], h + 1)
                    o = ps[:, 4 + h // 2, (h % 2) * T:(h % 2 + 1) * T]
                    nc.tensor.matmul(o, ones, ML_T[:, 2 * h], start=True, stop=False)
                    last = nc.tensor.matmul(o, ones, ML_T[:, 2 * h + 1], start=False, stop=True)
                    if h % 2:
                        last.then_inc(m["sums"], 1)
                pe.wait_ge(m["h"], ML_HEADS)
                for u in range(8, 12):
                    project(n0 + u, e0 + u, XG)
                pe.wait_ge(mo_ready, 4 * rcols(i) + 4)
                w_out(n0 + 12, e0 + 12)

            def attention(g0, groups):
                def scores(g):
                    if g >= len(groups):
                        return
                    if g >= 2:
                        pe.wait_ge(att["exp"], g0 + g - 1)
                    for at_, n, q, k in groups[g]["scores"]:
                        at_ += 1024 * (g % 2)
                        last = nc.tensor.matmul(ps[:, at_ // 512, at_ % 512:at_ % 512 + n], q, k, start=True, stop=True)
                    last.then_inc(att["scores"], 1)

                scores(0)
                scores(1)
                for g, G in enumerate(groups):
                    pe.wait_ge(att["probs"], g0 + g + 1)
                    if g >= 1:
                        pe.wait_ge(att["pt"], g0 + g)
                    for j in range(G["slots"] * G["width"] // P):
                        if (j * P) % 256 >= G["k0"]:
                            last = nc.tensor.transpose(ps[:, 4 + j // 4, (j % 4) * P:(j % 4 + 1) * P],
                                                       ATT_P[g % 2][:, j * P:(j + 1) * P], ident)
                    last.then_inc(att["turned"], 1)
                    scores(g + 2)
                    pe.wait_ge(att["pt"], g0 + g + 1)
                    if g >= 2:
                        pe.wait_ge(att["taken"], g0 + g - 1)
                    for r, col, vs in G["values"]:
                        for j, (v, block_) in enumerate(vs):
                            last = nc.tensor.matmul(ps[r, 6 + g % 2, col:col + P], v,
                                                    ATT_PT[g % 2][:, block_ * P:(block_ + 1) * P],
                                                    start=(j == 0), stop=(j == len(vs) - 1))
                    last.then_inc(att["out"], 1)

            def sw(i):
                m = own[i]
                n0, e0 = at(i, "units"), at(i, "banks")

                def sums(p):
                    pe.wait_ge(m["sq"], p + 1)
                    nc.tensor.matmul(ps[:, 4 + p % 4, :], halves,
                                     SW_SQ[:, 2 * (p % 4):2 * (p % 4) + 2].rearrange("p c t -> p (c t)"),
                                     start=True, stop=True).then_inc(m["sums"], 1)
                mixer_head(i)
                for p in range(4):
                    sums(p)
                project(n0 + 4, e0 + 4, XG)
                project(n0 + 5, e0 + 5, XG)
                project_tokens(n0 + 6, e0 + 6, XG)
                pe.wait_ge(m["rs"], 4)
                sums(4)
                sums(5)
                pe.wait_ge(bank_read, e0 + 7 + 4)
                pe.wait_ge(m["qk"], 6)
                attention(att_before(i), quad_groups(SW_QK, SW_QK[:, 8:12], SW_V, SW_KV, True))
                pe.wait_ge(mo_ready, 4 * rcols(i) + 4)
                w_out(n0 + 7, e0 + 7)

            def banks_clear(g):
                for what in ("exp", "pt", "taken"):
                    pe.wait_ge(att[what], g)

            def second(i):
                m = own[i]
                n0, e0 = at(i, "units"), at(i, "banks")
                project(n0, e0, MO, (m["memready"], 0))
                norm_sums(i, e0 + 3)
                project(n0 + 1, e0 + 1, MO)
                pe.wait_ge(m["memsum"], 1)
                nc.tensor.matmul(ps[:, 4, 0:T], ones, SE_MSUM, start=True, stop=True).then_inc(m["memsums"], 1)
                token_columns(i, e0 + 3)
                pe.wait_ge(m["memrs"], 1)
                for b in range(TB):
                    last = nc.tensor.matmul(ps[:, 4, T + b:T + b + 1], SE_RMEM[0:1, b * P:(b + 1) * P], ones[0:1, 0:1],
                                            start=True, stop=True)
                last.then_inc(m["memcols"], 1)
                project_tokens(n0 + 2, e0 + 2, MO)
                pe.wait_ge(rcol_ready, rcols(i) + 1)
                project_tokens(n0 + 3, e0 + 3, MO)
                project(n0 + 4, e0 + 4, XG, (xg_ready, KC * i))
                for u in range(5, 9):
                    project(n0 + u, e0 + u, XG)
                project_tokens(n0 + 9, e0 + 9, XG)
                for p in range(3):
                    pe.wait_ge(m["sq"], p + 1)
                    nc.tensor.matmul(ps[:, 5 + p, :], halves,
                                     SE_SQ[:, 2 * p:2 * p + 2].rearrange("p c t -> p (c t)"),
                                     start=True, stop=True).then_inc(m["sums"], 1)
                for p in range(3):
                    pe.wait_ge(m["x"], p + 1)
                    pair = (SE_QB[:, 2 * p:2 * p + 2] if p < 2 else SE_KB).rearrange("p c t -> p (c t)")
                    nc.tensor.matmul(ps[:, 5 + p, :], rot32, pair, start=True, stop=True).then_inc(m["rot"], 1)
                pe.wait_ge(bank_read, e0 + 10 + 4)
                attention(att_before(i, 0), memory_groups())
                pe.wait_ge(m["roped"], 3)
                banks_clear(att_before(i, 1))
                attention(att_before(i, 1), quad_groups(SE_QB, SE_KB, SE_VB, 2, False))
                for half in range(2):
                    u0 = 10 + 9 * half
                    banks_clear(att_before(i, 2 + half))

                    def turn(p):
                        r = 3 + 6 * half + p
                        pe.wait_ge(bank_read, e0 + u0 + p + 5)
                        if p >= 2:
                            pe.wait_ge(m["roped"], r - 1)
                        nc.tensor.matmul(ps[:, 4 + p % 2, :], rot, SE_X[p % 2].rearrange("p c t -> p (c t)"),
                                         start=True, stop=True).then_inc(m["rot"], 1)
                    for u in range(6):
                        project(n0 + u0 + u, e0 + u0 + u, XG)
                        if u:
                            turn(u - 1)
                    project_tokens(n0 + u0 + 6, e0 + u0 + 6, XG)
                    turn(5)
                    project_tokens(n0 + u0 + 7, e0 + u0 + 7, XG)
                    project_tokens(n0 + u0 + 8, e0 + u0 + 8, XG)
                    pe.wait_ge(bank_read, e0 + u0 + 9 + 4)
                    pe.wait_ge(m["roped"], 9 + 6 * half)
                    attention(att_before(i, 2 + half), dilated_groups())
                banks_clear(att_before(i, 4))
                for u in range(28, 34):
                    project(n0 + u, e0 + u, XG)
                n, e = n0 + 34, e0 + 34
                for br in range(3):
                    pe.wait_ge(m["mlo"], br + 1)
                    if br:
                        pe.wait_ge(m["merged"], 4 * br)
                    rows(n, MO, 4 * (br % 2), True, False)
                    rows(n + 1, MO, 4 * (br % 2) + 2, False, True)
                    for u in range(4):
                        project(n + 2 + u, e + u, XG)
                    n, e = n + 6, e + 4
                for u in range(4):
                    pe.wait_ge(m["low"], 4)
                    project(n + u, e + u, MO)
                pe.wait_ge(m["fsum"], 1)
                nc.tensor.matmul(ps[:, 4, 0:T], ones, SE_YSUM, start=True, stop=True).then_inc(m["fin"], 1)

            for i, (kind, _) in enumerate(phases):
                if i == 0:
                    pe.wait_ge(consts_loaded, 32)
                {"ffn": ffn, "ple": ple, "hg": hg, "ml": ml, "sw": sw, "second": second}[kind](i)

        @block.scalar
        def _(act):
            def high(m, dm=0, turn=0):
                if m >= NU:
                    return
                act.wait_ge(raw_full[m % RAW], 16 * turn + 16 * (m // RAW + 1))
                if m >= SPLIT:
                    act.wait_ge(weights_used, m + 1 - SPLIT + dm)
                nc.scalar.copy(w_hi[:, m % SPLIT, :], raw[:, m % RAW, :]).then_inc(weights_hi, 1)

            def norm(i):
                act.wait_ge(x_updated, KC * (i + 1))
                nc.scalar.activation(SQ, x[:], ACT.Square).then_inc(squares_ready, 1)
                act.wait_ge(sums_ready, i + 1)
                sums = bank(at(i, "banks") + 3)[:, 0:T]
                nc.scalar.activation(rstd[:], sums, ACT.Ln, bias=EPSB, scale=1.0 / D_MODEL).then_inc(act_chain, 1)
                chain[0] += 1
                act.wait_ge(act_chain, chain[0])
                nc.scalar.activation(rstd[:], rstd[:], ACT.Exp, scale=-0.5).then_inc(rstd_ready, 1)

            chain = [0]

            def link(ins):
                chain[0] += 1
                ins.then_inc(act_chain, 1)
                act.wait_ge(act_chain, chain[0])

            def ffn(i):
                n0, h0 = at(i, "units"), at(i, "hidden")
                norm(i)

                def up(j, n, dn=0, dh=0, turn=0):
                    act.wait_ge(up_scaled, h0 + j + 1 + dh)
                    nc.scalar.activation(FFN_T[:, 2 + j % 2], FFN_T[:, j % 2], ACT.Silu).then_inc(silu_ready, 1)
                    high(n + SPLIT, dn, turn)
                    act.wait_ge(hidden_value, h0 + j + 1 + dh)
                    nc.scalar.copy(mo_hi[:, j % 4], FFN_H[:, j % 2]).then_inc(hidden_hi, 1)
                for j in range(4):
                    up(j, n0 + j)
                high(n0 + 4 + SPLIT)
                with act.Fori(0, (STEPS - 3) // 2) as it:
                    for s in (2, 3):
                        up(2 * s, n0 + 3 * s - 1, 6 * it, 4 * it, it)
                        up(2 * s + 1, n0 + 3 * s, 6 * it, 4 * it, it)
                        high(n0 + 3 * s + 1 + SPLIT, 6 * it, it)
                s = STEPS - 1
                up(2 * s, n0 + 3 * s - 1)
                up(2 * s + 1, n0 + 3 * s)
                high(n0 + 3 * s + 1 + SPLIT)
                high(n0 + 3 * s + 2 + SPLIT)

            def ple(i):
                n0, e0 = at(i, "units"), at(i, "banks")
                act.wait_ge(p_loaded, 16 * (at(i, "ple") + 1))
                act.wait_ge(weights_used, n0)
                nc.scalar.copy(mo_hi[:, 0:2], PLE_P).then_inc(p_hi_ready, 1)
                norm(i)
                high(n0 + SPLIT)
                for u in range(4):
                    act.wait_ge(bank_read, e0 + u + 5)
                    pair = PLE_T[:, 2 * u:2 * u + 2]
                    nc.scalar.activation(pair, pair, ACT.Sigmoid).then_inc(ple_gate, 1)
                    high(n0 + 1 + u + SPLIT)

            def gates_out(i, m, unit, e, value, func):
                for u in range(4):
                    act.wait_ge(bank_read, e + u + 5)
                    pair = value[:, 2 * u:2 * u + 2]
                    nc.scalar.activation(pair, pair, func).then_inc(m["gate"], 1)
                    high(unit + u + SPLIT)
                    act.wait_ge(m["prod"], u + 1)
                    nc.scalar.copy(mo_hi[:, 2 * u:2 * u + 2], OUT[:, 2 * u:2 * u + 2]).then_inc(mo_high, 1)
                for u in range(4, 8):
                    high(unit + u + SPLIT)

            def hg(i):
                m = own[i]
                n0, e0 = at(i, "units"), at(i, "banks")
                if phases[i][1] > 0:
                    act.wait_ge(m["lbdiff"], 1)
                    nc.scalar.activation(tiny[:, 16:48], tiny[:, 16:48], ACT.Exp).then_inc(m["lbexp"], 1)
                norm(i)
                for u in range(4):
                    act.wait_ge(bank_read, e0 + u + 5)
                    k, b = HG_K[:, 2 * u:2 * u + 2], HG_B[:, 2 * u:2 * u + 2]
                    nc.scalar.activation(b, k, ACT.Sigmoid)
                    nc.scalar.activation(k, k, ACT.Sigmoid, scale=-1.0).then_inc(m["sig"], 1)
                    high(n0 + u + SPLIT)
                for c in range(KC):
                    act.wait_ge(m["clamp"], c // 2 + 1)
                    nc.scalar.activation(HG_B[:, c], HG_B[:, c], ACT.Ln, bias=tiny[:, 8 + c:9 + c],
                                         scale=tiny[:, c:c + 1]).then_inc(m["logf"], 1)
                for u in range(4, 8):
                    act.wait_ge(bank_read, e0 + u + 5)
                    q = HG_Q[:, 2 * (u - 4):2 * (u - 4) + 2]
                    nc.scalar.activation(q, q, ACT.Silu).then_inc(m["qsilu"], 1)
                    high(n0 + u + SPLIT)
                for u in range(8, 12):
                    high(n0 + u + SPLIT)
                for l, w in enumerate(LEVELS):
                    D = HG_D[l % 2].rearrange("p (n a w) -> p n a w", a=2, w=w)
                    for a in (1, 0):
                        act.wait_ge(m["diff"], 2 * l + 2 - a)
                        nc.scalar.activation(D[:, :, a, :], D[:, :, a, :], ACT.Exp).then_inc(m["exp"], 1)
                l = len(LEVELS)
                D = HG_D[l % 2].rearrange("p (h a w) -> p h a w", a=2, w=P)
                act.wait_ge(m["diff"], 2 * l + 1)
                nc.scalar.activation(D[:, :, 1, :], HG_B[:, :, P:T], ACT.Exp).then_inc(m["exp"], 1)
                nc.scalar.activation(D[:, :, 0, :], D[:, :, 0, :], ACT.Exp).then_inc(m["exp"], 1)
                act.wait_ge(m["level"], l + 2)
                nc.scalar.copy(HG_OFF[:, :, :].rearrange("p h t -> p (h t)"),
                               ps[:, 0:2, :].rearrange("p b t -> p (b t)")).then_inc(m["off"], 1)
                for p in range(4):
                    act.wait_ge(m["o"], p + 1)
                    nc.scalar.activation(HG_SQ[:, 2 * p:2 * p + 2].rearrange("p c t -> p (c t)"), ps[:, p, :],
                                         ACT.Square).then_inc(m["sq"], 1)
                for p in range(4):
                    act.wait_ge(m["sums"], p + 1)
                    ins = nc.scalar.activation(HG_RS[:, 2 * p:2 * p + 2].rearrange("p c t -> p (c t)"),
                                               ps[:, 4 + p, :], ACT.Ln, bias=EPSB, scale=1.0 / P)
                link(ins)
                for p in range(4):
                    r = HG_RS[:, 2 * p:2 * p + 2]
                    nc.scalar.activation(r, r, ACT.Exp, scale=-0.5).then_inc(m["rs"], 1)
                gates_out(i, m, n0 + 12, e0 + 12, HG_K, ACT.Silu)

            def ml(i):
                m = own[i]
                n0, e0 = at(i, "units"), at(i, "banks")
                norm(i)
                for u in range(8):
                    high(n0 + u + SPLIT)
                    if u == 4:
                        g, f, sp = ML_ROWS[0:4, 0:2], ML_ROWS[0:4, 1], ML_ROWS[0:4, 2]
                        act.wait_ge(m["lin"], 1)
                        link(nc.scalar.activation(g, g, ACT.Tanh, scale=1.0 / GATE_CAP))
                        link(nc.scalar.activation(sp, f, ACT.Exp, scale=-GATE_CAP))
                        nc.scalar.activation(sp, sp, ACT.Ln, bias=ones[0:4, 0:1]).then_inc(m["soft"], 1)
                for h in range(ML_HEADS):
                    act.wait_ge(m["arg"], h + 1)
                    nc.scalar.activation(ML_W[:, h], ML_W[:, h], ACT.Exp).then_inc(m["exp"], 1)
                act.wait_ge(m["guard"], 1)
                nc.scalar.activation(ML_GUARD.rearrange("p c t -> p (c t)"),
                                     ps[:, 6:8, :].rearrange("p b t -> p (b t)"), ACT.Exp).then_inc(m["gexp"], 1)
                act.wait_ge(m["den"], ML_HEADS)
                nc.scalar.activation(ML_DEN.rearrange("p c t -> p (c t)"),
                                     ps[:, 4:6, :].rearrange("p b t -> p (b t)"), ACT.Abs).then_inc(m["gexp"], 1)
                for h in range(ML_HEADS):
                    act.wait_ge(m["h"], h + 1)
                    nc.scalar.activation(ML_T[:, 2 * h:2 * h + 2], ML_H[:, 2 * h:2 * h + 2],
                                         ACT.Square).then_inc(m["sq"], 1)
                for p in range(2):
                    act.wait_ge(m["sums"], p + 1)
                    ins = nc.scalar.activation(ML_GUARD[:, 2 * p:2 * p + 2].rearrange("p c t -> p (c t)"), ps[:, 4 + p, :],
                                               ACT.Ln, bias=EPSB, scale=1.0 / ML_DV)
                link(ins)
                for p in range(2):
                    r = ML_GUARD[:, 2 * p:2 * p + 2]
                    nc.scalar.activation(r, r, ACT.Exp, scale=-0.5).then_inc(m["rs"], 1)
                gates_out(i, m, n0 + 8, e0 + 8, ML_T, ACT.Sigmoid)

            def attention(g0, groups, sinks=False, from_psum=False):
                def exps(g):
                    if g == len(groups):
                        return
                    G = groups[g]
                    t = tiny[:, 32 * (g % 2):32 * (g % 2) + 32]
                    act.wait_ge(att["bias"], g0 + g + 1)
                    if sinks:
                        nc.scalar.activation(t[:, 12:16], t[:, 12:16], ACT.Exp, scale=G["scale"])
                    for s in range(G["slots"]):
                        p = ATT_P[g % 2][:, s * G["width"] + G["k0"]:(s + 1) * G["width"]]
                        src = ps[:, 2 * (g % 2) + s // 2, (s % 2) * 256:(s % 2 + 1) * 256] if from_psum else p
                        last = nc.scalar.activation(p, src, ACT.Exp, bias=t[:, 4 + s:5 + s], scale=G["scale"],
                                                    accum_out=t[:, 8 + s:9 + s])
                    last.then_inc(att["exp"], 1)

                exps(0)
                for g, G in enumerate(groups):
                    exps(g + 1)
                    act.wait_ge(att["turned"], g0 + g + 1)
                    if g >= 2:
                        act.wait_ge(att["out"], g0 + g - 1)
                    n = G["slots"] * G["width"]
                    src = ps[:, 4:6, :].rearrange("p b t -> p (b t)")[:, 0:n]
                    dst = ATT_PT[g % 2][:, 0:n]
                    if G["k0"]:
                        src, dst = (v.rearrange("p (s k) -> p s k", k=256)[:, :, G["k0"]:] for v in (src, dst))
                    nc.scalar.copy(dst, src).then_inc(att["pt"], 1)

            def sw(i):
                m = own[i]
                n0, e0 = at(i, "units"), at(i, "banks")
                norm(i)

                def roots(p0, p1):
                    for p in range(p0, p1):
                        act.wait_ge(m["sums"], p + 1)
                        ins = nc.scalar.activation(
                            SW_SQ[:, 2 * (p % 4):2 * (p % 4) + 2].rearrange("p c t -> p (c t)"), ps[:, 4 + p % 4, :],
                            ACT.Ln, bias=EPSB, scale=1.0 / HD)
                    link(ins)
                    for p in range(p0, p1):
                        r = SW_SQ[:, 2 * (p % 4):2 * (p % 4) + 2]
                        nc.scalar.activation(r, r, ACT.Exp, scale=-0.5).then_inc(m["rs"], 1)

                for u in range(6):
                    act.wait_ge(bank_read, e0 + u + 5)
                    if u >= 4:
                        act.wait_ge(m["qk"], u - 3)
                    nc.scalar.activation(SW_SQ[:, 2 * (u % 4):2 * (u % 4) + 2], SW_QK[:, 2 * u:2 * u + 2],
                                         ACT.Square).then_inc(m["sq"], 1)
                    high(n0 + u + SPLIT)
                    if u == 3:
                        roots(0, 4)
                high(n0 + 6 + SPLIT)
                roots(4, 6)
                attention(att_before(i), quad_groups(SW_QK, SW_QK[:, 8:12], SW_V, SW_KV, True), sinks=True)
                for u in range(4):
                    act.wait_ge(att["taken"], att_before(i) + 2 * u + 2)
                    nc.scalar.copy(mo_hi[:, 2 * u:2 * u + 2], SW_O[:, 2 * u:2 * u + 2]).then_inc(mo_high, 1)
                for u in range(4):
                    high(n0 + 7 + u + SPLIT)

            def second(i):
                m = own[i]
                n0, e0 = at(i, "units"), at(i, "banks")
                norm(i)
                act.wait_ge(p_loaded, 16 * (at(i, "ple") + 1))
                nc.scalar.activation(SE_MSQ, SE_MEM, ACT.Square).then_inc(m["memsq"], 1)
                act.wait_ge(m["memsums"], 1)
                link(nc.scalar.activation(SE_RMEM, ps[:, 4, 0:T], ACT.Ln, bias=EPSB, scale=1.0 / D_MODEL))
                nc.scalar.activation(SE_RMEM, SE_RMEM, ACT.Exp, scale=-0.5).then_inc(m["memrs"], 1)
                for u in range(6):
                    high(n0 + u + SPLIT)
                for p in range(3):
                    act.wait_ge(bank_read, e0 + 6 + p + 5)
                    pair = SE_QB[:, 2 * p:2 * p + 2] if p < 2 else SE_KB
                    nc.scalar.activation(SE_SQ[:, 2 * p:2 * p + 2], pair, ACT.Square).then_inc(m["sq"], 1)
                    high(n0 + 6 + p + SPLIT)
                high(n0 + 9 + SPLIT)
                for p in range(3):
                    act.wait_ge(m["sums"], p + 1)
                    ins = nc.scalar.activation(SE_SQ[:, 2 * p:2 * p + 2].rearrange("p c t -> p (c t)"), ps[:, 5 + p, :],
                                               ACT.Ln, bias=EPSB, scale=1.0 / HD)
                link(ins)
                for p in range(3):
                    r = SE_SQ[:, 2 * p:2 * p + 2]
                    nc.scalar.activation(r, r, ACT.Exp, scale=-0.5).then_inc(m["rs"], 1)
                attention(att_before(i, 0), memory_groups(), from_psum=True)
                attention(att_before(i, 1), quad_groups(SE_QB, SE_KB, SE_VB, 2, False), from_psum=True)
                for half in range(2):
                    for u in range(9):
                        high(n0 + 10 + 9 * half + u + SPLIT)
                    attention(att_before(i, 2 + half), dilated_groups())
                for u in range(6):
                    act.wait_ge(bank_read, e0 + 28 + u + 5)
                    t = SE_GATE[u % 2]
                    nc.scalar.activation(t, t, ACT.Silu).then_inc(m["gate"], 1)
                    high(n0 + 28 + u + SPLIT)

                def fill(br):
                    if br == 2:
                        act.wait_ge(weights_used, n0 + 36)
                    s = 4 * (br % 2)
                    act.wait_ge(m["gated"], 6)
                    nc.scalar.copy(mo_hi[:, s:s + 4], SE_O[:, 4 * br:4 * br + 4]).then_inc(m["mhi"], 1)
                fill(0)
                fill(1)
                n, e = n0 + 34, e0 + 34
                for br in range(3):
                    high(n + SPLIT)
                    high(n + 1 + SPLIT)
                    if br == 1:
                        fill(2)
                    for u in range(4):
                        act.wait_ge(bank_read, e + u + 5)
                        t = SE_GATE[u % 2]
                        for c in range(2):
                            b = S_BM + 8 * br + 2 * u + c
                            ins = nc.scalar.activation(t[:, c], t[:, c], ACT.Sigmoid, bias=smalls[:, b:b + 1])
                        ins.then_inc(m["merge"], 1)
                        high(n + 2 + u + SPLIT)
                        if br == 2:
                            act.wait_ge(m["merged"], 8 + u + 1)
                            nc.scalar.copy(mo_hi[:, 2 * u:2 * u + 2],
                                           SE_MERGED[:, 2 * u:2 * u + 2]).then_inc(m["high"], 1)
                    n, e = n + 6, e + 4
                for u in range(4):
                    act.wait_ge(bank_read, e + u + 5)
                    nc.scalar.activation(SE_YSQ[:, 2 * u:2 * u + 2], SE_Y[:, 2 * u:2 * u + 2],
                                         ACT.Square).then_inc(m["fsq"], 1)
                    high(n + u + SPLIT)
                act.wait_ge(m["fin"], 1)
                link(nc.scalar.activation(SE_YR, ps[:, 4, 0:T], ACT.Ln, bias=EPSB, scale=1.0 / D_MODEL))
                nc.scalar.activation(SE_YR, SE_YR, ACT.Exp, scale=-0.5).then_inc(m["frs"], 1)

            act.wait_ge(eps_ready, 1)
            for i in range(SPLIT):
                high(i)
            for i, (kind, _) in enumerate(phases):
                {"ffn": ffn, "ple": ple, "hg": hg, "ml": ml, "sw": sw, "second": second}[kind](i)

        @block.vector
        def _(dve):
            chain = [0]

            def link(ins):
                chain[0] += 1
                ins.then_inc(dve_chain, 1)
                dve.wait_ge(dve_chain, chain[0])

            V = nc.vector

            def low(m, dm=0):
                if m >= NU:
                    return
                dve.wait_ge(weights_hi, m + 1 + dm)
                V.tensor_tensor(w_lo[:, m % SPLIT, :], raw[:, m % RAW, :], w_hi[:, m % SPLIT, :].bitcast(F32),
                                ALU.subtract).then_inc(weights_split, 1)

            def row(v, n):
                return v.unsqueeze(1).broadcast_to([P, n, T])

            def pair(e, fixed=False):
                return (ps[:, e, :] if fixed else bank(e)).rearrange("p (c t) -> p c t", c=2)

            def norm(i):
                dve.wait_ge(squares_ready, i + 1)
                V.tensor_reduce(SQ_SUM, SQ.rearrange("p c t -> p t c"), AX_X, ALU.add).then_inc(square_sum, 1)
                dve.wait_ge(rstd_ready, i + 1)

            def next_operand(i, c0, n):
                if i + 1 == nphase:
                    return
                g = next_gain(i + 1)
                for c in range(c0, c0 + n):
                    V.tensor_scalar(xg_hi[:, c], x[:, c], gain(g, c), None, ALU.mult).then_inc(x_updated, 1)
                for c in range(c0, c0 + n):
                    dve.wait_ge(x_updated, KC * (i + 1) + c + 1)
                    V.scalar_tensor_tensor(xg_lo[:, c], x[:, c], gain(g, c), xg_hi[:, c].bitcast(F32), ALU.mult,
                                           ALU.subtract).then_inc(xg_ready, 1)

            def scale(n, e, dst):
                dve.wait_ge(weights_used, n + 1)
                V.tensor_tensor(dst, pair(e), row(rstd[:], 2), ALU.mult).then_inc(bank_read, 1)

            def scale_tokens(n, e, dst, col):
                dve.wait_ge(weights_used, n + 1)
                for b in range(TB):
                    ins = V.tensor_scalar(dst[:, b], pair(e)[:, b], rcol[:, col + b:col + b + 1], None, ALU.mult)
                ins.then_inc(bank_read, 1)

            def columns(i, e, col=0):
                dve.wait_ge(rcol_sums, rcols(i) + 1 + (col > 0))
                V.tensor_copy(rcol[:, col:col + 2], bank(e)[:, 256:258]).then_inc(rcol_ready, 1)

            def ffn(i):
                n0, e0, h0 = at(i, "units"), at(i, "banks"), at(i, "hidden")
                norm(i)

                def up(j, n, dn=0, dh=0):
                    e = e0 + j
                    dve.wait_ge(weights_used, n + 1 + dn)
                    V.tensor_tensor(FFN_T[:, j % 2], pair(e)[:, 0], rstd[:], ALU.mult).then_inc(up_scaled, 1)
                    V.tensor_tensor(FFN_T[:, 4 + j % 2], pair(e)[:, 1], rstd[:], ALU.mult).then_inc(bank_read, 1)
                    dve.wait_ge(bank_read, e + 5 + dh)
                    dve.wait_ge(silu_ready, h0 + j + 1 + dh)
                    V.tensor_tensor(FFN_H[:, j % 2], FFN_T[:, 2 + j % 2], FFN_T[:, 4 + j % 2],
                                    ALU.mult).then_inc(hidden_value, 1)
                    low(n + SPLIT, dn)
                    dve.wait_ge(hidden_hi, h0 + j + 1 + dh)
                    V.tensor_tensor(mo_lo[:, j % 4], FFN_H[:, j % 2], mo_hi[:, j % 4].bitcast(F32),
                                    ALU.subtract).then_inc(hidden_ready, 1)
                for j in range(4):
                    up(j, n0 + j)
                low(n0 + 4 + SPLIT)
                with dve.Fori(0, (STEPS - 3) // 2) as it:
                    for s in (2, 3):
                        up(2 * s, n0 + 3 * s - 1, 6 * it, 4 * it)
                        up(2 * s + 1, n0 + 3 * s, 6 * it, 4 * it)
                        low(n0 + 3 * s + 1 + SPLIT, 6 * it)
                s = STEPS - 1
                up(2 * s, n0 + 3 * s - 1)
                up(2 * s + 1, n0 + 3 * s)
                low(n0 + 3 * s + 1 + SPLIT)
                for u in range(4):
                    if u < 3:
                        dve.wait_ge(acc_ready, at(i, "acc") + u + 1)
                    else:
                        dve.wait_ge(weights_used, n0 + HCH + STEPS)
                    two = x[:, 2 * u:2 * u + 2]
                    link(V.scalar_tensor_tensor(two, pair(4 + u, True), 0.5, two, ALU.mult, ALU.add))
                    next_operand(i, 2 * u, 2)
                low(n0 + 3 * s + 2 + SPLIT)

            def ple(i):
                n0, e0 = at(i, "units"), at(i, "banks")
                dve.wait_ge(p_hi_ready, at(i, "ple") + 1)
                V.tensor_tensor(mo_lo[:, 0:2], PLE_P, mo_hi[:, 0:2].bitcast(F32), ALU.subtract).then_inc(p_ready, 1)
                norm(i)
                low(n0 + SPLIT)
                for u in range(4):
                    scale(n0 + 1 + u, e0 + u, PLE_T[:, 2 * u:2 * u + 2])
                    dve.wait_ge(ple_gate, 4 * at(i, "ple") + u + 1)
                    two = PLE_T[:, 2 * u:2 * u + 2]
                    link(V.tensor_tensor(two, two, ps[:, 4 + u, :].rearrange("p (c t) -> p c t", c=2), ALU.mult))
                    link(V.tensor_tensor(x[:, 2 * u:2 * u + 2], x[:, 2 * u:2 * u + 2], two, ALU.add))
                    if u < 3:
                        low(n0 + 1 + u + SPLIT)
                next_operand(i, 0, KC)
                low(n0 + 4 + SPLIT)

            def tail(i, m, unit, e, gate, value):
                for u in range(4):
                    g, v, o = gate[:, 2 * u:2 * u + 2], value[:, 2 * u:2 * u + 2], OUT[:, 2 * u:2 * u + 2]
                    scale(unit + u, e + u, g)
                    dve.wait_ge(m["gate"], u + 1)
                    V.tensor_tensor(o, v, g, ALU.mult).then_inc(m["prod"], 1)
                    low(unit + u + SPLIT)
                    dve.wait_ge(mo_high, 4 * rcols(i) + u + 1)
                    V.tensor_tensor(mo_lo[:, 2 * u:2 * u + 2], o, mo_hi[:, 2 * u:2 * u + 2].bitcast(F32),
                                    ALU.subtract).then_inc(mo_ready, 1)
                residual(i, unit + 4, e + 4)

            def residual(i, unit, e):
                for u in range(4):
                    dve.wait_ge(weights_used, unit + u + 1)
                    two = x[:, 2 * u:2 * u + 2]
                    V.tensor_tensor(two, two, pair(e + u), ALU.add).then_inc(bank_read, 1)
                    dve.wait_ge(bank_read, e + u + 5)
                    next_operand(i, 2 * u, 2)
                    low(unit + u + SPLIT)

            def lower_bounds(i, layer):
                m = own[i]
                if layer == 0:
                    V.memset(tiny[:, 0:8], 1.0)
                    link(V.memset(tiny[:, 8:16], 0.0))
                    return
                lb = smalls[:, S_LB:S_LB + DEPTH * KC]
                e = tiny[:, 16:48]
                by_depth = "p (l c) -> p c l"
                link(V.tensor_reduce(tiny[:, 48:56], lb.rearrange(by_depth, c=KC), AX_X, ALU.max))
                V.tensor_tensor(e.rearrange("p (l c) -> p l c", c=KC), lb.rearrange("p (l c) -> p l c", c=KC),
                                tiny[:, 48:56].unsqueeze(1).broadcast_to([P, DEPTH, KC]),
                                ALU.subtract).then_inc(m["lbdiff"], 1)
                dve.wait_ge(m["lbexp"], 1)
                V.tensor_reduce(tiny[:, 56:64], e.rearrange(by_depth, c=KC), AX_X, ALU.add)
                part = e[:, KC:KC * (layer + 1)]
                V.tensor_reduce(tiny[:, 64:72], part.rearrange(by_depth, c=KC), AX_X, ALU.add)
                if layer + 1 < DEPTH:
                    rest = e[:, KC * (layer + 1):]
                    link(V.tensor_reduce(tiny[:, 72:80], rest.rearrange(by_depth, c=KC), AX_X, ALU.add))
                    link(V.tensor_tensor(tiny[:, 72:80], tiny[:, 72:80], e[:, 0:KC], ALU.add))
                else:
                    link(V.tensor_copy(tiny[:, 72:80], e[:, 0:KC]))
                link(V.reciprocal(tiny[:, 48:56], tiny[:, 56:64]))
                V.tensor_tensor(tiny[:, 0:8], tiny[:, 72:80], tiny[:, 48:56], ALU.mult)
                link(V.tensor_tensor(tiny[:, 8:16], tiny[:, 64:72], tiny[:, 48:56], ALU.mult))

            def hg(i):
                m = own[i]
                n0, e0 = at(i, "units"), at(i, "banks")
                lower_bounds(i, phases[i][1])
                norm(i)
                for u in range(4):
                    if u == 1:
                        columns(i, e0 + 3)
                    two = slice(2 * u, 2 * u + 2)
                    scale(n0 + u, e0 + u, HG_K[:, two])
                    dve.wait_ge(m["sig"], u + 1)
                    V.tensor_scalar(HG_B[:, two], HG_B[:, two], 2.0 ** -60, None, ALU.max).then_inc(m["clamp"], 1)
                    for c in (2 * u, 2 * u + 1):
                        ins = V.tensor_scalar(HG_K[:, c], HG_K[:, c], tiny[:, c:c + 1], None, ALU.mult)
                    if u == 3:
                        ins.then_inc(m["qk"], 1)
                    low(n0 + u + SPLIT)
                for u in range(4, 8):
                    scale(n0 + u, e0 + u, HG_Q[:, 2 * (u - 4):2 * (u - 4) + 2])
                    low(n0 + u + SPLIT)
                    for g in range(4 * (u - 4), 4 * (u - 3)):
                        h, b = g // 2, slice((g % 2) * P, (g % 2 + 1) * P)
                        dve.wait_ge(m["logf"], h + 1)
                        V.tensor_tensor_scan(HG_B[:, h, b], ones, HG_B[:, h, b], 0.0, ALU.mult,
                                             ALU.add).then_inc(m["scan"], 1)
                for u in range(8, 12):
                    scale_tokens(n0 + u, e0 + u, HG_V[:, :, 256 * (u - 8):256 * (u - 7)], 0)
                    low(n0 + u + SPLIT)
                dve.wait_ge(m["scan"], 16)
                flat = "p c (n a w) -> p (c n) a w"
                L = len(LEVELS)

                def diffs(l):
                    if l >= 2:
                        dve.wait_ge(m["level"], l)
                    if l == L:
                        D = HG_D[l % 2].rearrange("p (h a w) -> p h a w", a=2, w=P)
                        V.tensor_tensor(D[:, :, 0, :], HG_B[:, :, P - 1:P].broadcast_to([P, HG_HEADS, P]),
                                        HG_B[:, :, 0:P], ALU.subtract).then_inc(m["diff"], 1)
                        return
                    w = LEVELS[l]
                    D = HG_D[l % 2].rearrange("p (n a w) -> p n a w", a=2, w=w)
                    B = HG_FLAT_B.rearrange("p (n a w) -> p n a w", a=2, w=w)
                    mid = B[:, :, 0, w - 1:w].broadcast_to([P, UNIT // (2 * w), w])
                    V.tensor_tensor(D[:, :, 1, :], B[:, :, 1, :], mid, ALU.subtract).then_inc(m["diff"], 1)
                    V.tensor_tensor(D[:, :, 0, :], mid, B[:, :, 0, :], ALU.subtract).then_inc(m["diff"], 1)

                def decayed(l):
                    w = LEVELS[l] if l < L else P
                    v = "p (n a w) -> p n a w"
                    D, Q, K = (t.rearrange(v, a=2, w=w) for t in (HG_D[l % 2], HG_FLAT_Q, HG_FLAT_K))
                    dve.wait_ge(m["exp"], 2 * l + 1)
                    V.tensor_tensor(D[:, :, 1, :], D[:, :, 1, :], Q[:, :, 1, :], ALU.mult)
                    dve.wait_ge(m["exp"], 2 * l + 2)
                    V.tensor_tensor(D[:, :, 0, :], D[:, :, 0, :], K[:, :, 0, :], ALU.mult).then_inc(m["qk"], 1)

                def take(s):
                    dve.wait_ge(m["level"], s + 1)
                    A = ps[:, 4 * (s % 2):4 * (s % 2) + 4, :].rearrange("p b (g t) -> p (b g) t", t=P)
                    if s == 0:
                        V.tensor_tensor(HG_AT, A, ident.unsqueeze(1).broadcast_to([P, 16, P]),
                                        ALU.mult).then_inc(m["taken"], 1)
                    else:
                        dve.wait_ge(m["taken"], s)
                        mask = levels[:, (s - 1) * P:s * P].unsqueeze(1).broadcast_to([P, 16, P])
                        V.copy_predicated(HG_AT, mask, A).then_inc(m["taken"], 1)

                diffs(0)
                for l in range(L + 1):
                    decayed(l)
                    if l < L:
                        diffs(l + 1)
                    take(l)
                for p in range(4):
                    dve.wait_ge(m["rs"], p + 1)
                    for c in (2 * p, 2 * p + 1):
                        ins = V.scalar_tensor_tensor(HG_B[:, c], ps[:, c // 2, (c % 2) * T:(c % 2 + 1) * T],
                                                     smalls[:, S_HGN + phases[i][1] // 3:S_HGN + phases[i][1] // 3 + 1],
                                                     HG_RS[:, c], ALU.mult, ALU.mult)
                    ins.then_inc(m["done"], 1)
                dve.wait_ge(m["done"], 4)
                tail(i, m, n0 + 12, e0 + 12, HG_K, HG_B)

            def ml(i):
                m = own[i]
                n0, e0 = at(i, "units"), at(i, "banks")
                g = next_gain(i)
                V.tensor_tensor(tiny[:, 0:64].rearrange("p (k g) -> p k g", g=8),
                                smalls[:, S_WIF:S_WIF + 64].rearrange("p (k g) -> p k g", g=8),
                                smalls[:, g:g + KC].unsqueeze(2).broadcast_to([P, KC, 8]), ALU.mult).then_inc(m["wif"], 1)
                norm(i)
                R = [ML_ROWS[0:4, j] for j in range(8)]
                one_row = ones[0:4, 0:1].broadcast_to([4, T])
                for u in range(8):
                    if u == 1:
                        columns(i, e0 + 3)
                    if u < 4:
                        dst = ML_Q if u < 2 else ML_K
                        scale(n0 + u, e0 + u, dst[:, 2 * (u % 2):2 * (u % 2) + 2])
                    else:
                        scale_tokens(n0 + u, e0 + u, ML_V[:, :, 256 * (u - 4):256 * (u - 3)], 0)
                    low(n0 + u + SPLIT)
                    if u == 3:
                        dve.wait_ge(m["gates"], 1)
                        for j in range(2):
                            link(V.tensor_tensor(R[j], ps[0:4, 4, j * T:(j + 1) * T], rstd[0:4, :], ALU.mult))
                            ins = V.tensor_scalar(R[j], R[j], smalls[0:4, S_BIF + j:S_BIF + j + 1], None, ALU.add)
                        ins.then_inc(m["lin"], 1)
                    if u == 5:
                        dve.wait_ge(m["soft"], 1)
                        link(V.tensor_tensor_scan(R[3], one_row, R[2], 0.0, ALU.mult, ALU.subtract))
                        link(V.scalar_tensor_tensor(R[4], R[0], GATE_CAP, R[3], ALU.mult, ALU.subtract))
                        link(V.tensor_tensor_scan(R[5], one_row, R[4], 0.0, ALU.mult, ALU.max))
                        V.tensor_scalar(R[6], R[5], -1.0, None, ALU.mult)
                        V.scalar_tensor_tensor(R[7], R[3], -1.0, R[5], ALU.mult, ALU.subtract).then_inc(m["row"], 1)
                dve.wait_ge(m["cols"], 1)
                V.tensor_copy(tiny[:, 64:72], ps[:, 4, 0:8]).then_inc(m["ucol"], 1)
                dve.wait_ge(m["ucol"], 1)
                dve.wait_ge(m["bcast"], 1)
                for h in range(ML_HEADS):
                    neg_m = ps[:, 6 + h // 2, (h % 2) * T:(h % 2 + 1) * T]
                    V.tensor_scalar(ML_W[:, h, 0:T], neg_m, tiny[:, 64 + h:65 + h], 0.0, ALU.add, ALU.min)
                    V.tensor_scalar(ML_W[:, h, T:T + P], neg_m[:, P:T], tiny[:, 68 + h:69 + h], 0.0, ALU.add,
                                    ALU.min).then_inc(m["arg"], 1)
                for h in range(ML_HEADS):
                    dve.wait_ge(m["exp"], h + 1)
                    V.tensor_tensor(ML_W[:, h, 0:P], ML_W[:, h, 0:P], causal, ALU.mult)
                    link(V.tensor_tensor(ML_W[:, h, T:T + P], ML_W[:, h, T:T + P], causal, ALU.mult))
                    dve.wait_ge(m["scores"], h + 1)
                    V.scalar_tensor_tensor(ML_W[:, h], ps[:, h, 0:384], ML_DQK ** -0.5, ML_W[:, h], ALU.mult,
                                           ALU.mult).then_inc(m["w"], 1)
                dve.wait_ge(m["gexp"], 2)
                den = ML_DEN.rearrange("p c t -> p (c t)")
                link(V.tensor_tensor(den, den, ML_GUARD.rearrange("p c t -> p (c t)"), ALU.max))
                V.reciprocal(den, den).then_inc(m["nrm"], 1)
                dve.wait_ge(m["nrm"], 1)
                for h in range(ML_HEADS):
                    dve.wait_ge(m["num"], h + 1)
                    V.tensor_tensor(ML_H[:, 2 * h:2 * h + 2], pair(h, True), row(ML_DEN[:, h], 2),
                                    ALU.mult).then_inc(m["h"], 1)
                for c in range(KC):
                    dve.wait_ge(m["rs"], c // 4 + 1)
                    if c == 0:
                        dve.wait_ge(m["h"], ML_HEADS)
                    ins = V.scalar_tensor_tensor(ML_H[:, c], ML_H[:, c], gain(S_MLN, c), ML_GUARD[:, c // 2], ALU.mult,
                                                 ALU.mult)
                link(ins)
                tail(i, m, n0 + 8, e0 + 8, ML_T, ML_H)

            def attention(g0, groups, out, bias=None, sinks=False):
                def logits(g):
                    if g == len(groups):
                        return
                    G = groups[g]
                    t = tiny[:, 32 * (g % 2):32 * (g % 2) + 32]
                    n, w, k0 = G["slots"], G["width"], G["k0"]
                    dve.wait_ge(att["scores"], g0 + g + 1)
                    if g >= 2:
                        dve.wait_ge(att["turned"], g0 + g - 1)
                    src = ps[:, 2 * (g % 2):2 * (g % 2) + 2, :].rearrange("p b t -> p (b t)")[:, 0:n * w]
                    src = src.rearrange("p (s k) -> p s k", k=w)[:, :, k0:]
                    if bias is not None:
                        dst = ATT_P[g % 2][:, 0:n * w].rearrange("p (s k) -> p s k", k=w)[:, :, k0:]
                        link(bias(G, dst, src))
                        src = dst
                    link(V.tensor_reduce(t[:, 0:n], src, AX_X, ALU.max))
                    if sinks:
                        sink = smalls[:, S_SINK + 4 * G["kv"]:S_SINK + 4 * G["kv"] + 4].rearrange("p (a b) -> p b a", b=2)
                        mx, sx = (t[:, c:c + 4].rearrange("p (b a) -> p b a", b=2) for c in (0, 12))
                        link(V.scalar_tensor_tensor(mx, sink, 1.0 / G["scale"], mx, ALU.mult, ALU.max))
                        V.scalar_tensor_tensor(sx, sink, 1.0 / G["scale"], mx, ALU.mult, ALU.subtract)
                    V.tensor_scalar(t[:, 4:4 + n], t[:, 0:n], -G["scale"], None, ALU.mult).then_inc(att["bias"], 1)

                def probs(g):
                    G = groups[g]
                    t = tiny[:, 32 * (g % 2):32 * (g % 2) + 32]
                    n, w, k0 = G["slots"], G["width"], G["k0"]
                    dve.wait_ge(att["exp"], g0 + g + 1)
                    if sinks:
                        link(V.tensor_tensor(t[:, 8:8 + n], t[:, 8:8 + n], t[:, 12:12 + n], ALU.add))
                    link(V.reciprocal(t[:, 16:16 + n], t[:, 8:8 + n]))
                    for s in range(n):
                        p = ATT_P[g % 2][:, s * w + k0:(s + 1) * w]
                        ins = V.tensor_scalar(p, p, t[:, 16 + s:17 + s], None, ALU.mult)
                    ins.then_inc(att["probs"], 1)

                def take(g):
                    dve.wait_ge(att["out"], g0 + g + 1)
                    dst, r, n = out(groups[g])
                    V.tensor_copy(dst, ps[r, 6 + g % 2, 0:n * P].rearrange("p (c t) -> p c t", t=P)).then_inc(att["taken"], 1)

                logits(0)
                for g in range(len(groups)):
                    probs(g)
                    logits(g + 1)
                    if g:
                        take(g - 1)
                take(len(groups) - 1)

            def normalise(dst, g, roots, count):
                for c in range(2):
                    ins = V.scalar_tensor_tensor(dst[:, c], dst[:, c], g, roots[:, c], ALU.mult, ALU.mult)
                ins.then_inc(count, 1)

            def sw(i):
                m = own[i]
                n0, e0 = at(i, "units"), at(i, "banks")
                norm(i)
                for u in range(4):
                    if u == 1:
                        columns(i, e0 + 3)
                    scale(n0 + u, e0 + u, SW_QK[:, 2 * u:2 * u + 2])
                    low(n0 + u + SPLIT)

                def roots(p):
                    dve.wait_ge(m["rs"], p + 1)
                    normalise(SW_QK[:, 2 * p:2 * p + 2], gain(S_SWN, p // 4), SW_SQ[:, 2 * (p % 4):2 * (p % 4) + 2],
                              m["qk"])
                for p in range(4):
                    roots(p)
                for u in range(4, 6):
                    scale(n0 + u, e0 + u, SW_QK[:, 2 * u:2 * u + 2])
                    low(n0 + u + SPLIT)
                scale_tokens(n0 + 6, e0 + 6, SW_V, 0)
                low(n0 + 6 + SPLIT)
                roots(4)
                roots(5)
                dve.wait_ge(phase_consts, 16)

                def alibi(G, dst, src):
                    for s in range(4):
                        h = 4 * G["kv"] + (s % 2) * 2 + s // 2
                        slope = 2.0 ** (-8.0 * (h + 1) / SW_HEADS) / G["scale"]
                        ins = V.scalar_tensor_tensor(dst[:, s], SW_BIAS[:, G["k0"]:], slope, src[:, s], ALU.mult, ALU.add)
                    return ins
                attention(att_before(i), quad_groups(SW_QK, SW_QK[:, 8:12], SW_V, SW_KV, True),
                          lambda G: (SW_O[:, 2 * G["kv"]:2 * G["kv"] + 2, G["n"] * P:(G["n"] + 1) * P], slice(0, P), 2),
                          bias=alibi, sinks=True)
                for u in range(4):
                    dve.wait_ge(mo_high, 4 * rcols(i) + u + 1)
                    V.tensor_tensor(mo_lo[:, 2 * u:2 * u + 2], SW_O[:, 2 * u:2 * u + 2],
                                    mo_hi[:, 2 * u:2 * u + 2].bitcast(F32), ALU.subtract).then_inc(mo_ready, 1)
                residual(i, n0 + 7, e0 + 7)

            def second(i):
                m = own[i]
                n0, e0 = at(i, "units"), at(i, "banks")
                dve.wait_ge(p_loaded, 16 * (at(i, "ple") + 1))
                for c in range(KC):
                    V.tensor_scalar(mo_hi[:, c], SE_MEM[:, c], gain(S_GMEM, c), None, ALU.mult).then_inc(m["memhi"], 1)
                for c in range(KC):
                    dve.wait_ge(m["memhi"], c + 1)
                    V.scalar_tensor_tensor(mo_lo[:, c], SE_MEM[:, c], gain(S_GMEM, c), mo_hi[:, c].bitcast(F32),
                                           ALU.mult, ALU.subtract).then_inc(m["memready"], 1)
                norm(i)
                dve.wait_ge(m["memsq"], 1)
                V.tensor_reduce(SE_MSUM, SE_MSQ.rearrange("p c t -> p t c"), AX_X, ALU.add).then_inc(m["memsum"], 1)
                dve.wait_ge(m["memrs"], 1)
                for u in range(2):
                    dve.wait_ge(weights_used, n0 + u + 1)
                    V.tensor_tensor(SE_KM[:, 2 * u:2 * u + 2], pair(e0 + u), row(SE_RMEM, 2), ALU.mult).then_inc(bank_read, 1)
                    low(n0 + u + SPLIT)
                columns(i, e0 + 3)
                dve.wait_ge(m["memcols"], 1)
                link(V.tensor_copy(rcol[:, 2:4], ps[:, 4, T:T + 2]))
                for u in range(2, 4):
                    scale_tokens(n0 + u, e0 + u, SE_VM[:, :, 256 * (u - 2):256 * (u - 1)], 2)
                    low(n0 + u + SPLIT)
                for u in range(4, 6):
                    scale(n0 + u, e0 + u, SE_QM[:, 2 * (u - 4):2 * (u - 4) + 2])
                    low(n0 + u + SPLIT)
                B = [SE_QB[:, 0:2], SE_QB[:, 2:4], SE_KB]
                for p in range(3):
                    scale(n0 + 6 + p, e0 + 6 + p, B[p])
                    low(n0 + 6 + p + SPLIT)
                dve.wait_ge(weights_used, n0 + 10)
                for b in range(TB):
                    ins = V.tensor_scalar(SE_VB[:, b], pair(e0 + 9)[:, b, 0:P], rcol[:, b:b + 1], None, ALU.mult)
                ins.then_inc(bank_read, 1)
                low(n0 + 9 + SPLIT)
                dve.wait_ge(phase_consts, PC)

                def rope(r, src, cos, sin, turned, dst):
                    y, z = SE_COS[r % 2], SE_SIN[r % 2]
                    V.tensor_tensor(y, src, row(cos, 2), ALU.mult)
                    dve.wait_ge(m["rot"], r + 1)
                    link(V.tensor_tensor(z, turned, row(sin, 2), ALU.mult))
                    V.tensor_tensor(dst, y, z, ALU.add).then_inc(m["roped"], 1)
                for p in range(3):
                    dve.wait_ge(m["rs"], p + 1)
                    normalise(B[p], gain(S_BN, p // 2), SE_SQ[:, 2 * p:2 * p + 2], m["x"])
                dve.wait_ge(m["x"], 3)
                for p in range(3):
                    rope(p, B[p], COS2, SIN2, pair(5 + p, True), B[p])
                attention(att_before(i, 0), memory_groups(),
                          lambda G: (SE_O[:, 8:12, G["n"] * P:(G["n"] + 1) * P], slice(0, P), 4))
                attention(att_before(i, 1), quad_groups(SE_QB, SE_KB, SE_VB, 2, False),
                          lambda G: (SE_O[:, 4 + 2 * G["kv"]:6 + 2 * G["kv"], G["n"] * P:(G["n"] + 1) * P],
                                     slice(0, P), 2))
                for half in range(2):
                    u0 = 10 + 9 * half
                    for u in range(6):
                        scale(n0 + u0 + u, e0 + u0 + u, SE_X[u % 2])
                        dve.wait_ge(bank_read, e0 + u0 + u + 5)
                        low(n0 + u0 + u + SPLIT)
                        dst = (SE_QA if u < 3 else SE_KA)[:, 2 * (u % 3):2 * (u % 3) + 2]
                        rope(3 + 6 * half + u, SE_X[u % 2], COS, SIN, pair(4 + u % 2, True), dst)
                    for g in range(A_GROUPS):
                        u = u0 + 6 + g
                        scale_tokens(n0 + u, e0 + u, SE_VA[:, :, 256 * g:256 * (g + 1)], 0)
                        low(n0 + u + SPLIT)
                    attention(att_before(i, 2 + half), dilated_groups(),
                              lambda G: (SE_O[head_half(G["h"]), 2 * half + G["h"] // 2:2 * half + G["h"] // 2 + 1,
                                              G["n"] * P:(G["n"] + 1) * P], head_half(G["h"]), 1),
                              bias=lambda G, dst, src: V.tensor_tensor(dst, src, SE_MASK[:, G["n"]:G["n"] + 1, :],
                                                                       ALU.add))
                for u in range(6):
                    t = SE_GATE[u % 2]
                    scale(n0 + 28 + u, e0 + 28 + u, t)
                    dve.wait_ge(m["gate"], u + 1)
                    V.tensor_tensor(SE_O[:, 2 * u:2 * u + 2], SE_O[:, 2 * u:2 * u + 2], t, ALU.mult).then_inc(m["gated"], 1)
                    low(n0 + 28 + u + SPLIT)

                def fill(br):
                    s = 4 * (br % 2)
                    dve.wait_ge(m["mhi"], br + 1)
                    V.tensor_tensor(mo_lo[:, s:s + 4], SE_O[:, 4 * br:4 * br + 4], mo_hi[:, s:s + 4].bitcast(F32),
                                    ALU.subtract).then_inc(m["mlo"], 1)
                fill(0)
                fill(1)
                n, e = n0 + 34, e0 + 34
                for br in range(3):
                    low(n + SPLIT)
                    low(n + 1 + SPLIT)
                    if br == 1:
                        fill(2)
                    for u in range(4):
                        t, two = SE_GATE[u % 2], SE_MERGED[:, 2 * u:2 * u + 2]
                        scale(n + 2 + u, e + u, t)
                        dve.wait_ge(m["merge"], 4 * br + u + 1)
                        if br == 0:
                            V.tensor_tensor(two, t, pair(4 + u, True), ALU.mult).then_inc(m["merged"], 1)
                        else:
                            link(V.tensor_tensor(t, t, pair(4 + u, True), ALU.mult))
                            V.tensor_tensor(two, two, t, ALU.add).then_inc(m["merged"], 1)
                        low(n + 2 + u + SPLIT)
                        if br == 2:
                            dve.wait_ge(m["high"], u + 1)
                            V.tensor_tensor(mo_lo[:, 2 * u:2 * u + 2], two, mo_hi[:, 2 * u:2 * u + 2].bitcast(F32),
                                            ALU.subtract).then_inc(m["low"], 1)
                    n, e = n + 6, e + 4
                for u in range(4):
                    dve.wait_ge(weights_used, n + u + 1)
                    V.tensor_copy(SE_Y[:, 2 * u:2 * u + 2], pair(e + u)).then_inc(bank_read, 1)
                    low(n + u + SPLIT)
                dve.wait_ge(m["fsq"], 4)
                V.tensor_reduce(SE_YSUM, SE_YSQ.rearrange("p c t -> p t c"), AX_X, ALU.add).then_inc(m["fsum"], 1)
                dve.wait_ge(m["frs"], 1)
                for c in range(KC):
                    ins = V.scalar_tensor_tensor(SE_Y[:, c], SE_Y[:, c], gain(S_GPOST, c), SE_YR, ALU.mult, ALU.mult)
                link(ins)
                V.tensor_tensor(x[:], x[:], SE_Y, ALU.add).then_inc(out_ready, 1)

            PC = 16 * sum(k in ("sw", "second") for k, _ in phases)
            V.memset(eps[:], EPS).then_inc(eps_ready, 1)
            V.memset(rcol[:], 0.0).then_inc(bank_read, 4)
            dve.wait_ge(consts_loaded, 32)
            link(V.tensor_copy(levels[:], LEVELS_IN))
            for i in range(SPLIT):
                low(i)
            dve.wait_ge(x_loaded, 32)
            next_operand(-1, 0, KC)
            for i, (kind, _) in enumerate(phases):
                {"ffn": ffn, "ple": ple, "hg": hg, "ml": ml, "sw": sw, "second": second}[kind](i)
            if phases[-1][0] != "second":
                link(V.memset(eps[:], EPS))
                V.memset(eps[:], EPS).then_inc(out_ready, 1)


INS = ["x_t", "p_t", "mem_t", "weights", "smalls", "c_common", "c_levels", "c_swa", "c_second"]


def kernel(**inputs):
    import concourse.bacc as bacc
    from concourse.bass_utils import run_bass_kernel_spmd

    nc = bacc.Bacc("TRN2", target_bir_lowering=False, num_devices=1)
    laid, arrays, args = lay_out(inputs, PHASES), {}, []
    for name in INS:
        a = laid[name]
        arrays[name + "_dram"] = a
        args.append(nc.dram_tensor(name + "_dram", a.shape, mybir.dt.from_np(a.dtype), kind="ExternalInput").ap())
    args.append(nc.dram_tensor("out_dram", (P, KC, T), F32, kind="ExternalOutput").ap())
    build(nc, PHASES, *args)
    r = run_bass_kernel_spmd(nc, [arrays], core_ids=[0])
    got = r.results[0]["out_dram"]
    return np.ascontiguousarray(got.transpose(2, 1, 0)).reshape(1, T, D_MODEL)
```

```python
from contextlib import ExitStack

import numpy as np

import concourse.bass as bass
from concourse import mybir

F32 = mybir.dt.float32
F32R = mybir.dt.float32r
U8 = mybir.dt.uint8
ALU = mybir.AluOpType
ACT = mybir.ActivationFunctionType
AX_X = mybir.AxisListType.X

P = 128
T = 256
TB = T // P
D_MODEL = 1024
KC = D_MODEL // P
D_FF = 2816
HCH = D_FF // P
STEPS = HCH // 2
DEPTH = 4
EPS = 1e-6
PLE_DIM = 256
HG_HEADS = 8
ML_HEADS = 4
ML_DQK = 128
ML_DV = 256
GATE_CAP = 15.0
SW_HEADS = 16
SW_KV = 4
HD = 64
A_HEADS = 8
A_GROUPS = 3
B_HEADS = 8
M_HEADS = 4

UNIT = 2048
RAW = 6
SPLIT = 3
BANKS = 4

KINDS = {
    "ffn": dict(units=HCH + STEPS, banks=HCH, norms=1, resid=KC, hidden=HCH, acc=3),
    "ple": dict(units=5, banks=4, norms=1, resid=KC, ple=1),
    "hg": dict(units=20, banks=20, norms=1, resid=KC, hg=1),
    "ml": dict(units=16, banks=16, norms=1, resid=KC, ml=1),
    "sw": dict(units=11, banks=11, norms=1, resid=KC, sw=1),
    "second": dict(units=56, banks=50, norms=1, resid=KC, second=1),
}
PHASES = [(k, l) for l in range(DEPTH) for k in ("ffn", ("hg", "ml", "sw")[l % 3], "ffn", "ple")]
PHASES.append(("second", 0))


def starts(phases):
    done, out = {}, []
    for kind, _ in phases:
        out.append(dict(done))
        for what, n in KINDS[kind].items():
            done[what] = done.get(what, 0) + n
    out.append(done)
    return out


def columns_unit(w, cols):
    return w[:, cols].reshape(KC, P, 256).transpose(1, 0, 2).reshape(P, UNIT)


def rows_unit(w, r0):
    return w[r0:r0 + 256].reshape(2, P, D_MODEL).transpose(1, 0, 2).reshape(P, UNIT)


def span(a, n=256):
    return np.arange(a, a + n)


def weight_units(inputs, phases):
    a = {k: np.asarray(v) for k, v in inputs.items()}
    ffn = 0
    for kind, layer in phases:
        if kind == "ffn":
            gu, down = a["w_ffn_gu"][layer, ffn % 2], a["w_ffn_down"][layer, ffn % 2]
            ffn += 1

            def up(j):
                return columns_unit(gu, np.concatenate([span(P * j, P), span(D_FF + P * j, P)]))
            yield up(0)
            yield up(1)
            for s in range(1, STEPS):
                yield up(2 * s)
                yield up(2 * s + 1)
                yield rows_unit(down, 256 * (s - 1))
            yield rows_unit(down, 256 * (STEPS - 1))
        elif kind == "ple":
            yield rows_unit(a["w_ple_proj"][layer], 0)
            for u in range(4):
                yield columns_unit(a["w_ple_gate"][layer], span(256 * u))
        elif kind == "hg":
            w = a["hg_w_in"][layer // 3]
            for part in (1, 0, 2, 3):
                for u in range(4):
                    yield columns_unit(w, span(part * D_MODEL + 256 * u))
            for u in range(4):
                yield columns_unit(a["hg_w_out"][layer // 3], span(256 * u))
        elif kind == "ml":
            for u in range(12):
                yield columns_unit(a["ml_w_qkvo"][0], span(256 * u))
            for u in range(4):
                yield columns_unit(a["ml_w_out"][0], span(256 * u))
        elif kind == "sw":
            w = a["sw_w_qkv"][0]
            for u in range(2):
                k0 = SW_HEADS * HD + 2 * u * HD
                yield columns_unit(w, np.concatenate([span(k0, HD), span(k0, HD), span(k0 + HD, HD), span(k0 + HD, HD)]))
            for u in range(4):
                yield columns_unit(w, span(256 * u))
            yield columns_unit(w, span((SW_HEADS + SW_KV) * HD))
            for u in range(4):
                yield columns_unit(a["sw_w_o"][0], span(256 * u))
        else:
            yield from second_units(a)


def second_units(a):
    w = a["w_in_2"][0]
    mkv = a["w_mem_kv_2"][0]
    gh = A_GROUPS * A_HEADS * HD
    b0 = 3 * gh
    bk = b0 + B_HEADS * HD
    bv = bk + 2 * HD
    mq = bv + 2 * HD
    ga = mq + 512
    mg = ga + 3 * 512
    for u in range(4):
        yield columns_unit(mkv, span(256 * u))
    for u in range(2):
        yield columns_unit(w, span(b0 + 256 * u))
    yield columns_unit(w, np.concatenate([span(bk, HD), span(bk, HD), span(bk + HD, HD), span(bk + HD, HD)]))
    for u in range(2):
        yield columns_unit(w, span(mq + 256 * u))
    yield columns_unit(w, np.concatenate([span(bv, P), span(bv, P)]))
    for half in range(2):
        for part in range(3):
            for g in range(A_GROUPS):
                yield columns_unit(w, span(part * gh + g * 512 + 256 * half))
    for u in range(6):
        yield columns_unit(w, span(ga + 256 * u))
    for br, name in enumerate(("w_br_a_2", "w_br_b_2", "w_br_m_2")):
        for u in range(2):
            yield rows_unit(a[name][0], 256 * u)
        for u in range(4):
            yield columns_unit(w, span(mg + br * D_MODEL + 256 * u))
    for u in range(4):
        yield columns_unit(a["w_out_2"][0], span(256 * u))


S_GAIN = 0
S_GPRE = S_GAIN + DEPTH * 4 * KC
S_GMEM = S_GPRE + KC
S_GPOST = S_GMEM + KC
S_LB = S_GPOST + KC
S_HGN = S_LB + DEPTH * KC
S_MLN = S_HGN + 2
S_BIF = S_MLN + KC
S_WIF = S_BIF + 2
S_SWN = S_WIF + KC * 8
S_SINK = S_SWN + 2
S_BN = S_SINK + SW_HEADS
S_BM = S_BN + 2
SMALLS = S_BM + 3 * KC


def small_parameters(inputs):
    a = {k: np.asarray(v) for k, v in inputs.items()}
    s = np.zeros((P, SMALLS), np.float32)

    def put(at, v):
        v = np.asarray(v).reshape(-1, P)
        s[:, at:at + v.shape[0]] = v.T
    put(S_GAIN, a["norm_gains"])
    put(S_GPRE, a["g_pre_2"])
    put(S_GMEM, a["g_mem_2"])
    put(S_GPOST, a["g_post_2"])
    put(S_LB, a["hg_lower_bounds"])
    put(S_HGN, a["hg_g_norm"])
    put(S_MLN, a["ml_norm"])
    s[0:4, S_BIF] = a["ml_b_if"][0, 0:4]
    s[0:4, S_BIF + 1] = a["ml_b_if"][0, 4:8]
    s[:, S_WIF:S_WIF + KC * 8] = a["ml_w_if"][0].reshape(KC, P, 8).transpose(1, 0, 2).reshape(P, KC * 8)
    for i, name in enumerate(("sw_q_norm", "sw_k_norm")):
        s[:, S_SWN + i] = np.tile(a[name][0], 2)
    s[:, S_SINK:S_SINK + SW_HEADS] = a["sw_sinks"][0][None, :]
    for i, name in enumerate(("q_norm_2", "k_norm_2")):
        s[:, S_BN + i] = np.tile(a[name][0], 2)
    put(S_BM, a["b_merge_2"])
    return s


LEVELS = (64, 32, 16, 8, 4, 2, 1)
RECT_LEVELS = 3
NEG = -1e30


def constants():
    p = np.arange(P)
    ident = np.eye(P, dtype=np.float32)
    ones = np.ones((P, P), np.float32)
    halves = (p[:, None] // HD == p[None, :] // HD).astype(np.float32)
    causal = (p[:, None] <= p[None, :]).astype(np.float32)
    rot = np.zeros((P, P), np.float32)
    rot32 = np.zeros((P, P), np.float32)
    for m in range(P):
        for r, w in ((rot, HD), (rot32, HD // 2)):
            lo = m % w < w // 2
            r[m + w // 2 if lo else m - w // 2, m] = -1.0 if lo else 1.0
    selector = np.zeros((P, ML_HEADS, P), np.float32)
    for h in range(ML_HEADS):
        selector[h, h] = 1.0
    common = np.concatenate([ident, ones, halves, causal, rot, rot32, selector.reshape(P, -1)], axis=1)

    level = np.zeros((P, len(LEVELS), P), np.float32)
    for i, m in enumerate(LEVELS):
        s, t = p[:, None], p[None, :]
        level[:, i] = (s // (2 * m) == t // (2 * m)) & (s % (2 * m) < m) & (t % (2 * m) >= m)

    q, k = p[:, None], np.arange(2 * P)[None, :]
    dist = (q + P - k).astype(np.float32)
    window = np.where((dist >= 0) & (dist < 128), 0.0, NEG).astype(np.float32)
    swa = np.where(window < 0, NEG, -dist).astype(np.float32)

    pos = np.arange(T)
    d = p % HD
    inv = np.power(10000.0, -np.arange(HD // 2) * 2.0 / HD)
    ang = (pos[None, :] * inv[d % (HD // 2)][:, None])
    inv2 = np.power(10000.0, -np.arange(HD // 4) * 2.0 / (HD // 2))
    place = np.where((d < HD // 2)[:, None], (pos // 64)[None, :], (pos % 64)[None, :])
    ang2 = place * inv2[d % (HD // 4)][:, None]
    ropes = np.concatenate([np.cos(ang), np.sin(ang), np.cos(ang2), np.sin(ang2)], axis=1).astype(np.float32)
    tq = (np.arange(TB)[:, None, None, None] * P + p[None, :, None, None])
    tk = np.arange(T)[None, None, None, :]
    diff = np.abs(tq - tk)[:, :, 0, :]
    groups = np.stack([diff <= 64, diff % 4 == 0, diff % 16 == 0], axis=2)
    groups = np.where(groups, 0.0, NEG).astype(np.float32).transpose(1, 0, 2, 3).reshape(P, -1)
    return {
        "c_common": common,
        "c_levels": level.reshape(P, -1),
        "c_swa": swa,
        "c_second": np.concatenate([ropes, groups], axis=1),
    }


def lay_out(inputs, phases):
    x, p, mem = (np.asarray(inputs[n]) for n in ("x", "p", "mem_2"))

    def feature_major(a):
        return np.ascontiguousarray(a.T.reshape(-1, P, T).transpose(1, 0, 2))
    n = sum(KINDS[k]["units"] for k, _ in phases)
    weights = np.empty((n, P, UNIT), np.float32)
    for i, u in enumerate(weight_units(inputs, phases)):
        weights[i] = u
    assert i == n - 1
    out = {
        "x_t": feature_major(x[0]),
        "p_t": np.stack([feature_major(p[l, 0]) for l in range(DEPTH)]),
        "mem_t": feature_major(mem[0]),
        "weights": weights,
        "smalls": small_parameters(inputs),
    }
    out.update(constants())
    return out


def build(nc, phases, x_t, p_t, mem_t, weights, smalls_d, c_common, c_levels, c_swa, c_second, out):
    begin = starts(phases)
    NU = begin[-1]["units"]
    with ExitStack() as ctx:
        def sb(name, shape, dt=F32):
            return ctx.enter_context(nc.sbuf_tensor(name, shape, dt))

        def sem(name):
            return ctx.enter_context(nc.semaphore(name))

        raw = sb("raw", [P, RAW, UNIT])
        w_hi = sb("w_hi", [P, SPLIT, UNIT], F32R)
        w_lo = sb("w_lo", [P, SPLIT, UNIT], F32R)
        x = sb("x", [P, KC, T])
        xg_hi = sb("xg_hi", [P, KC, T], F32R)
        xg_lo = sb("xg_lo", [P, KC, T], F32R)
        mo_hi = sb("mo_hi", [P, KC, T], F32R)
        mo_lo = sb("mo_lo", [P, KC, T], F32R)
        common = sb("common", [P, 1280])
        smalls = sb("smalls", [P, SMALLS])
        levels = sb("levels", [P, len(LEVELS) * P], U8)
        rstd = sb("rstd", [P, T])
        rcol = sb("rcol", [P, 4])
        tiny = sb("tiny", [P, 96])
        S = sb("scratch", [P, 7 * UNIT + UNIT // 2])
        ps = ctx.enter_context(nc.psum_tensor("ps", [P, 8, 512], F32))

        eps = sb("eps", [P, 1])
        EPSB = eps[:, 0:1]

        ident, ones, halves, causal, rot, rot32 = (common[:, i * P:(i + 1) * P] for i in range(6))

        def selector(h):
            return common[0:ML_HEADS, (6 + h) * P:(7 + h) * P]

        def gain(at, c):
            return smalls[:, at + c:at + c + 1]

        def chunks(at, n, t=T):
            return S[:, at:at + n * t].rearrange("p (c t) -> p c t", t=t)

        raw_full = [sem(f"raw_full{i}") for i in range(RAW)]
        weights_hi = sem("weights_hi")
        weights_split = sem("weights_split")
        weights_used = sem("weights_used")
        bank_read = sem("bank_read")
        acc_ready = sem("acc_ready")
        consts_loaded = sem("consts_loaded")
        x_loaded = sem("x_loaded")
        x_updated = sem("x_updated")
        xg_ready = sem("xg_ready")
        squares_ready = sem("squares_ready")
        square_sum = sem("square_sum")
        sums_ready = sem("sums_ready")
        rstd_ready = sem("rstd_ready")
        up_scaled = sem("up_scaled")
        silu_ready = sem("silu_ready")
        mo_high = sem("mo_high")
        hidden_value = sem("hidden_value")
        hidden_hi = sem("hidden_hi")
        hidden_ready = sem("hidden_ready")
        p_loaded = sem("p_loaded")
        p_hi_ready = sem("p_hi_ready")
        p_ready = sem("p_ready")
        ple_gate = sem("ple_gate")
        eps_ready = sem("eps_ready")
        rcol_sums = sem("rcol_sums")
        mo_ready = sem("mo_ready")
        dve_chain = sem("dve_chain")
        act_chain = sem("act_chain")
        phase_consts = sem("phase_consts")
        out_ready = sem("out_ready")
        out_stored = sem("out_stored")

        nphase = len(phases)

        def at(i, what):
            return begin[i].get(what, 0)

        def rcols(i):
            return sum(k not in ("ffn", "ple") for k, _ in phases[:i])

        def bank(e):
            return ps[:, e % BANKS, :]

        def norm_bank(i):
            return bank(at(i, "banks") + 3) if phases[i][0] == "ple" else ps[:, 7, :]

        def next_gain(i):
            kind, layer = phases[i]
            if kind == "second":
                return S_GPRE
            place = {"hg": 1, "ml": 1, "sw": 1, "ple": 3}.get(kind)
            if place is None:
                place = 2 if i > 0 and phases[i - 1][0] in ("hg", "ml", "sw") else 0
            return S_GAIN + (4 * layer + place) * KC

        SQ = chunks(0, KC)
        SQ_SUM = S[:, UNIT:UNIT + T]
        FFN_T = chunks(UNIT + T, 6)
        FFN_H = chunks(UNIT + 7 * T, 2)
        PLE_P = chunks(6 * UNIT, 2)
        PLE_T = chunks(2 * UNIT, KC)
        HG_B, HG_Q, HG_K = (chunks(i * UNIT, KC) for i in range(3))
        HG_V = S[:, 3 * UNIT:4 * UNIT].rearrange("p (b f) -> p b f", b=TB)
        HG_D = [S[:, (4 + i) * UNIT:(5 + i) * UNIT] for i in range(2)]
        HG_AT = S[:, 6 * UNIT:7 * UNIT].rearrange("p (g t) -> p g t", t=P)
        HG_OFF = S[:, 7 * UNIT:7 * UNIT + 1024].rearrange("p (h t) -> p h t", t=P)
        HG_SQ = HG_D[0].rearrange("p (c t) -> p c t", t=T)
        HG_RS = HG_D[1].rearrange("p (c t) -> p c t", t=T)
        LEVELS_IN = S[:, 6 * UNIT:6 * UNIT + len(LEVELS) * P]
        HG_FLAT_B, HG_FLAT_Q, HG_FLAT_K = (S[:, i * UNIT:(i + 1) * UNIT] for i in range(3))
        OUT = chunks(UNIT, KC)
        ML_Q = chunks(UNIT, 4)
        ML_K = chunks(UNIT + 1024, 4)
        ML_V = S[:, 2 * UNIT:3 * UNIT].rearrange("p (b f) -> p b f", b=TB)
        ML_H = chunks(3 * UNIT, KC)
        ML_W = S[:, 4 * UNIT:4 * UNIT + ML_HEADS * 384].rearrange("p (h t) -> p h t", t=384)
        ML_GUARD = chunks(5 * UNIT, 4)
        ML_DEN = chunks(5 * UNIT + 1024, 4)
        ML_ROWS = chunks(6 * UNIT, 8)
        ML_T = chunks(0, KC)
        ATT_2 = ([S[:, 4 * UNIT + i * 1024:4 * UNIT + (i + 1) * 1024] for i in range(2)],
                 [S[:, 5 * UNIT + i * 1024:5 * UNIT + (i + 1) * 1024] for i in range(2)])
        ATT_SW = (ATT_2[0] + [S[:, 0:1024]], ATT_2[1])
        ATT_A = ([S[:, 4 * UNIT + i * 768:4 * UNIT + (i + 1) * 768] for i in range(3)],
                 [S[:, 4 * UNIT + i * 768:4 * UNIT + (i + 1) * 768] for i in range(3, 5)])
        SW_QK = chunks(UNIT, 12)
        SW_V = S[:, 5120:5632].rearrange("p (b f) -> p b f", b=TB)
        SW_SQ = chunks(3 * UNIT, 8)
        SW_O = chunks(6 * UNIT, 8)
        SW_BIAS = S[:, 7 * UNIT:7 * UNIT + 256]
        SE_QM, SE_KM = chunks(0, 4), chunks(1024, 4)
        SE_VM = S[:, 2048:3072].rearrange("p (b f) -> p b f", b=TB)
        SE_QB, SE_KB = chunks(3072, 4), chunks(4096, 2)
        SE_VB = S[:, 4608:4864].rearrange("p (b f) -> p b f", b=TB)
        SE_QA, SE_KA = chunks(0, 6), chunks(1536, 6)
        SE_VA = S[:, 3072:4608].rearrange("p (b f) -> p b f", b=TB)
        SE_O = chunks(4864, 12)
        SE_MSUM, SE_RMEM = S[:, 4864:5120], S[:, 5120:5376]
        SE_MEM, SE_MSQ = chunks(4 * UNIT, KC), chunks(5 * UNIT, KC)
        SE_SQ = chunks(4 * UNIT, 6)
        SE_X = [chunks(4 * UNIT + i * 512, 2) for i in range(2)]
        SE_COS = [chunks(5 * UNIT + i * 512, 2) for i in range(2)]
        SE_SIN = [chunks(5 * UNIT + 1024 + i * 512, 2) for i in range(2)]
        SE_GATE = [chunks(4 * UNIT + i * 512, 2) for i in range(2)]
        SE_MERGED, SE_Y, SE_YSQ = chunks(0, KC), chunks(2048, KC), chunks(5 * UNIT, KC)
        SE_YR = S[:, 4 * UNIT:4 * UNIT + T]
        SE_CONST = S[:, 6 * UNIT:6 * UNIT + 2560]
        COS, SIN, COS2, SIN2 = (S[:, 6 * UNIT + i * T:6 * UNIT + (i + 1) * T] for i in range(4))
        SE_MASK = S[:, 6 * UNIT + 1024:6 * UNIT + 2560].rearrange("p (b k) -> p b k", b=TB)

        def sw_pair(u):
            c = 8 + 2 * u if u < 2 else 2 * (u - 2)
            return SW_QK[:, c:c + 2]

        def head_half(h):
            return slice((h % 2) * HD, (h % 2 + 1) * HD)

        def quad_groups(Q, K, V, kvs, window):
            out = []
            for kv in range(kvs):
                for n in range(TB):
                    k0 = P if window and n == 0 else 0
                    g = dict(slots=4, width=256, k0=k0, scale=HD ** -0.5, scores=[], values=[], kv=kv, n=n)
                    for hh in range(4):
                        r, slot = head_half(hh), (hh % 2) * 2 + hh // 2
                        c = 2 * kv + hh // 2
                        keys = slice(0, T - k0)
                        g["scores"].append((slot * 256 + k0, T - k0, Q[r, c, n * P:(n + 1) * P], K[r, kv, keys]))
                        vs = [(V[:, (b * P - k0) // P, kv * HD:(kv + 1) * HD], 2 * slot + b) for b in range(k0 // P, 2)]
                        g["values"].append((r, (hh // 2) * P, vs))
                    out.append(g)
            return out

        def memory_groups():
            out = []
            for n in range(TB):
                g = dict(slots=4, width=256, k0=0, scale=P ** -0.5, scores=[], values=[], n=n)
                for h in range(M_HEADS):
                    g["scores"].append((h * 256, 256, SE_QM[:, h, n * P:(n + 1) * P], SE_KM[:, h, :]))
                    vs = [(SE_VM[:, b, h * P:(h + 1) * P], 2 * h + b) for b in range(2)]
                    g["values"].append((slice(0, P), h * P, vs))
                out.append(g)
            return out

        def dilated_groups():
            out = []
            for h in range(4):
                for n in range(TB):
                    r = head_half(h)
                    g = dict(slots=1, width=768, k0=0, scale=HD ** -0.5, scores=[], values=[], h=h, n=n)
                    for a in range(A_GROUPS):
                        c = 2 * a + h // 2
                        g["scores"].append((a * 256, 256, SE_QA[r, c, n * P:(n + 1) * P], SE_KA[r, c, :]))
                    vs = [(SE_VA[:, b, a * 256 + h * HD:a * 256 + (h + 1) * HD], 2 * a + b)
                          for a in range(A_GROUPS) for b in range(2)]
                    g["values"].append((r, 0, vs))
                    out.append(g)
            return out

        def new_sems(tag, names):
            return {n: sem(f"{tag}_{n}") for n in names.split()}

        ATT = "scores bias exp probs turned pt out taken"
        own = []
        for i, (kind, _) in enumerate(phases):
            names = {"hg": "lbdiff lbexp sig clamp qsilu logf scan diff exp qk level taken off o sq sums rs done gate prod",
                     "ml": "wif gates lin soft row cols ucol bcast arg exp scores w num den guard gexp nrm h sq sums rs done gate prod",
                     "sw": "sq sums rs qk",
                     "second": "memhi memready memsq memsum memsums memrs memcols sq sums rs x rot roped gate gated mhi mlo merge merged high low fsq fin frs"
                     }.get(kind, "")
            own.append(new_sems(f"{kind}{i}", names) if names else {})
        att = new_sems("att", ATT)

        def att_before(i, stage=0):
            g = 2 * SW_KV * sum(k == "sw" for k, _ in phases[:i])
            return g + sum((2, 4, 8, 8)[:stage])


        block = ctx.enter_context(nc.Block())

        @block.sync
        def _(sp):
            sp.dma_start(raw[:, 0, :], weights[0]).then_inc(raw_full[0], 16)
            sp.dma_start(smalls[:], smalls_d).then_inc(x_loaded, 16)
            sp.dma_start(x[:], x_t).then_inc(x_loaded, 16)
            for i in range(1, RAW):
                sp.dma_start(raw[:, i, :], weights[i]).then_inc(raw_full[i], 16)
            rounds = NU // RAW
            with sp.Fori(1, rounds) as it:
                for i in range(RAW):
                    sp.wait_ge(weights_split, RAW * it + (i + 1 - RAW))
                    sp.dma_start(raw[:, i, :], weights[RAW * it + i]).then_inc(raw_full[i], 16)
            for n in range(rounds * RAW, NU):
                sp.wait_ge(weights_split, n + 1 - RAW)
                sp.dma_start(raw[:, n % RAW, :], weights[n]).then_inc(raw_full[n % RAW], 16)
            for half in range(2):
                sp.wait_ge(out_ready, half + 1)
                sp.dma_start(out[:, 4 * half:4 * half + 4], x[:, 4 * half:4 * half + 4]).then_inc(out_stored, 16)
            sp.wait_ge(out_stored, 32)

        @block.gpsimd
        def _(pool):
            pool.wait_ge(x_loaded, 32)
            pool.dma_start(common[:], c_common).then_inc(consts_loaded, 16)
            pool.wait_ge(consts_loaded, 16)
            pool.wait_ge(x_updated, KC)
            pool.dma_start(LEVELS_IN, c_levels).then_inc(consts_loaded, 16)
            seen = 0
            for i, (kind, layer) in enumerate(phases):
                if kind == "ple":
                    pool.wait_ge(x_updated, KC * i)
                    pool.dma_start(PLE_P, p_t[layer]).then_inc(p_loaded, 16)
                elif kind == "sw":
                    pool.wait_ge(x_updated, KC * (i + 1))
                    pool.dma_start(SW_BIAS, c_swa).then_inc(phase_consts, 16)
                elif kind == "second":
                    pool.wait_ge(p_loaded, 16 * at(i, "ple"))
                    pool.wait_ge(x_updated, KC * max(i - 1, 1))
                    pool.dma_start(SE_MEM, mem_t).then_inc(p_loaded, 16)
                    pool.wait_ge(x_updated, KC * (i + 1))
                    pool.dma_start(SE_CONST, c_second).then_inc(phase_consts, 16)


        @block.tensor
        def _(pe):
            def passes(w, a, k, wc, ac, w_first):
                for wp, ap in ((w_hi, a[0]), (w_lo, a[0]), (w_hi, a[1])):
                    weight = wp[:, w, wc]
                    act = ap[:, k, ac]
                    yield (weight, act) if w_first else (act, weight)

            XG = (xg_hi, xg_lo)
            MO = (mo_hi, mo_lo)

            def project(n, e, a, operand_ready=None, by=1, dn=0, de=0):
                pe.wait_ge(weights_split, n + 1 + dn)
                pe.wait_ge(bank_read, e + 1 + de)
                for k in range(KC):
                    if operand_ready:
                        pe.wait_ge(operand_ready[0], operand_ready[1] + k // by + 1)
                    for half in range(2):
                        wc = slice(k * 256 + half * P, k * 256 + (half + 1) * P)
                        for j, (l, r) in enumerate(passes(n % SPLIT, a, k, wc, slice(0, T), True)):
                            last = nc.tensor.matmul(bank(e)[:, half * T:(half + 1) * T], l, r,
                                                    start=(k == 0 and j == 0 and half == 0),
                                                    stop=(k == KC - 1 and j == 2), skip_group_check=True)
                last.then_inc(weights_used, 1)

            def project_tokens(n, e, a):
                pe.wait_ge(weights_split, n + 1)
                pe.wait_ge(bank_read, e + 1)
                for b in range(TB):
                    for k in range(KC):
                        wc = slice(k * 256, (k + 1) * 256)
                        for j, (l, r) in enumerate(passes(n % SPLIT, a, k, wc, slice(b * P, (b + 1) * P), False)):
                            last = nc.tensor.matmul(bank(e)[:, b * T:(b + 1) * T], l, r,
                                                    start=(k == 0 and j == 0), stop=(k == KC - 1 and j == 2))
                last.then_inc(weights_used, 1)

            def rows(n, a, slot, first, last_unit, dn=0, chunk_sem=None, cleared=None):
                pe.wait_ge(weights_split, n + 1 + dn)
                for c in range(KC):
                    if cleared and c % 2 == 0:
                        pe.wait_ge(cleared[0], cleared[1] + cleared[2] * (c // 2))
                    for k in range(2):
                        wc = slice(k * D_MODEL + c * P, k * D_MODEL + (c + 1) * P)
                        for j, (l, r) in enumerate(passes(n % SPLIT, a, slot + k, wc, slice(0, T), True)):
                            last = nc.tensor.matmul(ps[:, 4 + c // 2, (c % 2) * T:(c % 2 + 1) * T], l, r,
                                                    start=(first and k == 0 and j == 0 and c % 2 == 0),
                                                    stop=(last_unit and k == 1 and j == 2), skip_group_check=True)
                    if chunk_sem is not None and c in (1, 3, 5):
                        last.then_inc(chunk_sem, 1)
                last.then_inc(weights_used, 1)

            def norm_sums(i):
                if i == 0:
                    pe.wait_ge(consts_loaded, 16)
                if phases[i][0] == "ple":
                    pe.wait_ge(bank_read, at(i, "banks") + 4)
                pe.wait_ge(square_sum, i + 1)
                nc.tensor.matmul(norm_bank(i)[:, 0:T], ones, SQ_SUM, start=True, stop=True).then_inc(sums_ready, 1)

            def token_columns(i):
                pe.wait_ge(rstd_ready, i + 1)
                for b in range(TB):
                    last = nc.tensor.matmul(norm_bank(i)[:, 256 + b:257 + b], rstd[0:1, b * P:(b + 1) * P],
                                            ones[0:1, 0:1], start=True, stop=True)
                last.then_inc(rcol_sums, 1)

            def ffn(i):
                n0, e0, h0 = at(i, "units"), at(i, "banks"), at(i, "hidden")
                x0 = KC * i
                project(n0, e0, XG, (xg_ready, x0))
                project(n0 + 1, e0 + 1, XG)
                norm_sums(i)
                project(n0 + 2, e0 + 2, XG)
                project(n0 + 3, e0 + 3, XG)
                pe.wait_ge(rstd_ready, i + 1)

                def down(s, n, dn=0, dh=0):
                    pe.wait_ge(hidden_ready, h0 + 2 * s + 2 + dh)
                    rows(n, MO, (2 * s) % 4, first=(s == 0), last_unit=(s == STEPS - 1), dn=dn,
                         chunk_sem=acc_ready if s == STEPS - 1 else None)
                down(0, n0 + 4)
                with pe.Fori(0, (STEPS - 3) // 2) as it:
                    for s in (2, 3):
                        project(n0 + 3 * s - 1, e0 + 2 * s, XG, dn=6 * it, de=4 * it)
                        project(n0 + 3 * s, e0 + 2 * s + 1, XG, dn=6 * it, de=4 * it)
                        down(s - 1, n0 + 3 * s + 1, dn=6 * it, dh=4 * it)
                s = STEPS - 1
                project(n0 + 3 * s - 1, e0 + 2 * s, XG)
                project(n0 + 3 * s, e0 + 2 * s + 1, XG)
                down(s - 1, n0 + 3 * s + 1)
                down(s, n0 + 3 * s + 2)

            def ple(i):
                n0, e0, x0 = at(i, "units"), at(i, "banks"), KC * i
                pe.wait_ge(p_ready, at(i, "ple") + 1)
                rows(n0, MO, 4, True, True, cleared=(x_updated, x0 + 1, 2))
                project(n0 + 1, e0, XG, (xg_ready, x0))
                norm_sums(i)
                project(n0 + 2, e0 + 1, XG)
                project(n0 + 3, e0 + 2, XG)
                pe.wait_ge(rstd_ready, i + 1)
                project(n0 + 4, e0 + 3, XG)

            def mixer_head(i):
                n0, e0 = at(i, "units"), at(i, "banks")
                project(n0, e0, XG, (xg_ready, KC * i))
                project(n0 + 1, e0 + 1, XG)
                norm_sums(i)
                project(n0 + 2, e0 + 2, XG)
                token_columns(i)
                project(n0 + 3, e0 + 3, XG)

            def w_out(i, n, e):
                for u in range(4):
                    project(n + u, e + u, MO, (mo_ready, 4 * rcols(i)) if u == 0 else None, by=2)

            def hg(i):
                m = own[i]
                n0, e0 = at(i, "units"), at(i, "banks")
                mixer_head(i)
                for u in range(4, 8):
                    project(n0 + u, e0 + u, XG)
                for u in range(8, 12):
                    project_tokens(n0 + u, e0 + u, XG)
                pe.wait_ge(bank_read, e0 + 12 + 4)
                pe.wait_ge(m["qsilu"], 4)
                pe.wait_ge(m["qk"], 1)
                for g in range(16):
                    h, b = g // 2, g % 2
                    last = nc.tensor.matmul(ps[:, g // 4, (g % 4) * P:(g % 4 + 1) * P],
                                            HG_K[:, h, b * P:(b + 1) * P], HG_Q[:, h, b * P:(b + 1) * P],
                                            start=True, stop=True)
                last.then_inc(m["level"], 1)
                for l in range(len(LEVELS)):
                    pe.wait_ge(m["qk"], l + 2)
                    if l >= 1:
                        pe.wait_ge(m["taken"], l)
                    D = HG_D[l % 2]
                    for g in range(16):
                        blk = D[:, g * P:(g + 1) * P]
                        last = nc.tensor.matmul(ps[:, 4 * ((l + 1) % 2) + g // 4, (g % 4) * P:(g % 4 + 1) * P],
                                                blk, blk, start=True, stop=True)
                    last.then_inc(m["level"], 1)
                l = len(LEVELS)
                pe.wait_ge(m["qk"], l + 2)
                pe.wait_ge(m["taken"], l)
                D = HG_D[l % 2]
                for h in range(HG_HEADS):
                    last = nc.tensor.matmul(ps[:, h // 4, (h % 4) * P:(h % 4 + 1) * P],
                                            D[:, h * T:h * T + P], D[:, h * T + P:(h + 1) * T],
                                            start=True, stop=True)
                last.then_inc(m["level"], 1)
                pe.wait_ge(m["taken"], len(LEVELS) + 1)
                pe.wait_ge(m["off"], 1)
                for h in range(HG_HEADS):
                    o = ps[:, h // 2, (h % 2) * T:(h % 2 + 1) * T]
                    v = HG_V[:, :, h * P:(h + 1) * P]
                    nc.tensor.matmul(o[:, 0:P], v[:, 0, :], HG_AT[:, 2 * h, :], start=True, stop=True)
                    nc.tensor.matmul(o[:, P:T], v[:, 0, :], HG_OFF[:, h, :], start=True, stop=False)
                    last = nc.tensor.matmul(o[:, P:T], v[:, 1, :], HG_AT[:, 2 * h + 1, :], start=False, stop=True)
                    if h % 2:
                        last.then_inc(m["o"], 1)
                for h in range(HG_HEADS):
                    if h % 2 == 0:
                        pe.wait_ge(m["sq"], h // 2 + 1)
                    last = nc.tensor.matmul(ps[:, 4 + h // 2, (h % 2) * T:(h % 2 + 1) * T], ones, HG_SQ[:, h, :],
                                            start=True, stop=True)
                    if h % 2:
                        last.then_inc(m["sums"], 1)
                pe.wait_ge(m["done"], 4)
                for u in range(12, 16):
                    project(n0 + u, e0 + u, XG)
                w_out(i, n0 + 16, e0 + 16)

            def ml(i):
                m = own[i]
                n0, e0 = at(i, "units"), at(i, "banks")
                mixer_head(i)
                pe.wait_ge(m["wif"], 1)
                for g in range(2):
                    for k in range(KC):
                        last = nc.tensor.matmul(ps[0:4, 4, g * T:(g + 1) * T], tiny[:, k * 8 + 4 * g:k * 8 + 4 * g + 4],
                                                x[:, k, :], start=(k == 0), stop=(k == KC - 1))
                last.then_inc(m["gates"], 1)
                for u in range(4, 8):
                    project_tokens(n0 + u, e0 + u, XG)
                pe.wait_ge(m["row"], 1)
                for b in range(TB):
                    last = nc.tensor.matmul(ps[:, 4, 4 * b:4 * b + 4], ML_ROWS[0:4, 4, b * P:(b + 1) * P],
                                            ident[0:4, 0:4], start=True, stop=True)
                last.then_inc(m["cols"], 1)
                for h in range(ML_HEADS):
                    last = nc.tensor.matmul(ps[:, 6 + h // 2, (h % 2) * T:(h % 2 + 1) * T], selector(h),
                                            ML_ROWS[0:4, 6, :], start=True, stop=True)
                last.then_inc(m["bcast"], 1)
                pe.wait_ge(bank_read, e0 + 8 + 4)
                for h in range(ML_HEADS):
                    nc.tensor.matmul(ps[:, h, 0:T], ML_K[:, h, 0:P], ML_Q[:, h, :], start=True, stop=True)
                    nc.tensor.matmul(ps[:, h, T:T + P], ML_K[:, h, P:T], ML_Q[:, h, P:T],
                                     start=True, stop=True).then_inc(m["scores"], 1)
                pe.wait_ge(m["ucol"], 1)
                pe.wait_ge(m["arg"], ML_HEADS)
                for h in range(ML_HEADS):
                    last = nc.tensor.matmul(ps[:, 6 + h // 2, (h % 2) * T:(h % 2 + 1) * T], selector(h),
                                            ML_ROWS[0:4, 7, :], start=True, stop=True)
                last.then_inc(m["guard"], 1)
                for h in range(ML_HEADS):
                    pe.wait_ge(m["w"], h + 1)
                    w0, w1 = ML_W[:, h, 0:T], ML_W[:, h, T:T + P]
                    for d in range(2):
                        v = ML_V[:, :, h * ML_DV + d * P:h * ML_DV + (d + 1) * P]
                        nc.tensor.matmul(ps[:, h, d * T:(d + 1) * T], v[:, 0], w0, start=True, stop=False,
                                         skip_group_check=True)
                        last = nc.tensor.matmul(ps[:, h, d * T + P:(d + 1) * T], v[:, 1], w1, start=False, stop=True,
                                                skip_group_check=True)
                    last.then_inc(m["num"], 1)
                    o = ps[:, 4 + h // 2, (h % 2) * T:(h % 2 + 1) * T]
                    nc.tensor.matmul(o, ones, w0, start=True, stop=False, skip_group_check=True)
                    nc.tensor.matmul(o[:, P:T], ones, w1, start=False, stop=True,
                                     skip_group_check=True).then_inc(m["den"], 1)
                pe.wait_ge(m["gexp"], 1)
                for h in range(ML_HEADS):
                    pe.wait_ge(m["sq"], h + 1)
                    o = ps[:, 6 + h // 2, (h % 2) * T:(h % 2 + 1) * T]
                    nc.tensor.matmul(o, ones, ML_T[:, 2 * h], start=True, stop=False)
                    last = nc.tensor.matmul(o, ones, ML_T[:, 2 * h + 1], start=False, stop=True)
                    if h % 2:
                        last.then_inc(m["sums"], 1)
                pe.wait_ge(m["h"], ML_HEADS)
                for u in range(8, 12):
                    project(n0 + u, e0 + u, XG)
                w_out(i, n0 + 12, e0 + 12)

            def attention(g0, groups, bufs, read="exp", late=False):
                PR, PT = bufs

                def scores(g):
                    if g >= len(groups):
                        return
                    if g >= 2:
                        pe.wait_ge(att[read], g0 + g - 1)
                    if "ready" in groups[g]:
                        pe.wait_ge(*groups[g]["ready"])
                    for at_, n, q, k in groups[g]["scores"]:
                        at_ += 1024 * (g % 2)
                        last = nc.tensor.matmul(ps[:, at_ // 512, at_ % 512:at_ % 512 + n], q, k, start=True, stop=True)
                    last.then_inc(att["scores"], 1)

                def turn(g):
                    G = groups[g]
                    pe.wait_ge(att["probs"], g0 + g + 1)
                    if g >= 1:
                        pe.wait_ge(att["pt"], g0 + g)
                    for j in range(G["slots"] * G["width"] // P):
                        if (j * P) % 256 >= G["k0"]:
                            last = nc.tensor.transpose(ps[:, 4 + j // 4, (j % 4) * P:(j % 4 + 1) * P],
                                                       PR[g % len(PR)][:, j * P:(j + 1) * P], ident)
                    last.then_inc(att["turned"], 1)

                def values(g):
                    pe.wait_ge(att["pt"], g0 + g + 1)
                    if g >= 2:
                        pe.wait_ge(att["taken"], g0 + g - 1)
                    for r, col, vs in groups[g]["values"]:
                        for j, (v, block_) in enumerate(vs):
                            last = nc.tensor.matmul(ps[r, 6 + g % 2, col:col + P], v,
                                                    PT[g % 2][:, block_ * P:(block_ + 1) * P],
                                                    start=(j == 0), stop=(j == len(vs) - 1))
                    last.then_inc(att["out"], 1)

                scores(0)
                scores(1)
                for g in range(len(groups)):
                    if g or not late:
                        scores(g + 2)
                    turn(g)
                    if g == 0 and late:
                        scores(2)
                    if g:
                        values(g - 1)
                values(len(groups) - 1)

            def sw(i):
                m = own[i]
                n0, e0 = at(i, "units"), at(i, "banks")

                def sums(p):
                    pe.wait_ge(m["sq"], p + 1)
                    nc.tensor.matmul(ps[:, 4 + p % 4, :], halves,
                                     SW_SQ[:, 2 * (p % 4):2 * (p % 4) + 2].rearrange("p c t -> p (c t)"),
                                     start=True, stop=True).then_inc(m["sums"], 1)
                mixer_head(i)
                for p in range(4):
                    sums(p)
                project(n0 + 4, e0 + 4, XG)
                project(n0 + 5, e0 + 5, XG)
                project_tokens(n0 + 6, e0 + 6, XG)
                pe.wait_ge(m["rs"], 4)
                sums(4)
                sums(5)
                pe.wait_ge(bank_read, e0 + 7 + 4)
                groups = quad_groups(SW_QK, SW_QK[:, 8:12], SW_V, SW_KV, True)
                for G in groups:
                    G["ready"] = (m["qk"], 4 if G["kv"] < 2 else 6)
                attention(att_before(i), groups, ATT_SW, read="bias")
                w_out(i, n0 + 7, e0 + 7)

            def banks_clear(g):
                for what in ("exp", "pt", "taken"):
                    pe.wait_ge(att[what], g)

            def second(i):
                m = own[i]
                n0, e0 = at(i, "units"), at(i, "banks")
                project(n0, e0, MO, (m["memready"], 0))
                pe.wait_ge(m["memsum"], 1)
                nc.tensor.matmul(ps[:, 4, 0:T], ones, SE_MSUM, start=True, stop=True).then_inc(m["memsums"], 1)
                project(n0 + 1, e0 + 1, MO)
                norm_sums(i)
                pe.wait_ge(m["memrs"], 1)
                for b in range(TB):
                    last = nc.tensor.matmul(ps[:, 4, T + b:T + b + 1], SE_RMEM[0:1, b * P:(b + 1) * P], ones[0:1, 0:1],
                                            start=True, stop=True)
                last.then_inc(m["memcols"], 1)
                project_tokens(n0 + 2, e0 + 2, MO)
                token_columns(i)
                project_tokens(n0 + 3, e0 + 3, MO)
                project(n0 + 4, e0 + 4, XG, (xg_ready, KC * i))
                for u in range(5, 8):
                    project(n0 + u, e0 + u, XG)
                for p in range(3):
                    pe.wait_ge(m["sq"], p + 1)
                    nc.tensor.matmul(ps[:, 5 + p, :], halves,
                                     SE_SQ[:, 2 * p:2 * p + 2].rearrange("p c t -> p (c t)"),
                                     start=True, stop=True).then_inc(m["sums"], 1)
                project(n0 + 8, e0 + 8, XG)
                project_tokens(n0 + 9, e0 + 9, XG)
                for p in range(3):
                    pe.wait_ge(m["x"], p + 1)
                    pair = (SE_QB[:, 2 * p:2 * p + 2] if p < 2 else SE_KB).rearrange("p c t -> p (c t)")
                    nc.tensor.matmul(ps[:, 5 + p, :], rot32, pair, start=True, stop=True).then_inc(m["rot"], 1)
                pe.wait_ge(bank_read, e0 + 10 + 4)
                branch_b = quad_groups(SE_QB, SE_KB, SE_VB, 2, False)
                for G in branch_b:
                    G["ready"] = (m["roped"], 3)
                attention(att_before(i, 0), memory_groups() + branch_b, ATT_2, late=True)
                for half in range(2):
                    u0 = 10 + 9 * half
                    banks_clear(att_before(i, 2 + half))

                    def turn(p):
                        r = 3 + 6 * half + p
                        pe.wait_ge(bank_read, e0 + u0 + p + 5)
                        if p >= 2:
                            pe.wait_ge(m["roped"], r - 1)
                        nc.tensor.matmul(ps[:, 4 + p % 2, :], rot, SE_X[p % 2].rearrange("p c t -> p (c t)"),
                                         start=True, stop=True).then_inc(m["rot"], 1)
                    for u in range(6):
                        project(n0 + u0 + u, e0 + u0 + u, XG)
                        if u:
                            turn(u - 1)
                    project_tokens(n0 + u0 + 6, e0 + u0 + 6, XG)
                    turn(5)
                    project_tokens(n0 + u0 + 7, e0 + u0 + 7, XG)
                    project_tokens(n0 + u0 + 8, e0 + u0 + 8, XG)
                    pe.wait_ge(bank_read, e0 + u0 + 9 + 4)
                    pe.wait_ge(m["roped"], 9 + 6 * half)
                    attention(att_before(i, 2 + half), dilated_groups(), ATT_A, read="bias")
                banks_clear(att_before(i, 4))
                for u in range(28, 34):
                    project(n0 + u, e0 + u, XG)
                n, e = n0 + 34, e0 + 34
                for br in range(3):
                    pe.wait_ge(m["mlo"], br + 1)
                    rows(n, MO, 4 * (br % 2), True, False, cleared=(m["merged"], 4 * br - 3, 1) if br else None)
                    rows(n + 1, MO, 4 * (br % 2) + 2, False, True)
                    for u in range(4):
                        project(n + 2 + u, e + u, XG)
                    n, e = n + 6, e + 4

                def square_sums(u):
                    if u == 0:
                        pe.wait_ge(m["merged"], 9)
                    pe.wait_ge(m["fsq"], u + 1)
                    for c in (2 * u, 2 * u + 1):
                        last = nc.tensor.matmul(ps[:, 4, 0:T], ones, SE_YSQ[:, c, :], start=(c == 0), stop=(c == KC - 1))
                    return last
                for u in range(4):
                    project(n + u, e + u, MO, (m["low"], 0) if u == 0 else None, by=2)
                    if u:
                        square_sums(u - 1)
                square_sums(3).then_inc(m["fin"], 1)

            for i, (kind, _) in enumerate(phases):
                {"ffn": ffn, "ple": ple, "hg": hg, "ml": ml, "sw": sw, "second": second}[kind](i)

        @block.scalar
        def _(act):
            def high(m, dm=0, turn=0):
                if m >= NU:
                    return
                act.wait_ge(raw_full[m % RAW], 16 * turn + 16 * (m // RAW + 1))
                if m >= SPLIT:
                    act.wait_ge(weights_used, m + 1 - SPLIT + dm)
                nc.scalar.copy(w_hi[:, m % SPLIT, :], raw[:, m % RAW, :]).then_inc(weights_hi, 1)

            def norm(i, early, besides=None):
                act.wait_ge(x_updated, KC * (i + 1))
                nc.scalar.activation(SQ, x[:], ACT.Square).then_inc(squares_ready, 1)
                high(early)
                if besides:
                    besides()
                act.wait_ge(sums_ready, i + 1)
                sums = norm_bank(i)[:, 0:T]
                nc.scalar.activation(rstd[:], sums, ACT.Ln, bias=EPSB, scale=1.0 / D_MODEL).then_inc(act_chain, 1)
                chain[0] += 1
                act.wait_ge(act_chain, chain[0])
                nc.scalar.activation(rstd[:], rstd[:], ACT.Exp, scale=-0.5).then_inc(rstd_ready, 1)

            chain = [0]

            def link(ins):
                chain[0] += 1
                ins.then_inc(act_chain, 1)
                act.wait_ge(act_chain, chain[0])

            def ffn(i):
                n0, h0 = at(i, "units"), at(i, "hidden")
                norm(i, n0 + SPLIT)

                def up(j, n, dn=0, dh=0, turn=0, early=False):
                    act.wait_ge(up_scaled, h0 + j + 1 + dh)
                    nc.scalar.activation(FFN_T[:, 2 + j % 2], FFN_T[:, j % 2], ACT.Silu).then_inc(silu_ready, 1)
                    if not early:
                        high(n + SPLIT, dn, turn)
                    act.wait_ge(hidden_value, h0 + j + 1 + dh)
                    nc.scalar.copy(mo_hi[:, j % 4], FFN_H[:, j % 2]).then_inc(hidden_hi, 1)
                for j in range(4):
                    up(j, n0 + j, early=(j == 0))
                high(n0 + 4 + SPLIT)
                if i + 1 < nphase and phases[i + 1][0] == "ple":
                    act.wait_ge(p_loaded, 16 * (at(i, "ple") + 1))
                    nc.scalar.copy(mo_hi[:, 4:6], PLE_P).then_inc(p_hi_ready, 1)
                with act.Fori(0, (STEPS - 3) // 2) as it:
                    for s in (2, 3):
                        up(2 * s, n0 + 3 * s - 1, 6 * it, 4 * it, it)
                        up(2 * s + 1, n0 + 3 * s, 6 * it, 4 * it, it)
                        high(n0 + 3 * s + 1 + SPLIT, 6 * it, it)
                s = STEPS - 1
                up(2 * s, n0 + 3 * s - 1)
                up(2 * s + 1, n0 + 3 * s)
                high(n0 + 3 * s + 1 + SPLIT)
                high(n0 + 3 * s + 2 + SPLIT)

            def ple(i):
                n0, e0 = at(i, "units"), at(i, "banks")
                norm(i, n0 + SPLIT)
                for u in range(4):
                    high(n0 + 1 + u + SPLIT)
                    act.wait_ge(bank_read, e0 + u + 5)
                    pair = PLE_T[:, 2 * u:2 * u + 2]
                    nc.scalar.activation(pair, pair, ACT.Sigmoid).then_inc(ple_gate, 1)
                    if u == 1 and phases[i + 1:i + 2] == [("second", 0)]:
                        act.wait_ge(p_loaded, 16 * (at(i, "ple") + 2))
                        nc.scalar.activation(SE_MSQ, SE_MEM, ACT.Square).then_inc(own[i + 1]["memsq"], 1)

            def gates_out(i, m, unit, e, value, func):
                for u in range(4):
                    if u < 3:
                        high(unit + u + SPLIT)
                    act.wait_ge(bank_read, e + u + 5)
                    pair = value[:, 2 * u:2 * u + 2]
                    nc.scalar.activation(pair, pair, func).then_inc(m["gate"], 1)
                    act.wait_ge(m["prod"], u + 1)
                    nc.scalar.copy(mo_hi[:, 2 * u:2 * u + 2], OUT[:, 2 * u:2 * u + 2]).then_inc(mo_high, 1)
                    if u == 3:
                        high(unit + u + SPLIT)
                for u in range(4, 8):
                    high(unit + u + SPLIT)

            def hg(i):
                m = own[i]
                n0, e0 = at(i, "units"), at(i, "banks")
                if phases[i][1] > 0:
                    act.wait_ge(m["lbdiff"], 1)
                    nc.scalar.activation(tiny[:, 16:48], tiny[:, 16:48], ACT.Exp).then_inc(m["lbexp"], 1)
                norm(i, n0 + SPLIT)
                for u in range(4):
                    act.wait_ge(bank_read, e0 + u + 5)
                    k, b = HG_K[:, 2 * u:2 * u + 2], HG_B[:, 2 * u:2 * u + 2]
                    nc.scalar.activation(b, k, ACT.Sigmoid)
                    nc.scalar.activation(k, k, ACT.Sigmoid, scale=-1.0).then_inc(m["sig"], 1)
                    if u:
                        high(n0 + u + SPLIT)
                for u in range(4, 8):
                    high(n0 + u + SPLIT)
                    act.wait_ge(bank_read, e0 + u + 5)
                    q = HG_Q[:, 2 * (u - 4):2 * (u - 4) + 2]
                    nc.scalar.activation(q, q, ACT.Silu).then_inc(m["qsilu"], 1)
                    if u > 4:
                        continue
                    for c in range(KC):
                        act.wait_ge(m["clamp"], c // 2 + 1)
                        nc.scalar.activation(HG_B[:, c], HG_B[:, c], ACT.Ln, bias=tiny[:, 8 + c:9 + c],
                                             scale=tiny[:, c:c + 1]).then_inc(m["logf"], 1)

                def decays(l):
                    D = HG_D[l % 2].rearrange("p (n a w) -> p n a w", a=2, w=LEVELS[l])
                    for a in (1, 0):
                        act.wait_ge(m["diff"], 2 * l + 2 - a)
                        nc.scalar.activation(D[:, :, a, :], D[:, :, a, :], ACT.Exp).then_inc(m["exp"], 1)
                for u in range(8, 12):
                    high(n0 + u + SPLIT)
                    if u == 10:
                        decays(0)

                def take(s, w):
                    act.wait_ge(m["level"], s + 1)
                    act.wait_ge(m["taken"], s)
                    A = ps[:, 4 * (s % 2):4 * (s % 2) + 4, :].rearrange("p b (g t) -> p (b g) t", t=P)
                    for k0 in range(0, P, 2 * w):
                        ins = nc.scalar.copy(HG_AT[k0:k0 + w, :, k0 + w:k0 + 2 * w], A[k0:k0 + w, :, k0 + w:k0 + 2 * w])
                    ins.then_inc(m["taken"], 1)
                for l in range(1, len(LEVELS)):
                    if 2 <= l < 2 + RECT_LEVELS:
                        take(l - 1, LEVELS[l - 2])
                    decays(l)
                l = len(LEVELS)
                D = HG_D[l % 2].rearrange("p (h a w) -> p h a w", a=2, w=P)
                act.wait_ge(m["diff"], 2 * l + 1)
                nc.scalar.activation(D[:, :, 1, :], HG_B[:, :, P:T], ACT.Exp).then_inc(m["exp"], 1)
                nc.scalar.activation(D[:, :, 0, :], D[:, :, 0, :], ACT.Exp).then_inc(m["exp"], 1)
                act.wait_ge(m["level"], l + 2)
                nc.scalar.copy(HG_OFF[:, :, :].rearrange("p h t -> p (h t)"),
                               ps[:, 0:2, :].rearrange("p b t -> p (b t)")).then_inc(m["off"], 1)
                for p in range(4):
                    act.wait_ge(m["done"], p + 1)
                    nc.scalar.activation(HG_SQ[:, 2 * p:2 * p + 2], HG_B[:, 2 * p:2 * p + 2],
                                         ACT.Square).then_inc(m["sq"], 1)
                for p in range(4):
                    act.wait_ge(m["sums"], p + 1)
                    ins = nc.scalar.activation(HG_RS[:, 2 * p:2 * p + 2].rearrange("p c t -> p (c t)"),
                                               ps[:, 4 + p, :], ACT.Ln, bias=EPSB, scale=1.0 / P)
                link(ins)
                for p in range(4):
                    r = HG_RS[:, 2 * p:2 * p + 2]
                    nc.scalar.activation(r, r, ACT.Exp, scale=-0.5).then_inc(m["rs"], 1)
                gates_out(i, m, n0 + 12, e0 + 12, HG_K, ACT.Silu)

            def ml(i):
                m = own[i]
                n0, e0 = at(i, "units"), at(i, "banks")
                norm(i, n0 + SPLIT)
                for u in range(1, 8):
                    high(n0 + u + SPLIT)
                    if u == 4:
                        g, f, sp = ML_ROWS[0:4, 0:2], ML_ROWS[0:4, 1], ML_ROWS[0:4, 2]
                        act.wait_ge(m["lin"], 1)
                        link(nc.scalar.activation(g, g, ACT.Tanh, scale=1.0 / GATE_CAP))
                        link(nc.scalar.activation(sp, f, ACT.Exp, scale=-GATE_CAP))
                        nc.scalar.activation(sp, sp, ACT.Ln, bias=ones[0:4, 0:1]).then_inc(m["soft"], 1)
                for h in range(ML_HEADS):
                    act.wait_ge(m["arg"], h + 1)
                    nc.scalar.activation(ML_W[:, h], ML_W[:, h], ACT.Exp).then_inc(m["exp"], 1)
                act.wait_ge(m["guard"], 1)
                nc.scalar.activation(ML_GUARD.rearrange("p c t -> p (c t)"),
                                     ps[:, 6:8, :].rearrange("p b t -> p (b t)"), ACT.Exp).then_inc(m["gexp"], 1)
                for h in range(ML_HEADS):
                    act.wait_ge(m["h"], h + 1)
                    nc.scalar.activation(ML_T[:, 2 * h:2 * h + 2], ML_H[:, 2 * h:2 * h + 2],
                                         ACT.Square).then_inc(m["sq"], 1)
                act.wait_ge(m["den"], ML_HEADS)
                nc.scalar.activation(ML_DEN.rearrange("p c t -> p (c t)"),
                                     ps[:, 4:6, :].rearrange("p b t -> p (b t)"), ACT.Abs).then_inc(m["gexp"], 1)
                act.wait_ge(m["nrm"], 2)
                link(nc.scalar.activation(ML_GUARD, ML_GUARD, ACT.Ln))
                for p in range(2):
                    r = ML_GUARD[:, 2 * p:2 * p + 2]
                    nc.scalar.activation(r, r, ACT.Exp, scale=-0.5).then_inc(m["rs"], 1)
                gates_out(i, m, n0 + 8, e0 + 8, ML_T, ACT.Sigmoid)

            def attention(g0, groups, bufs, sinks=False, from_psum=False):
                PR, PT = bufs

                def exps(g):
                    if g == len(groups):
                        return
                    G = groups[g]
                    t = tiny[:, 32 * (g % 3):32 * (g % 3) + 32]
                    act.wait_ge(att["bias"], g0 + g + 1)
                    if from_psum and g >= len(PR):
                        act.wait_ge(att["turned"], g0 + g - len(PR) + 1)
                    if sinks:
                        nc.scalar.activation(t[:, 12:16], t[:, 12:16], ACT.Exp, scale=G["scale"])
                    for s in range(G["slots"]):
                        p = PR[g % len(PR)][:, s * G["width"] + G["k0"]:(s + 1) * G["width"]]
                        src = ps[:, 2 * (g % 2) + s // 2, (s % 2) * 256:(s % 2 + 1) * 256] if from_psum else p
                        last = nc.scalar.activation(p, src, ACT.Exp, bias=t[:, 4 + s:5 + s], scale=G["scale"],
                                                    accum_out=t[:, 8 + s:9 + s])
                    last.then_inc(att["exp"], 1)

                exps(0)
                for g, G in enumerate(groups):
                    exps(g + 1)
                    act.wait_ge(att["turned"], g0 + g + 1)
                    if g >= 2:
                        act.wait_ge(att["out"], g0 + g - 1)
                    n = G["slots"] * G["width"]
                    src = ps[:, 4:6, :].rearrange("p b t -> p (b t)")[:, 0:n]
                    dst = PT[g % 2][:, 0:n]
                    if G["k0"]:
                        src, dst = (v.rearrange("p (s k) -> p s k", k=256)[:, :, G["k0"]:] for v in (src, dst))
                    nc.scalar.copy(dst, src).then_inc(att["pt"], 1)

            def sw(i):
                m = own[i]
                n0, e0 = at(i, "units"), at(i, "banks")
                norm(i, n0 + SPLIT)

                def roots(p0, p1):
                    for p in range(p0, p1):
                        act.wait_ge(m["sums"], p + 1)
                        ins = nc.scalar.activation(
                            SW_SQ[:, 2 * (p % 4):2 * (p % 4) + 2].rearrange("p c t -> p (c t)"), ps[:, 4 + p % 4, :],
                            ACT.Ln, bias=EPSB, scale=1.0 / HD)
                    link(ins)
                    for p in range(p0, p1):
                        r = SW_SQ[:, 2 * (p % 4):2 * (p % 4) + 2]
                        nc.scalar.activation(r, r, ACT.Exp, scale=-0.5).then_inc(m["rs"], 1)

                for u in range(6):
                    act.wait_ge(bank_read, e0 + u + 5)
                    if u >= 4:
                        act.wait_ge(m["qk"], u - 3)
                    nc.scalar.activation(SW_SQ[:, 2 * (u % 4):2 * (u % 4) + 2], sw_pair(u),
                                         ACT.Square).then_inc(m["sq"], 1)
                    if u:
                        high(n0 + u + SPLIT)
                    if u == 3:
                        roots(0, 4)
                high(n0 + 6 + SPLIT)
                roots(4, 6)
                attention(att_before(i), quad_groups(SW_QK, SW_QK[:, 8:12], SW_V, SW_KV, True), ATT_SW, sinks=True)
                for u in range(4):
                    act.wait_ge(att["taken"], att_before(i) + 2 * u + 2)
                    nc.scalar.copy(mo_hi[:, 2 * u:2 * u + 2], SW_O[:, 2 * u:2 * u + 2]).then_inc(mo_high, 1)
                for u in range(4):
                    high(n0 + 7 + u + SPLIT)

            def second(i):
                m = own[i]
                n0, e0 = at(i, "units"), at(i, "banks")

                def memory_root():
                    act.wait_ge(m["memsums"], 1)
                    link(nc.scalar.activation(SE_RMEM, ps[:, 4, 0:T], ACT.Ln, bias=EPSB, scale=1.0 / D_MODEL))
                    nc.scalar.activation(SE_RMEM, SE_RMEM, ACT.Exp, scale=-0.5).then_inc(m["memrs"], 1)
                norm(i, n0 + SPLIT, memory_root)
                for u in range(1, 4):
                    high(n0 + u + SPLIT)
                for p in range(3):
                    act.wait_ge(bank_read, e0 + 4 + p + 5)
                    pair = SE_QB[:, 2 * p:2 * p + 2] if p < 2 else SE_KB
                    nc.scalar.activation(SE_SQ[:, 2 * p:2 * p + 2], pair, ACT.Square).then_inc(m["sq"], 1)
                    high(n0 + 4 + p + SPLIT)
                high(n0 + 7 + SPLIT)
                for p in range(3):
                    act.wait_ge(m["sums"], p + 1)
                    ins = nc.scalar.activation(SE_SQ[:, 2 * p:2 * p + 2].rearrange("p c t -> p (c t)"), ps[:, 5 + p, :],
                                               ACT.Ln, bias=EPSB, scale=1.0 / HD)
                link(ins)
                for p in range(3):
                    r = SE_SQ[:, 2 * p:2 * p + 2]
                    nc.scalar.activation(r, r, ACT.Exp, scale=-0.5).then_inc(m["rs"], 1)
                high(n0 + 8 + SPLIT)
                high(n0 + 9 + SPLIT)
                attention(att_before(i, 0), memory_groups() + quad_groups(SE_QB, SE_KB, SE_VB, 2, False), ATT_2,
                          from_psum=True)
                for half in range(2):
                    for u in range(9):
                        high(n0 + 10 + 9 * half + u + SPLIT)
                    attention(att_before(i, 2 + half), dilated_groups(), ATT_A)

                def fill(br):
                    if br == 2:
                        act.wait_ge(weights_used, n0 + 36)
                    s = 4 * (br % 2)
                    act.wait_ge(m["gated"], 2 * br + 2)
                    nc.scalar.copy(mo_hi[:, s:s + 4], SE_O[:, 4 * br:4 * br + 4]).then_inc(m["mhi"], 1)
                for u in range(6):
                    act.wait_ge(bank_read, e0 + 28 + u + 5)
                    t = SE_GATE[u % 2]
                    nc.scalar.activation(t, t, ACT.Silu).then_inc(m["gate"], 1)
                    high(n0 + 28 + u + SPLIT)
                    if u in (2, 4):
                        fill(u // 2 - 1)
                n, e = n0 + 34, e0 + 34
                for br in range(3):
                    high(n + SPLIT)
                    high(n + 1 + SPLIT)
                    if br == 1:
                        fill(2)
                    for u in range(4):
                        act.wait_ge(bank_read, e + u + 5)
                        t = SE_GATE[u % 2]
                        for c in range(2):
                            b = S_BM + 8 * br + 2 * u + c
                            ins = nc.scalar.activation(t[:, c], t[:, c], ACT.Sigmoid, bias=smalls[:, b:b + 1])
                        ins.then_inc(m["merge"], 1)
                        last = br == 2 and u == 3
                        if not last:
                            high(n + 2 + u + SPLIT)
                        if br == 2:
                            act.wait_ge(m["merged"], 8 + u + 1)
                            nc.scalar.copy(mo_hi[:, 2 * u:2 * u + 2],
                                           SE_MERGED[:, 2 * u:2 * u + 2]).then_inc(m["high"], 1)
                        if last:
                            high(n + 2 + u + SPLIT)
                    n, e = n + 6, e + 4
                for u in range(4):
                    act.wait_ge(bank_read, e + u + 5)
                    nc.scalar.activation(SE_YSQ[:, 2 * u:2 * u + 2], SE_Y[:, 2 * u:2 * u + 2],
                                         ACT.Square).then_inc(m["fsq"], 1)
                    high(n + u + SPLIT)
                act.wait_ge(m["fin"], 1)
                link(nc.scalar.activation(SE_YR, ps[:, 4, 0:T], ACT.Ln, bias=EPSB, scale=1.0 / D_MODEL))
                nc.scalar.activation(SE_YR, SE_YR, ACT.Exp, scale=-0.5).then_inc(m["frs"], 1)

            act.wait_ge(eps_ready, 1)
            for i in range(SPLIT):
                high(i)
            for i, (kind, _) in enumerate(phases):
                {"ffn": ffn, "ple": ple, "hg": hg, "ml": ml, "sw": sw, "second": second}[kind](i)

        @block.vector
        def _(dve):
            chain = [0]

            def link(ins):
                chain[0] += 1
                ins.then_inc(dve_chain, 1)
                dve.wait_ge(dve_chain, chain[0])

            V = nc.vector

            def low(m, dm=0):
                if m >= NU:
                    return
                dve.wait_ge(weights_hi, m + 1 + dm)
                V.tensor_tensor(w_lo[:, m % SPLIT, :], raw[:, m % RAW, :], w_hi[:, m % SPLIT, :].bitcast(F32),
                                ALU.subtract).then_inc(weights_split, 1)

            def row(v, n):
                return v.unsqueeze(1).broadcast_to([P, n, T])

            def pair(e, fixed=False):
                return (ps[:, e, :] if fixed else bank(e)).rearrange("p (c t) -> p c t", c=2)

            def norm(i, early, besides=None):
                dve.wait_ge(squares_ready, i + 1)
                V.tensor_reduce(SQ_SUM, SQ.rearrange("p c t -> p t c"), AX_X, ALU.add).then_inc(square_sum, 1)
                low(early)
                if besides:
                    besides()
                dve.wait_ge(rstd_ready, i + 1)

            def operand_parts(i):
                g = next_gain(i + 1)
                for c in range(KC):
                    V.tensor_scalar(xg_hi[:, c], x[:, c], gain(g, c), None, ALU.mult).then_inc(x_updated, 1)

                def lows():
                    for c in range(KC):
                        dve.wait_ge(x_updated, KC * (i + 1) + c + 1)
                        V.scalar_tensor_tensor(xg_lo[:, c], x[:, c], gain(g, c), xg_hi[:, c].bitcast(F32), ALU.mult,
                                               ALU.subtract).then_inc(xg_ready, 1)
                return lows

            def next_operand(i, c0, n):
                if i + 1 == nphase:
                    return
                g = next_gain(i + 1)
                for two in range(c0, c0 + n, 2):
                    for c in (two, two + 1):
                        V.tensor_scalar(xg_hi[:, c], x[:, c], gain(g, c), None, ALU.mult).then_inc(x_updated, 1)
                    for c in (two, two + 1):
                        dve.wait_ge(x_updated, KC * (i + 1) + c + 1)
                        V.scalar_tensor_tensor(xg_lo[:, c], x[:, c], gain(g, c), xg_hi[:, c].bitcast(F32), ALU.mult,
                                               ALU.subtract).then_inc(xg_ready, 1)

            def scale(n, e, dst):
                dve.wait_ge(weights_used, n + 1)
                V.tensor_tensor(dst, pair(e), row(rstd[:], 2), ALU.mult).then_inc(bank_read, 1)

            def scale_tokens(n, e, dst, col):
                dve.wait_ge(weights_used, n + 1)
                for b in range(TB):
                    ins = V.tensor_scalar(dst[:, b], pair(e)[:, b], rcol[:, col + b:col + b + 1], None, ALU.mult)
                ins.then_inc(bank_read, 1)

            def columns(i):
                dve.wait_ge(rcol_sums, rcols(i) + 1)
                link(V.tensor_copy(rcol[:, 0:2], norm_bank(i)[:, 256:258]))

            def ffn(i):
                n0, e0, h0 = at(i, "units"), at(i, "banks"), at(i, "hidden")
                norm(i, n0 + SPLIT)

                def up(j, n, dn=0, dh=0, early=False):
                    e = e0 + j
                    dve.wait_ge(weights_used, n + 1 + dn)
                    V.tensor_tensor(FFN_T[:, j % 2], pair(e)[:, 0], rstd[:], ALU.mult).then_inc(up_scaled, 1)
                    V.tensor_tensor(FFN_T[:, 4 + j % 2], pair(e)[:, 1], rstd[:], ALU.mult).then_inc(bank_read, 1)
                    dve.wait_ge(bank_read, e + 5 + dh)
                    dve.wait_ge(silu_ready, h0 + j + 1 + dh)
                    V.tensor_tensor(FFN_H[:, j % 2], FFN_T[:, 2 + j % 2], FFN_T[:, 4 + j % 2],
                                    ALU.mult).then_inc(hidden_value, 1)
                    if not early:
                        low(n + SPLIT, dn)
                    dve.wait_ge(hidden_hi, h0 + j + 1 + dh)
                    V.tensor_tensor(mo_lo[:, j % 4], FFN_H[:, j % 2], mo_hi[:, j % 4].bitcast(F32),
                                    ALU.subtract).then_inc(hidden_ready, 1)
                for j in range(4):
                    up(j, n0 + j, early=(j == 0))
                low(n0 + 4 + SPLIT)
                if i == 0:
                    dve.wait_ge(consts_loaded, 32)
                    link(V.tensor_copy(levels[:], LEVELS_IN))
                if i + 1 < nphase and phases[i + 1][0] == "ple":
                    dve.wait_ge(p_hi_ready, at(i, "ple") + 1)
                    V.tensor_tensor(mo_lo[:, 4:6], PLE_P, mo_hi[:, 4:6].bitcast(F32), ALU.subtract).then_inc(p_ready, 1)
                with dve.Fori(0, (STEPS - 3) // 2) as it:
                    for s in (2, 3):
                        up(2 * s, n0 + 3 * s - 1, 6 * it, 4 * it)
                        up(2 * s + 1, n0 + 3 * s, 6 * it, 4 * it)
                        low(n0 + 3 * s + 1 + SPLIT, 6 * it)
                s = STEPS - 1
                up(2 * s, n0 + 3 * s - 1)
                up(2 * s + 1, n0 + 3 * s)
                low(n0 + 3 * s + 1 + SPLIT)
                for u in range(4):
                    if u < 3:
                        dve.wait_ge(acc_ready, at(i, "acc") + u + 1)
                    else:
                        dve.wait_ge(weights_used, n0 + HCH + STEPS)
                    two = x[:, 2 * u:2 * u + 2]
                    link(V.scalar_tensor_tensor(two, pair(4 + u, True), 0.5, two, ALU.mult, ALU.add))
                    next_operand(i, 2 * u, 2)
                low(n0 + 3 * s + 2 + SPLIT)

            second_lows = []

            def ple(i):
                n0, e0 = at(i, "units"), at(i, "banks")
                to_second = phases[i + 1:i + 2] == [("second", 0)]
                norm(i, n0 + SPLIT, (lambda: memory_operand(i, 0, 4)) if to_second else None)

                def gated(u):
                    dve.wait_ge(ple_gate, 4 * at(i, "ple") + u + 1)
                    two = PLE_T[:, 2 * u:2 * u + 2]
                    link(V.tensor_tensor(two, two, pair(4 + u, True), ALU.mult))
                    link(V.tensor_tensor(x[:, 2 * u:2 * u + 2], x[:, 2 * u:2 * u + 2], two, ALU.add))
                for u in range(4):
                    if u == 3:
                        gated(2)
                        dve.wait_ge(weights_used, n0 + 5)
                        if not to_second:
                            next_operand(i, 0, 2)
                    scale(n0 + 1 + u, e0 + u, PLE_T[:, 2 * u:2 * u + 2])
                    if u in (1, 2):
                        gated(u - 1)
                    if u < 2 or (u == 2 and to_second):
                        low(n0 + 1 + u + SPLIT)
                    if to_second and u < 2:
                        memory_operand(i, 4 + 2 * u, 2)
                    if to_second and u == 2:
                        dve.wait_ge(own[i + 1]["memsq"], 1)
                        V.tensor_reduce(SE_MSUM, SE_MSQ.rearrange("p c t -> p t c"), AX_X,
                                        ALU.add).then_inc(own[i + 1]["memsum"], 1)
                if not to_second:
                    next_operand(i, 2, 4)
                gated(3)
                if not to_second:
                    next_operand(i, 6, 2)
                    low(n0 + 3 + SPLIT)
                if to_second:
                    second_lows.append(operand_parts(i))
                low(n0 + 4 + SPLIT)

            def memory_operand(i, c0, n):
                ready = own[i + 1]
                if c0 == 0:
                    dve.wait_ge(p_loaded, 16 * (at(i, "ple") + 2))
                    dve.wait_ge(weights_used, at(i, "units") + 1)
                for c in range(c0, c0 + n):
                    V.tensor_scalar(mo_hi[:, c], SE_MEM[:, c], gain(S_GMEM, c), None, ALU.mult).then_inc(ready["memhi"], 1)
                for c in range(c0, c0 + n):
                    dve.wait_ge(ready["memhi"], c + 1)
                    V.scalar_tensor_tensor(mo_lo[:, c], SE_MEM[:, c], gain(S_GMEM, c), mo_hi[:, c].bitcast(F32),
                                           ALU.mult, ALU.subtract).then_inc(ready["memready"], 1)

            def tail(i, m, unit, e, gate, value):

                def low_part(u):
                    dve.wait_ge(mo_high, 4 * rcols(i) + u + 1)
                    V.tensor_tensor(mo_lo[:, 2 * u:2 * u + 2], OUT[:, 2 * u:2 * u + 2],
                                    mo_hi[:, 2 * u:2 * u + 2].bitcast(F32), ALU.subtract).then_inc(mo_ready, 1)
                for u in range(4):
                    g, v, o = gate[:, 2 * u:2 * u + 2], value[:, 2 * u:2 * u + 2], OUT[:, 2 * u:2 * u + 2]
                    scale(unit + u, e + u, g)
                    if u:
                        low_part(u - 1)
                    if u < 3:
                        low(unit + u + SPLIT)
                    dve.wait_ge(m["gate"], u + 1)
                    V.tensor_tensor(o, v, g, ALU.mult).then_inc(m["prod"], 1)
                low_part(3)
                low(unit + 3 + SPLIT)
                residual(i, unit + 4, e + 4)

            def residual(i, unit, e):
                for u in range(4):
                    dve.wait_ge(weights_used, unit + u + 1)
                    two = x[:, 2 * u:2 * u + 2]
                    V.tensor_tensor(two, two, pair(e + u), ALU.add).then_inc(bank_read, 1)
                    dve.wait_ge(bank_read, e + u + 5)
                    next_operand(i, 2 * u, 2)
                    low(unit + u + SPLIT)

            def lower_bounds(i, layer):
                m = own[i]
                if layer == 0:
                    V.memset(tiny[:, 0:8], 1.0)
                    link(V.memset(tiny[:, 8:16], 0.0))
                    return
                lb = smalls[:, S_LB:S_LB + DEPTH * KC]
                e = tiny[:, 16:48]
                by_depth = "p (l c) -> p c l"
                link(V.tensor_reduce(tiny[:, 48:56], lb.rearrange(by_depth, c=KC), AX_X, ALU.max))
                V.tensor_tensor(e.rearrange("p (l c) -> p l c", c=KC), lb.rearrange("p (l c) -> p l c", c=KC),
                                tiny[:, 48:56].unsqueeze(1).broadcast_to([P, DEPTH, KC]),
                                ALU.subtract).then_inc(m["lbdiff"], 1)
                dve.wait_ge(m["lbexp"], 1)
                V.tensor_reduce(tiny[:, 56:64], e.rearrange(by_depth, c=KC), AX_X, ALU.add)
                part = e[:, KC:KC * (layer + 1)]
                V.tensor_reduce(tiny[:, 64:72], part.rearrange(by_depth, c=KC), AX_X, ALU.add)
                if layer + 1 < DEPTH:
                    rest = e[:, KC * (layer + 1):]
                    link(V.tensor_reduce(tiny[:, 72:80], rest.rearrange(by_depth, c=KC), AX_X, ALU.add))
                    link(V.tensor_tensor(tiny[:, 72:80], tiny[:, 72:80], e[:, 0:KC], ALU.add))
                else:
                    link(V.tensor_copy(tiny[:, 72:80], e[:, 0:KC]))
                link(V.reciprocal(tiny[:, 48:56], tiny[:, 56:64]))
                V.tensor_tensor(tiny[:, 0:8], tiny[:, 72:80], tiny[:, 48:56], ALU.mult)
                link(V.tensor_tensor(tiny[:, 8:16], tiny[:, 64:72], tiny[:, 48:56], ALU.mult))

            def hg(i):
                m = own[i]
                n0, e0 = at(i, "units"), at(i, "banks")
                lower_bounds(i, phases[i][1])
                norm(i, n0 + SPLIT)
                for u in range(4):
                    if u == 2:
                        columns(i)
                    two = slice(2 * u, 2 * u + 2)
                    scale(n0 + u, e0 + u, HG_K[:, two])
                    dve.wait_ge(m["sig"], u + 1)
                    V.tensor_scalar(HG_B[:, two], HG_B[:, two], 2.0 ** -60, None, ALU.max).then_inc(m["clamp"], 1)
                    for c in (2 * u, 2 * u + 1):
                        ins = V.tensor_scalar(HG_K[:, c], HG_K[:, c], tiny[:, c:c + 1], None, ALU.mult)
                    if u == 3:
                        ins.then_inc(m["qk"], 1)
                    if u:
                        low(n0 + u + SPLIT)

                def cumulate(g0):
                    for g in range(g0, g0 + 4):
                        h, b = g // 2, slice((g % 2) * P, (g % 2 + 1) * P)
                        dve.wait_ge(m["logf"], h + 1)
                        V.tensor_tensor_scan(HG_B[:, h, b], ones, HG_B[:, h, b], 0.0, ALU.mult,
                                             ALU.add).then_inc(m["scan"], 1)
                for u in range(4, 8):
                    scale(n0 + u, e0 + u, HG_Q[:, 2 * (u - 4):2 * (u - 4) + 2])
                    low(n0 + u + SPLIT)
                    if u > 4:
                        cumulate(4 * (u - 5))
                L = len(LEVELS)

                def diffs(l):
                    if l >= 2:
                        dve.wait_ge(m["level"], l)
                    if l == L:
                        D = HG_D[l % 2].rearrange("p (h a w) -> p h a w", a=2, w=P)
                        V.tensor_tensor(D[:, :, 0, :], HG_B[:, :, P - 1:P].broadcast_to([P, HG_HEADS, P]),
                                        HG_B[:, :, 0:P], ALU.subtract).then_inc(m["diff"], 1)
                        return
                    w = LEVELS[l]
                    D = HG_D[l % 2].rearrange("p (n a w) -> p n a w", a=2, w=w)
                    B = HG_FLAT_B.rearrange("p (n a w) -> p n a w", a=2, w=w)
                    mid = B[:, :, 0, w - 1:w].broadcast_to([P, UNIT // (2 * w), w])
                    V.tensor_tensor(D[:, :, 1, :], B[:, :, 1, :], mid, ALU.subtract).then_inc(m["diff"], 1)
                    V.tensor_tensor(D[:, :, 0, :], mid, B[:, :, 0, :], ALU.subtract).then_inc(m["diff"], 1)

                def decayed(l):
                    w = LEVELS[l] if l < L else P
                    v = "p (n a w) -> p n a w"
                    D, Q, K = (t.rearrange(v, a=2, w=w) for t in (HG_D[l % 2], HG_FLAT_Q, HG_FLAT_K))
                    dve.wait_ge(m["exp"], 2 * l + 1)
                    V.tensor_tensor(D[:, :, 1, :], D[:, :, 1, :], Q[:, :, 1, :], ALU.mult)
                    dve.wait_ge(m["exp"], 2 * l + 2)
                    V.tensor_tensor(D[:, :, 0, :], D[:, :, 0, :], K[:, :, 0, :], ALU.mult).then_inc(m["qk"], 1)

                def take(s):
                    dve.wait_ge(m["level"], s + 1)
                    A = ps[:, 4 * (s % 2):4 * (s % 2) + 4, :].rearrange("p b (g t) -> p (b g) t", t=P)
                    if s == 0:
                        V.tensor_tensor(HG_AT, A, ident.unsqueeze(1).broadcast_to([P, 16, P]),
                                        ALU.mult).then_inc(m["taken"], 1)
                    else:
                        dve.wait_ge(m["taken"], s)
                        mask = levels[:, (s - 1) * P:s * P].unsqueeze(1).broadcast_to([P, 16, P])
                        V.copy_predicated(HG_AT, mask, A).then_inc(m["taken"], 1)

                for u in range(8, 12):
                    scale_tokens(n0 + u, e0 + u, HG_V[:, :, 256 * (u - 8):256 * (u - 7)], 0)
                    if u < 11:
                        low(n0 + u + SPLIT)
                    if u == 8:
                        cumulate(12)
                    elif u == 9:
                        dve.wait_ge(m["scan"], 16)
                        diffs(0)
                    elif u == 11:
                        dve.wait_ge(m["qsilu"], 4)
                        decayed(0)
                        diffs(1)
                for l in range(L + 1):
                    if l:
                        decayed(l)
                    if 0 < l < L:
                        diffs(l + 1)
                    if not 1 <= l <= RECT_LEVELS:
                        take(l)
                for p in range(4):
                    dve.wait_ge(m["o"], p + 1)
                    V.tensor_copy(HG_B[:, 2 * p:2 * p + 2], pair(p, True)).then_inc(m["done"], 1)
                low(n0 + 11 + SPLIT)
                dve.wait_ge(m["done"], 4)
                for c in range(KC):
                    dve.wait_ge(m["rs"], c // 2 + 1)
                    ins = V.scalar_tensor_tensor(HG_B[:, c], HG_B[:, c],
                                                 smalls[:, S_HGN + phases[i][1] // 3:S_HGN + phases[i][1] // 3 + 1],
                                                 HG_RS[:, c], ALU.mult, ALU.mult)
                link(ins)
                tail(i, m, n0 + 12, e0 + 12, HG_K, HG_B)

            def ml(i):
                m = own[i]
                n0, e0 = at(i, "units"), at(i, "banks")
                g = next_gain(i)
                V.tensor_tensor(tiny[:, 0:64].rearrange("p (k g) -> p k g", g=8),
                                smalls[:, S_WIF:S_WIF + 64].rearrange("p (k g) -> p k g", g=8),
                                smalls[:, g:g + KC].unsqueeze(2).broadcast_to([P, KC, 8]), ALU.mult).then_inc(m["wif"], 1)
                norm(i, n0 + SPLIT)
                R = [ML_ROWS[0:4, j] for j in range(8)]
                one_row = ones[0:4, 0:1].broadcast_to([4, T])
                for u in range(8):
                    if u == 2:
                        columns(i)
                    if u < 4:
                        dst = ML_Q if u < 2 else ML_K
                        scale(n0 + u, e0 + u, dst[:, 2 * (u % 2):2 * (u % 2) + 2])
                    else:
                        scale_tokens(n0 + u, e0 + u, ML_V[:, :, 256 * (u - 4):256 * (u - 3)], 0)
                    if u:
                        low(n0 + u + SPLIT)
                    if u == 3:
                        dve.wait_ge(m["gates"], 1)
                        for j in range(2):
                            link(V.tensor_tensor(R[j], ps[0:4, 4, j * T:(j + 1) * T], rstd[0:4, :], ALU.mult))
                            ins = V.tensor_scalar(R[j], R[j], smalls[0:4, S_BIF + j:S_BIF + j + 1], None, ALU.add)
                        ins.then_inc(m["lin"], 1)
                    if u == 5:
                        dve.wait_ge(m["soft"], 1)
                        link(V.tensor_tensor_scan(R[3], one_row, R[2], 0.0, ALU.mult, ALU.subtract))
                        link(V.scalar_tensor_tensor(R[4], R[0], GATE_CAP, R[3], ALU.mult, ALU.subtract))
                        link(V.tensor_tensor_scan(R[5], one_row, R[4], 0.0, ALU.mult, ALU.max))
                        V.tensor_scalar(R[6], R[5], -1.0, None, ALU.mult)
                        V.scalar_tensor_tensor(R[7], R[3], -1.0, R[5], ALU.mult, ALU.subtract).then_inc(m["row"], 1)
                dve.wait_ge(m["cols"], 1)
                V.tensor_copy(tiny[:, 64:72], ps[:, 4, 0:8]).then_inc(m["ucol"], 1)
                dve.wait_ge(m["ucol"], 1)
                dve.wait_ge(m["bcast"], 1)
                for h in range(ML_HEADS):
                    neg_m = ps[:, 6 + h // 2, (h % 2) * T:(h % 2 + 1) * T]
                    V.tensor_scalar(ML_W[:, h, 0:T], neg_m, tiny[:, 64 + h:65 + h], 0.0, ALU.add, ALU.min)
                    V.tensor_scalar(ML_W[:, h, T:T + P], neg_m[:, P:T], tiny[:, 68 + h:69 + h], 0.0, ALU.add,
                                    ALU.min).then_inc(m["arg"], 1)
                for h in range(ML_HEADS):
                    dve.wait_ge(m["exp"], h + 1)
                    V.tensor_tensor(ML_W[:, h, 0:P], ML_W[:, h, 0:P], causal, ALU.mult)
                    link(V.tensor_tensor(ML_W[:, h, T:T + P], ML_W[:, h, T:T + P], causal, ALU.mult))
                    dve.wait_ge(m["scores"], h + 1)
                    V.scalar_tensor_tensor(ML_W[:, h], ps[:, h, 0:384], ML_DQK ** -0.5, ML_W[:, h], ALU.mult,
                                           ALU.mult).then_inc(m["w"], 1)
                for h in range(ML_HEADS):
                    dve.wait_ge(m["num"], h + 1)
                    V.tensor_copy(ML_H[:, 2 * h:2 * h + 2], pair(h, True)).then_inc(m["h"], 1)
                dve.wait_ge(m["gexp"], 2)
                link(V.tensor_tensor(ML_DEN, ML_DEN, ML_GUARD, ALU.max))
                link(V.scalar_tensor_tensor(ML_DEN, ML_DEN, EPS, ML_DEN, ALU.mult, ALU.mult))
                for p in range(2):
                    two = slice(2 * p, 2 * p + 2)
                    dve.wait_ge(m["sums"], p + 1)
                    V.scalar_tensor_tensor(ML_GUARD[:, two], pair(6 + p, True), 1.0 / ML_DV, ML_DEN[:, two], ALU.mult,
                                           ALU.add).then_inc(m["nrm"], 1)
                dve.wait_ge(m["h"], ML_HEADS)
                for c in range(KC):
                    dve.wait_ge(m["rs"], c // 4 + 1)
                    ins = V.scalar_tensor_tensor(ML_H[:, c], ML_H[:, c], gain(S_MLN, c), ML_GUARD[:, c // 2], ALU.mult,
                                                 ALU.mult)
                link(ins)
                tail(i, m, n0 + 8, e0 + 8, ML_T, ML_H)

            def attention(g0, groups, bufs, out, bias=None, sinks=False, besides={}):
                PR = bufs[0]

                def logits(g):
                    if g >= len(groups):
                        return
                    G = groups[g]
                    t = tiny[:, 32 * (g % 3):32 * (g % 3) + 32]
                    n, w, k0 = G["slots"], G["width"], G["k0"]
                    dve.wait_ge(att["scores"], g0 + g + 1)
                    if bias is not None and g >= len(PR):
                        dve.wait_ge(att["turned"], g0 + g - len(PR) + 1)
                    src = ps[:, 2 * (g % 2):2 * (g % 2) + 2, :].rearrange("p b t -> p (b t)")[:, 0:n * w]
                    src = src.rearrange("p (s k) -> p s k", k=w)[:, :, k0:]
                    if bias is not None:
                        dst = PR[g % len(PR)][:, 0:n * w].rearrange("p (s k) -> p s k", k=w)[:, :, k0:]
                        link(bias(G, dst, src))
                        src = dst
                    link(V.tensor_reduce(t[:, 0:n], src, AX_X, ALU.max))
                    if sinks:
                        sink = smalls[:, S_SINK + 4 * G["kv"]:S_SINK + 4 * G["kv"] + 4].rearrange("p (a b) -> p b a", b=2)
                        mx, sx = (t[:, c:c + 4].rearrange("p (b a) -> p b a", b=2) for c in (0, 12))
                        link(V.scalar_tensor_tensor(mx, sink, 1.0 / G["scale"], mx, ALU.mult, ALU.max))
                        V.scalar_tensor_tensor(sx, sink, 1.0 / G["scale"], mx, ALU.mult, ALU.subtract)
                    V.tensor_scalar(t[:, 4:4 + n], t[:, 0:n], -G["scale"], None, ALU.mult).then_inc(att["bias"], 1)

                def probs(g):
                    G = groups[g]
                    t = tiny[:, 32 * (g % 3):32 * (g % 3) + 32]
                    n, w, k0 = G["slots"], G["width"], G["k0"]
                    dve.wait_ge(att["exp"], g0 + g + 1)
                    if sinks:
                        link(V.tensor_tensor(t[:, 8:8 + n], t[:, 8:8 + n], t[:, 12:12 + n], ALU.add))
                    link(V.reciprocal(t[:, 16:16 + n], t[:, 8:8 + n]))
                    for s in range(n):
                        p = PR[g % len(PR)][:, s * w + k0:(s + 1) * w]
                        ins = V.tensor_scalar(p, p, t[:, 16 + s:17 + s], None, ALU.mult)
                    ins.then_inc(att["probs"], 1)

                def take(g):
                    dve.wait_ge(att["out"], g0 + g + 1)
                    dst, r, n = out(groups[g])
                    V.tensor_copy(dst, ps[r, 6 + g % 2, 0:n * P].rearrange("p (c t) -> p c t", t=P)).then_inc(att["taken"], 1)

                logits(0)
                logits(1)
                if -1 in besides:
                    besides[-1]()
                for g in range(len(groups)):
                    probs(g)
                    if g in besides:
                        besides[g]()
                    logits(g + 2)
                    if g:
                        take(g - 1)
                take(len(groups) - 1)

            def normalise(dst, g, roots, count):
                for c in range(2):
                    ins = V.scalar_tensor_tensor(dst[:, c], dst[:, c], g, roots[:, c], ALU.mult, ALU.mult)
                ins.then_inc(count, 1)

            def sw(i):
                m = own[i]
                n0, e0 = at(i, "units"), at(i, "banks")
                norm(i, n0 + SPLIT)
                for u in range(4):
                    if u == 2:
                        columns(i)
                    scale(n0 + u, e0 + u, sw_pair(u))
                    if u:
                        low(n0 + u + SPLIT)

                def roots(p):
                    dve.wait_ge(m["rs"], p + 1)
                    normalise(sw_pair(p), gain(S_SWN, p < 2), SW_SQ[:, 2 * (p % 4):2 * (p % 4) + 2],
                              m["qk"])
                for p in range(4):
                    roots(p)
                for u in range(4, 6):
                    scale(n0 + u, e0 + u, sw_pair(u))
                    low(n0 + u + SPLIT)
                scale_tokens(n0 + 6, e0 + 6, SW_V, 0)
                low(n0 + 6 + SPLIT)
                dve.wait_ge(phase_consts, 16)

                def alibi(G, dst, src):
                    for s in range(4):
                        h = 4 * G["kv"] + (s % 2) * 2 + s // 2
                        slope = 2.0 ** (-8.0 * (h + 1) / SW_HEADS) / G["scale"]
                        ins = V.scalar_tensor_tensor(dst[:, s], SW_BIAS[:, G["k0"]:], slope, src[:, s], ALU.mult, ALU.add)
                    return ins
                attention(att_before(i), quad_groups(SW_QK, SW_QK[:, 8:12], SW_V, SW_KV, True), ATT_SW,
                          lambda G: (SW_O[:, 2 * G["kv"]:2 * G["kv"] + 2, G["n"] * P:(G["n"] + 1) * P], slice(0, P), 2),
                          bias=alibi, sinks=True, besides={-1: lambda: (roots(4), roots(5))})
                for u in range(4):
                    dve.wait_ge(mo_high, 4 * rcols(i) + u + 1)
                    V.tensor_tensor(mo_lo[:, 2 * u:2 * u + 2], SW_O[:, 2 * u:2 * u + 2],
                                    mo_hi[:, 2 * u:2 * u + 2].bitcast(F32), ALU.subtract).then_inc(mo_ready, 1)
                residual(i, n0 + 7, e0 + 7)

            def second(i):
                m = own[i]
                n0, e0 = at(i, "units"), at(i, "banks")
                norm(i, n0 + SPLIT, second_lows[0])
                dve.wait_ge(m["memrs"], 1)
                for u in range(2):
                    dve.wait_ge(weights_used, n0 + u + 1)
                    V.tensor_tensor(SE_KM[:, 2 * u:2 * u + 2], pair(e0 + u), row(SE_RMEM, 2), ALU.mult).then_inc(bank_read, 1)
                    if u:
                        low(n0 + u + SPLIT)
                dve.wait_ge(m["memcols"], 1)
                link(V.tensor_copy(rcol[:, 2:4], ps[:, 4, T:T + 2]))
                for u in range(2, 4):
                    if u == 3:
                        columns(i)
                    scale_tokens(n0 + u, e0 + u, SE_VM[:, :, 256 * (u - 2):256 * (u - 1)], 2)
                    low(n0 + u + SPLIT)
                B = [SE_QB[:, 0:2], SE_QB[:, 2:4], SE_KB]
                for p in range(3):
                    scale(n0 + 4 + p, e0 + 4 + p, B[p])
                    low(n0 + 4 + p + SPLIT)
                scale(n0 + 7, e0 + 7, SE_QM[:, 0:2])
                low(n0 + 7 + SPLIT)
                for p in range(3):
                    dve.wait_ge(m["rs"], p + 1)
                    normalise(B[p], gain(S_BN, p // 2), SE_SQ[:, 2 * p:2 * p + 2], m["x"])
                scale(n0 + 8, e0 + 8, SE_QM[:, 2:4])
                low(n0 + 8 + SPLIT)
                dve.wait_ge(weights_used, n0 + 10)
                for b in range(TB):
                    ins = V.tensor_scalar(SE_VB[:, b], pair(e0 + 9)[:, b, 0:P], rcol[:, b:b + 1], None, ALU.mult)
                ins.then_inc(bank_read, 1)
                low(n0 + 9 + SPLIT)
                dve.wait_ge(phase_consts, PC)

                def rope(r, src, cos, sin, turned, dst):
                    y, z = SE_COS[r % 2], SE_SIN[r % 2]
                    V.tensor_tensor(y, src, row(cos, 2), ALU.mult)
                    dve.wait_ge(m["rot"], r + 1)
                    link(V.tensor_tensor(z, turned, row(sin, 2), ALU.mult))
                    V.tensor_tensor(dst, y, z, ALU.add).then_inc(m["roped"], 1)

                Z = [SE_O[:, 2 * p:2 * p + 2] for p in range(3)]

                def rope_sines():
                    for p in range(3):
                        dve.wait_ge(m["rot"], p + 1)
                        V.tensor_tensor(Z[p], pair(5 + p, True), row(SIN2, 2), ALU.mult)

                def rope_rest(p):
                    if p == 0:
                        dve.wait_ge(m["x"], 3)
                    link(V.tensor_tensor(B[p], B[p], row(COS2, 2), ALU.mult))
                    V.tensor_tensor(B[p], B[p], Z[p], ALU.add).then_inc(m["roped"], 1)

                def place(G):
                    cs, n = (slice(4 + 2 * G["kv"], 6 + 2 * G["kv"]), 2) if "kv" in G else (slice(8, 12), 4)
                    return SE_O[:, cs, G["n"] * P:(G["n"] + 1) * P], slice(0, P), n
                attention(att_before(i, 0), memory_groups() + quad_groups(SE_QB, SE_KB, SE_VB, 2, False), ATT_2, place,
                          besides={-1: rope_sines, 0: lambda: (rope_rest(0), rope_rest(1), rope_rest(2))})
                for half in range(2):
                    u0 = 10 + 9 * half
                    for u in range(6):
                        scale(n0 + u0 + u, e0 + u0 + u, SE_X[u % 2])
                        dve.wait_ge(bank_read, e0 + u0 + u + 5)
                        low(n0 + u0 + u + SPLIT)
                        dst = (SE_QA if u < 3 else SE_KA)[:, 2 * (u % 3):2 * (u % 3) + 2]
                        rope(3 + 6 * half + u, SE_X[u % 2], COS, SIN, pair(4 + u % 2, True), dst)
                    for g in range(A_GROUPS):
                        u = u0 + 6 + g
                        scale_tokens(n0 + u, e0 + u, SE_VA[:, :, 256 * g:256 * (g + 1)], 0)
                        low(n0 + u + SPLIT)
                    attention(att_before(i, 2 + half), dilated_groups(), ATT_A,
                              lambda G: (SE_O[head_half(G["h"]), 2 * half + G["h"] // 2:2 * half + G["h"] // 2 + 1,
                                              G["n"] * P:(G["n"] + 1) * P], head_half(G["h"]), 1),
                              bias=lambda G, dst, src: V.tensor_tensor(dst, src, SE_MASK[:, G["n"]:G["n"] + 1, :],
                                                                       ALU.add))

                def fill(br):
                    s = 4 * (br % 2)
                    dve.wait_ge(m["mhi"], br + 1)
                    V.tensor_tensor(mo_lo[:, s:s + 4], SE_O[:, 4 * br:4 * br + 4], mo_hi[:, s:s + 4].bitcast(F32),
                                    ALU.subtract).then_inc(m["mlo"], 1)
                for u in range(6):
                    t = SE_GATE[u % 2]
                    scale(n0 + 28 + u, e0 + 28 + u, t)
                    dve.wait_ge(m["gate"], u + 1)
                    V.tensor_tensor(SE_O[:, 2 * u:2 * u + 2], SE_O[:, 2 * u:2 * u + 2], t, ALU.mult).then_inc(m["gated"], 1)
                    low(n0 + 28 + u + SPLIT)
                    if u in (2, 4):
                        fill(u // 2 - 1)
                n, e = n0 + 34, e0 + 34
                for br in range(3):
                    low(n + SPLIT)
                    low(n + 1 + SPLIT)
                    if br == 1:
                        fill(2)
                    for u in range(4):
                        t, two = SE_GATE[u % 2], SE_MERGED[:, 2 * u:2 * u + 2]
                        scale(n + 2 + u, e + u, t)
                        dve.wait_ge(m["merge"], 4 * br + u + 1)
                        if br == 0:
                            V.tensor_tensor(two, t, pair(4 + u, True), ALU.mult).then_inc(m["merged"], 1)
                        else:
                            link(V.tensor_tensor(t, t, pair(4 + u, True), ALU.mult))
                            V.tensor_tensor(two, two, t, ALU.add).then_inc(m["merged"], 1)
                        last = br == 2 and u == 3
                        if not last:
                            low(n + 2 + u + SPLIT)
                        if br == 2:
                            dve.wait_ge(m["high"], u + 1)
                            V.tensor_tensor(mo_lo[:, 2 * u:2 * u + 2], two, mo_hi[:, 2 * u:2 * u + 2].bitcast(F32),
                                            ALU.subtract).then_inc(m["low"], 1)
                        if last:
                            low(n + 2 + u + SPLIT)
                    n, e = n + 6, e + 4
                for u in range(4):
                    dve.wait_ge(weights_used, n + u + 1)
                    V.tensor_copy(SE_Y[:, 2 * u:2 * u + 2], pair(e + u)).then_inc(bank_read, 1)
                    low(n + u + SPLIT)
                dve.wait_ge(m["frs"], 1)
                for c in range(KC):
                    ins = V.scalar_tensor_tensor(SE_Y[:, c], SE_Y[:, c], gain(S_GPOST, c), SE_YR, ALU.mult, ALU.mult)
                    if c % 4 == 3:
                        link(ins)
                        half = slice(c - 3, c + 1)
                        V.tensor_tensor(x[:, half], x[:, half], SE_Y[:, half], ALU.add).then_inc(out_ready, 1)

            PC = 16 * sum(k in ("sw", "second") for k, _ in phases)
            V.memset(eps[:], EPS).then_inc(eps_ready, 1)
            V.memset(rcol[:], 0.0).then_inc(bank_read, 4)
            low(0)
            dve.wait_ge(x_loaded, 32)
            next_operand(-1, 0, KC)
            for i in range(1, SPLIT):
                low(i)
            for i, (kind, _) in enumerate(phases):
                {"ffn": ffn, "ple": ple, "hg": hg, "ml": ml, "sw": sw, "second": second}[kind](i)
            if phases[-1][0] != "second":
                link(V.memset(eps[:], EPS))
                V.memset(eps[:], EPS).then_inc(out_ready, 2)


INS = ["x_t", "p_t", "mem_t", "weights", "smalls", "c_common", "c_levels", "c_swa", "c_second"]


def kernel(**inputs):
    import concourse.bacc as bacc
    from concourse.bass_utils import run_bass_kernel_spmd

    nc = bacc.Bacc("TRN2", target_bir_lowering=False, num_devices=1)
    laid, arrays, args = lay_out(inputs, PHASES), {}, []
    for name in INS:
        a = laid[name]
        arrays[name + "_dram"] = a
        args.append(nc.dram_tensor(name + "_dram", a.shape, mybir.dt.from_np(a.dtype), kind="ExternalInput").ap())
    args.append(nc.dram_tensor("out_dram", (P, KC, T), F32, kind="ExternalOutput").ap())
    build(nc, PHASES, *args)
    r = run_bass_kernel_spmd(nc, [arrays], core_ids=[0])
    got = r.results[0]["out_dram"]
    return np.ascontiguousarray(got.transpose(2, 1, 0)).reshape(1, T, D_MODEL)
```
